# Optimizing a Trainium2 kernel written in Bass

```python
import math
import jax, jax.numpy as jnp
from jax import lax
import numpy as np

D_MODEL = 1024
BATCH = 1
SEQ = 1024
DEPTH = 2

CTX_LEN = 256
GRID_W = 64
N_MIXERS = 2
EPS = 1e-6

FN_EXPAND = 2
FN_WIDTH = FN_EXPAND * D_MODEL
FN_GROUPS = 8
FN_GROUP_DIM = FN_WIDTH // FN_GROUPS

DN_HEADS = 8
DN_DK = 128
DN_DV = 256
DN_QK_WIDTH = DN_HEADS * DN_DK
DN_V_WIDTH = DN_HEADS * DN_DV
DN_QKV_WIDTH = 2 * DN_QK_WIDTH + DN_V_WIDTH
DN_PROJ_WIDTH = DN_QKV_WIDTH + DN_V_WIDTH + 4 * DN_HEADS
DN_CONV = 3
DN_CHUNK = 64

N_FOURIER_LAYERS = (DEPTH + 1) // 2
N_DELTA_LAYERS = DEPTH // 2

kernel_name = "hybrid_fourier_gdn_prefix_backbone"

def rmsnorm(x, g):
    xf = x.astype(jnp.float32)
    y = xf * lax.rsqrt(jnp.mean(xf * xf, axis=-1, keepdims=True) + EPS)
    return (y * g.astype(jnp.float32)).astype(x.dtype)

def l2norm(x):
    return x * lax.rsqrt(jnp.sum(x * x, axis=-1, keepdims=True) + EPS)

def adaln(cond, w, b):
    m = jax.nn.silu(cond) @ w + b
    return jnp.split(m, 3, axis=-1)

def fourier_mix(h, w_in, w_grp, w_out):
    u, z = jnp.split(h @ w_in, 2, axis=-1)
    b_, l_ = u.shape[:2]
    u = u.reshape(b_, l_, FN_GROUPS, FN_GROUP_DIM).astype(jnp.float32)
    f = jnp.real(jnp.fft.fft2(u, axes=(1, 3), norm="ortho")).astype(h.dtype)
    f = jnp.einsum("blgc,gcd->blgd", f, w_grp).reshape(b_, l_, FN_WIDTH)
    return (f * jax.nn.silu(z)) @ w_out

def short_conv_silu(u, w, rows, cols):
    b_, l_, ch = u.shape
    y = lax.conv_general_dilated(
        u.reshape(b_, rows, cols, ch), w[:, :, None, :].astype(u.dtype),
        window_strides=(1, 1), padding="SAME",
        dimension_numbers=("NHWC", "HWIO", "NHWC"), feature_group_count=ch)
    return jax.nn.silu(y.reshape(b_, l_, ch))

def gated_delta_chunked(q, k, v, g, beta, s0, with_output):
    b_, h_, l_, dk = q.shape
    dv = v.shape[-1]
    c_ = DN_CHUNK
    n_ = l_ // c_
    q = q.reshape(b_, h_, n_, c_, dk)
    k = k.reshape(b_, h_, n_, c_, dk)
    v = v.reshape(b_, h_, n_, c_, dv)
    g = jnp.cumsum(g.reshape(b_, h_, n_, c_), axis=-1)
    beta = beta.reshape(b_, h_, n_, c_)
    lower = jnp.tril(jnp.ones((c_, c_), dtype=bool))
    strict = jnp.tril(jnp.ones((c_, c_), dtype=bool), -1)
    diff = g[..., :, None] - g[..., None, :]
    decay = jnp.where(lower, jnp.exp(jnp.where(lower, diff, 0.0)), 0.0)
    kb = k * beta[..., None]
    kk = jnp.einsum("bhnid,bhnjd->bhnij", kb, k)
    a_mat = jnp.eye(c_, dtype=q.dtype) + jnp.where(strict, kk * decay, 0.0)
    rhs = jnp.concatenate([v * beta[..., None], kb * jnp.exp(g)[..., None]], axis=-1)
    sol = lax.linalg.triangular_solve(a_mat, rhs, left_side=True, lower=True, unit_diagonal=True)
    u, w = sol[..., :dv], sol[..., dv:]
    g_last = g[..., -1]
    k_tail = k * jnp.exp(g_last[..., None] - g)[..., None]
    to_scan = lambda t: jnp.moveaxis(t, 2, 0)
    if with_output:
        qk = jnp.einsum("bhnid,bhnjd->bhnij", q, k) * decay
        q_head = q * jnp.exp(g)[..., None]
        xs = tuple(map(to_scan, (u, w, k_tail, g_last, q_head, qk)))
    else:
        xs = tuple(map(to_scan, (u, w, k_tail, g_last)))

    def step(state, xs_c):
        u_c, w_c, kt_c, gl_c = xs_c[:4]
        v_new = u_c - jnp.einsum("bhcd,bhde->bhce", w_c, state)
        s_next = state * jnp.exp(gl_c)[..., None, None] + jnp.einsum("bhcd,bhce->bhde", kt_c, v_new)
        if with_output:
            qh_c, qk_c = xs_c[4:]
            o = jnp.einsum("bhcd,bhde->bhce", qh_c, state) + jnp.einsum("bhij,bhje->bhie", qk_c, v_new)
            return s_next, o
        return s_next, None

    s_final, o = lax.scan(step, s0, xs)
    if with_output:
        o = jnp.moveaxis(o, 0, 2).reshape(b_, h_, l_, dv)
    return o, s_final

def delta_project(h, w_in, conv_w, a_log, dt_bias, rows, cols):
    b_, l_, _ = h.shape
    p = h @ w_in
    qkv, z, a, bb = jnp.split(p, [DN_QKV_WIDTH, DN_QKV_WIDTH + DN_V_WIDTH,
                                  DN_QKV_WIDTH + DN_V_WIDTH + 2 * DN_HEADS], axis=-1)
    qkv = short_conv_silu(qkv, conv_w, rows, cols).astype(jnp.float32)
    q, k, v = jnp.split(qkv, [DN_QK_WIDTH, 2 * DN_QK_WIDTH], axis=-1)
    q = l2norm(q.reshape(b_, l_, DN_HEADS, DN_DK)).transpose(0, 2, 1, 3) * (DN_DK ** -0.5)
    k = l2norm(k.reshape(b_, l_, DN_HEADS, DN_DK)).transpose(0, 2, 1, 3)
    v = v.reshape(b_, l_, DN_HEADS, DN_DV).transpose(0, 2, 1, 3)
    a = a.astype(jnp.float32).reshape(b_, l_, 2, DN_HEADS)
    bb = bb.astype(jnp.float32).reshape(b_, l_, 2, DN_HEADS)
    g = -jnp.exp(a_log.astype(jnp.float32)) * jax.nn.softplus(a + dt_bias.astype(jnp.float32))
    beta = jax.nn.sigmoid(bb)
    g = jnp.transpose(g, (2, 0, 3, 1))
    beta = jnp.transpose(beta, (2, 0, 3, 1))
    return q, k, v, z, g, beta

def delta_output(o, z, norm_g, w_out):
    b_, h_, l_, dv = o.shape
    o = o * lax.rsqrt(jnp.mean(o * o, axis=-1, keepdims=True) + EPS) * norm_g.astype(jnp.float32)
    o = o.transpose(0, 2, 1, 3).reshape(b_, l_, h_ * dv).astype(z.dtype)
    return (o * jax.nn.silu(z)) @ w_out

def delta_mix(h_lat, h_ctx, w_in, conv_w, a_log, dt_bias, norm_g, w_out, rows, ctx_output):
    b_ = h_lat.shape[0]
    ql, kl, vl, zl, gl, bl = delta_project(h_lat, w_in, conv_w, a_log, dt_bias, rows, GRID_W)
    qc, kc, vc, zc, gc, bc = delta_project(h_ctx, w_in, conv_w, a_log, dt_bias, 1, h_ctx.shape[1])
    s0 = jnp.zeros((b_, DN_HEADS, DN_DK, DN_DV), jnp.float32)
    o_lat = 0.0
    o_ctx = 0.0
    for d in range(2):
        f = (lambda t: jnp.flip(t, axis=2)) if d == 1 else (lambda t: t)
        oc, s_ctx = gated_delta_chunked(f(qc), f(kc), f(vc), f(gc[d]), f(bc[d]), s0, ctx_output)
        ol, _ = gated_delta_chunked(f(ql), f(kl), f(vl), f(gl[d]), f(bl[d]), s_ctx, True)
        o_lat = o_lat + f(ol)
        if ctx_output:
            o_ctx = o_ctx + f(oc)
    out_lat = delta_output(o_lat, zl, norm_g, w_out)
    out_ctx = delta_output(o_ctx, zc, norm_g, w_out) if ctx_output else None
    return out_lat, out_ctx

def setup_inputs(seed: int = 0) -> dict:
    key = jax.random.key(seed)
    ks = jax.random.split(key, 20)
    f32 = jnp.float32
    D = D_MODEL
    nrm = lambda k, shape, s: jax.random.normal(k, shape, f32) * s
    log_dt = jax.random.uniform(ks[15], (N_DELTA_LAYERS, 2, DN_HEADS), f32,
                                math.log(1e-3), math.log(1e-1))
    dt = jnp.exp(log_dt)
    return {
        "x": nrm(ks[0], (BATCH, SEQ, D), 1.0),
        "c": nrm(ks[1], (BATCH, D), 1.0),
        "ctx": nrm(ks[2], (BATCH, CTX_LEN, D), 1.0),
        "c_ctx": nrm(ks[3], (D,), 1.0),
        "mod_w": nrm(ks[4], (DEPTH, D, 3 * D), 0.5 * D ** -0.5),
        "mod_b": nrm(ks[5], (DEPTH, 3 * D), 0.01),
        "norm_g": 1.0 + nrm(ks[6], (DEPTH, D), 0.01),
        "final_g": 1.0 + nrm(ks[7], (D,), 0.01),
        "fn_w_in": nrm(ks[8], (N_FOURIER_LAYERS, D, 2 * FN_WIDTH), D ** -0.5),
        "fn_w_grp": nrm(ks[9], (N_FOURIER_LAYERS, FN_GROUPS, FN_GROUP_DIM, FN_GROUP_DIM), FN_GROUP_DIM ** -0.5),
        "fn_w_out": nrm(ks[10], (N_FOURIER_LAYERS, FN_WIDTH, D), FN_WIDTH ** -0.5),
        "dn_w_in": nrm(ks[11], (N_DELTA_LAYERS, D, DN_PROJ_WIDTH), D ** -0.5),
        "dn_conv": nrm(ks[12], (N_DELTA_LAYERS, DN_CONV, DN_CONV, DN_QKV_WIDTH), 1.0 / DN_CONV),
        "dn_a_log": jnp.log(jax.random.uniform(ks[13], (N_DELTA_LAYERS, 2, DN_HEADS), f32, 1.0, 16.0)),
        "dn_dt_bias": dt + jnp.log(-jnp.expm1(-dt)),
        "dn_norm_g": 1.0 + nrm(ks[14], (N_DELTA_LAYERS, DN_DV), 0.01),
        "dn_w_out": nrm(ks[16], (N_DELTA_LAYERS, DN_V_WIDTH, D), DN_V_WIDTH ** -0.5),
    }

def reference(x, c, ctx, c_ctx, mod_w, mod_b, norm_g, final_g, fn_w_in, fn_w_grp, fn_w_out,
              dn_w_in, dn_conv, dn_a_log, dn_dt_bias, dn_norm_g, dn_w_out):
    rows = x.shape[1] // GRID_W
    h_lat, h_ctx = x, ctx
    cond_lat = c[:, None, :]
    cond_ctx = c_ctx[None, None, :]
    for i in range(DEPTH):
        last = i == DEPTH - 1
        mixer = i % N_MIXERS
        j = i // N_MIXERS
        sh_l, sc_l, gt_l = adaln(cond_lat, mod_w[i], mod_b[i])
        n_lat = rmsnorm(h_lat, norm_g[i]) * (1.0 + sc_l) + sh_l
        need_ctx = (not last) or mixer == 1
        if need_ctx:
            sh_c, sc_c, gt_c = adaln(cond_ctx, mod_w[i], mod_b[i])
            n_ctx = rmsnorm(h_ctx, norm_g[i]) * (1.0 + sc_c) + sh_c
        if mixer == 0:
            out_lat = fourier_mix(n_lat, fn_w_in[j], fn_w_grp[j], fn_w_out[j])
            out_ctx = fourier_mix(n_ctx, fn_w_in[j], fn_w_grp[j], fn_w_out[j]) if not last else None
        else:
            out_lat, out_ctx = delta_mix(n_lat, n_ctx, dn_w_in[j], dn_conv[j], dn_a_log[j],
                                         dn_dt_bias[j], dn_norm_g[j], dn_w_out[j], rows,
                                         not last)
        h_lat = h_lat + gt_l * out_lat
        if not last:
            h_ctx = h_ctx + gt_c * out_ctx
    return rmsnorm(h_lat, final_g)


_drawn_inputs = setup_inputs


def setup_inputs(seed=0):
    import zlib

    import numpy as np

    out = dict(_drawn_inputs(seed))
    spreads = {}
    factors = {'ctx': 29.168,
     'c_ctx': 29.956,
     'mod_b': 5.865,
     'norm_g': 8.0,
     'final_g': 34.193,
     'dn_norm_g': 59.831}
    for name, (base, spread) in spreads.items():
        noise = np.random.default_rng([zlib.crc32(name.encode()), seed]).standard_normal(out[name].shape)
        drawn = base * np.exp(spread * noise) if base else spread * noise
        out[name] = __import__('jax').numpy.asarray(drawn.astype(out[name].dtype))
    for name, factor in factors.items():
        out[name] = (out[name] * factor).astype(out[name].dtype)
    return out
```

```python
from contextlib import ExitStack

import numpy as np
import concourse.bass as bass
from concourse import mybir

F32 = mybir.dt.float32
I32 = mybir.dt.int32
ACT = mybir.ActivationFunctionType
ALU = mybir.AluOpType
AXX = mybir.AxisListType.X

P = 128
D = 1024
KT = D // P
LAT, CTX = 1024, 256
TOK = LAT + CTX
NL, NC_ = LAT // P, CTX // P
NT = NL + NC_
HL, HC = LAT // 2, CTX // 2
GW = 64
GR = LAT // GW
EPS = 1e-6
FG, FD = 8, 256
FW = FG * FD
H, DK, DV = 8, 128, 256
LEVELS = 7
BIG = -1.0e30
KB = 1024


def bcast(ap, shape):
    return ap.broadcast_to(shape)


class Core:

    def __init__(self, nc):
        self.nc = nc
        self.placed = {}
        sb = nc.alloc_sbuf_tensor
        self.ident = sb("ident", [P, P], F32)
        self.cols = sb("cols", [P, 82], F32)
        self.modT = sb("modT", [P, 48, 2], F32)
        self.acoef = sb("acoef", [P, 2, KT, 2], F32)
        self.gtok = sb("gtok", [P, NT, 16], F32)
        self.beta = sb("beta", [P, NT, 16], F32)
        self.nbeta = sb("nbeta", [P, NT, 16], F32)
        self.epst = sb("epst", [P, 1], F32)
        self.base = (nc.sbuf_base + 63) // 64 * 64
        self.psum = nc.alloc_psum_tensor("psum", [P, 8 * 512], F32)
        dr = lambda n, s: nc.dram_tensor(n, s, F32, kind="Internal").ap()
        self.y_d = dr("y_scr", (FW, TOK))
        self.y2_d = dr("y2_scr", (FW, LAT))
        self.h_d = dr("h_scr", (LAT, D))
        self.z_d = dr("z_scr", (FW, LAT))
        self.qT_d = dr("qT_scr", (H, P, LAT))
        self.kT_d = dr("kT_scr", (H, P, TOK))
        self.k_d = dr("k_scr", (TOK, D))
        self.v_d = dr("v_scr", (TOK, FW))

    def at(self, name, shape, kb, dt=F32):
        if name not in self.placed:
            self.placed[name] = self.nc.alloc_sbuf_tensor_at(name, shape, dt, offset=self.base + int(kb * KB))
        return self.placed[name]


def sems(nc, stack):
    return lambda name: stack.enter_context(nc.semaphore(name))


COL_MODB, COL_G, COL_C, COL_CC, COL_DN = 0, 48, 64, 72, 80


def input_phase(core, io):
    nc = core.nc
    pqT = core.at("pqT", [P, KT, TOK], 0)
    nT = core.at("nT", [P, KT, TOK], 40)
    xn = core.at("xn", [P, NT, D], 80)
    xm = core.at("xm", [P, 5, D], 120)
    ev = core.at("ev", [P, 5, D], 140)
    mw = [core.at(f"mw{s}", [P, KT, 256], 160 + 8 * s) for s in range(2)]
    dft = core.at("dft", [P, 2 * 4 * HL + 2 * HC], 176)
    b0 = core.at("b0", [64, D], 193)
    junk = core.at("junk", [P, D], 0)
    rows = core.at("rows", [82, P], 40)
    scond = core.at("scond", [P, KT, 2], 199)
    ss = core.at("ss", [P, 16], 199.25)
    altc = core.at("altc", [P, 2], 199.5)
    shs = core.at("shs", [P, KT, 2], 199.75)
    altr = core.at("altr", [64, HL], 197)
    cosL = dft[:, 0:4 * HL].rearrange("p (t k) -> p t k", t=4)
    sinL = dft[:, 4 * HL:8 * HL].rearrange("p (t k) -> p t k", t=4)
    cosC = dft[:, 8 * HL:8 * HL + HC]
    sinC = dft[:, 8 * HL + HC:8 * HL + 2 * HC]
    psum, cols, modT = core.psum, core.cols, core.modT
    NCH = 12
    with ExitStack() as st:
        sem = sems(nc, st)
        x_in = [sem(f"x_in{n}") for n in range(5)]
        rows_in, tab_in, id_in = sem("rows_in"), sem("tab_in"), sem("id_in")
        mw_in = [sem("mw_in0"), sem("mw_in1")]
        mw_used = sem("mw_used")
        rowsT, cols_rdy, cond_rdy = sem("rowsT"), sem("cols_rdy"), sem("cond_rdy")
        ss_rdy, var_rdy, std_rdy, eps_rdy = sem("ss_rdy"), sem("var_rdy"), sem("std_rdy"), sem("eps_rdy")
        vec = sem("vec_chain")
        xhat_rdy, fold_rdy, odd_rdy, mod_free = sem("xhat_rdy"), sem("fold_rdy"), sem("odd_rdy"), sem("mod_free")
        coef_rdy = sem("coef_rdy")
        dft_mm, dft_free_a, dft_free_v = sem("dft_mm"), sem("dft_free_a"), sem("dft_free_v")
        tr_mm, tr_free = sem("tr_mm"), sem("tr_free")
        block = st.enter_context(nc.Block())

        @block.sync
        def _(sp):
            sp.dma_start(core.ident[:], io["ident"]).then_inc(id_in, 16)
            r = lambda a: a.rearrange("(n p) -> n p", p=P)
            for lo, src in ((COL_MODB, io["mod_b"].rearrange("l (n p) -> (l n) p", p=P)),
                            (COL_G, io["norm_g"].rearrange("l (n p) -> (l n) p", p=P)),
                            (COL_C, io["c"].rearrange("l (n p) -> (l n) p", p=P)),
                            (COL_CC, r(io["c_ctx"])),
                            (COL_DN, io["dn_norm_g"].rearrange("l (n p) -> (l n) p", p=P))):
                sp.dma_start(rows[lo:lo + src.shape[0], :], src).then_inc(rows_in, 16)
            xv = io["x"][0].rearrange("(n p) d -> p n d", p=P)
            sp.dma_start(xn[:, 0:4, :], xv[:, 0:4, :]).then_inc(x_in[0], 16)
            sp.dma_start(xn[:, 4:8, :], xv[:, 4:8, :]).then_inc(x_in[1], 16)
            sp.dma_start(xn[:, 8:10, :], io["ctx"][0].rearrange("(n p) d -> p n d", p=P)).then_inc(x_in[2], 16)
            sp.dma_start(xm[:, 0:4, :], io["x_mirror"].rearrange("(n p) d -> p n d", p=P)).then_inc(x_in[3], 16)
            sp.dma_start(xm[:, 4, :], io["ctx_mirror"]).then_inc(x_in[4], 16)
            mv = [io["mod_w"][l].rearrange("(k p) (n c) -> n p k c", p=P, c=256) for l in range(2)]
            for s in range(2):
                sp.dma_start(mw[s][:], mv[0][s]).then_inc(mw_in[s], 16)
            sp.dma_start(dft[:], io["dft_tab"]).then_inc(tab_in, 16)
            sp.dma_start(altc[:], io["alt_col"]).then_inc(tab_in, 16)
            sp.dma_start(altr[0:1, :], io["alt_row"][:, 0:HL]).then_inc(tab_in, 16)
            sp.dma_start(altr[32:33, 0:HC], io["alt_row"][:, HL:HL + HC]).then_inc(tab_in, 16)
            with sp.Fori(0, NCH // 2 - 1) as i:
                for s in range(2):
                    sp.wait_ge(mw_used, i * 2 + (s + 1))
                    sp.dma_start(mw[s][:], mv[0][i * 2 + (s + 2)]).then_inc(mw_in[s], 16)
            with sp.Fori(0, NCH // 2) as i:
                for s in range(2):
                    sp.wait_ge(mw_used, i * 2 + (s + NCH - 1))
                    sp.dma_start(mw[s][:], mv[1][i * 2 + s]).then_inc(mw_in[s], 16)

        @block.scalar
        def _(act):
            for n in range(15):
                src = xn[:, n, :] if n < NT else xm[:, n - NT, :]
                act.wait_ge(x_in[0 if n < 4 else 1 if n < 8 else 2 if n < 10 else 3 if n < 14 else 4], 16)
                if n:
                    act.wait_ge(ss_rdy, n)
                act.activation(junk[:], src, ACT.Square, accum_out=ss[:, n:n + 1]).then_inc(ss_rdy, 1)
            act.wait_ge(var_rdy, 1)
            act.activation(ss[:, 0:15], ss[:, 0:15], ACT.Sqrt).then_inc(std_rdy, 1)
            act.wait_ge(cols_rdy, 1)
            for c in range(2):
                act.activation(scond[:, :, c], cols[:, COL_C + 8 * c:COL_C + 8 * c + 8], ACT.Silu).then_inc(cond_rdy, 1)
            act.wait_ge(coef_rdy, 3)
            for k in range(KT):
                b = 3 * (k % 2) * 512
                act.wait_ge(dft_mm, 2 * k + 1)
                a = core.acoef[:, 0, k, 0:1]
                act.activation(pqT[:, k, 1:HL], psum[:, b + 1:b + HL], ACT.Identity, scale=a)
                act.activation(pqT[:, k, 0:1], psum[:, b:b + 1], ACT.Identity,
                               scale=a, bias=shs[:, k, 0:1]).then_inc(dft_free_a, 1)
                for j, (t0, nt) in enumerate(((0, 4), (4, 4), (8, 2))):
                    g = 3 * k + j
                    bb = (6 + g % 2) * 512
                    c = int(j == 2)
                    act.wait_ge(tr_mm, g + 1)
                    act.activation(nT[:, k, t0 * P:(t0 + nt) * P], psum[:, bb:bb + nt * P], ACT.Identity,
                                   scale=core.acoef[:, 0, k, c:c + 1], bias=modT[:, k, c:c + 1]).then_inc(tr_free, 1)

        @block.vector
        def _(dve):
            chain = [0]

            def link(ins):
                chain[0] += 1
                ins.then_inc(vec, 1)
                dve.wait_ge(vec, chain[0])

            dve.memset(core.epst[:], EPS).then_inc(eps_rdy, 1)
            dve.sem_inc(mod_free, 2)
            dve.wait_ge(rowsT, 1)
            dve.tensor_copy(cols[:], psum[:, 0:82]).then_inc(cols_rdy, 1)
            dve.wait_ge(ss_rdy, 15)
            dve.tensor_scalar(ss[:, 0:15], ss[:, 0:15], 1.0 / D, EPS, ALU.mult, ALU.add).then_inc(var_rdy, 1)
            dve.wait_ge(std_rdy, 1)
            link(dve.reciprocal(ss[:, 0:15], ss[:, 0:15]))
            for n in range(15):
                x = xn[:, n, :] if n < NT else xm[:, n - NT, :]
                dve.tensor_scalar(x, x, ss[:, n:n + 1], None, ALU.mult).then_inc(xhat_rdy, 1)
            dve.wait_ge(xhat_rdy, 15)
            link(dve.tensor_tensor(ev[:, 0:4, :], xn[:, 0:4, :], xm[:, 0:4, :], ALU.add))
            link(dve.tensor_tensor(ev[:, 4, :], xn[:, 8, :], xm[:, 4, :], ALU.add))
            dve.tensor_copy(ev[0:1, 0, :], xn[0:1, 0, :])
            dve.tensor_copy(ev[0:1, 4, :], xn[0:1, 8, :])
            dve.tensor_copy(b0[0:1, :], xm[0:1, 0, :])
            dve.tensor_copy(b0[32:33, :], xm[0:1, 4, :]).then_inc(fold_rdy, 1)

            def mod_chunks(layer):
                with dve.Fori(0, NCH // 2) as i:
                    for s in range(2):
                        dve.wait_ge(mw_used, i * 2 + (layer * NCH + s + 1))
                        blk = i * 4 + (layer * 24 + 2 * s)
                        dve.tensor_tensor(modT[:, bass.ds(blk, 2), :],
                                          psum[:, 3072 + 512 * s:3072 + 512 * s + 4].rearrange("p (a b) -> p a b", a=2),
                                          cols[:, bass.ds(blk, 2)].unsqueeze(2).broadcast_to([P, 2, 2]),
                                          ALU.add).then_inc(mod_free, 1)

            def coefs(layer):
                dve.wait_ge(mod_free, 2 + NCH * (layer + 1))
                g = cols[:, COL_G + 8 * layer:COL_G + 8 * layer + 8].unsqueeze(2).broadcast_to([P, KT, 2])
                link(dve.tensor_scalar(core.acoef[:, layer], modT[:, 24 * layer + 8:24 * layer + 16, :], 1.0, None, ALU.add))
                dve.tensor_tensor(core.acoef[:, layer], core.acoef[:, layer], g, ALU.mult).then_inc(coef_rdy, 1)

            dve.wait_ge(cols_rdy, 1)
            mod_chunks(0)
            coefs(0)
            dve.tensor_scalar(shs[:, :, 0], modT[:, 0:8, 0], float(LAT) ** 0.5, None, ALU.mult).then_inc(coef_rdy, 1)
            dve.tensor_scalar(shs[:, :, 1], modT[:, 0:8, 1], float(CTX) ** 0.5, None, ALU.mult).then_inc(coef_rdy, 1)
            dve.wait_ge(coef_rdy, 3)
            for k in range(KT):
                b = 3 * (k % 2) * 512
                dve.wait_ge(dft_mm, 2 * k + 2)
                dve.tensor_scalar(pqT[:, k, HL:2 * HL], psum[:, b + 512:b + 1024],
                                  core.acoef[:, 0, k, 0:1], None, ALU.mult)
                dve.tensor_scalar(pqT[:, k, LAT + 1:TOK], psum[:, b + 1025:b + 1024 + 2 * HC],
                                  core.acoef[:, 0, k, 1:2], None, ALU.mult)
                dve.tensor_scalar(pqT[:, k, LAT:LAT + 1], psum[:, b + 1024:b + 1025],
                                  core.acoef[:, 0, k, 1:2], shs[:, k, 1:2], ALU.mult, ALU.add).then_inc(dft_free_v, 1)
            mod_chunks(1)
            coefs(1)

        @block.gpsimd
        def _(pool):
            pool.wait_ge(fold_rdy, 1)
            pool.tensor_tensor(xm[:, 0:4, :], xn[:, 0:4, :], xm[:, 0:4, :], ALU.subtract).then_inc(odd_rdy, 1)
            pool.tensor_tensor(xm[:, 4, :], xn[:, 8, :], xm[:, 4, :], ALU.subtract).then_inc(odd_rdy, 1)

        @block.tensor
        def _(pe):
            pe.wait_ge(id_in, 16)
            pe.wait_ge(rows_in, 80)
            pe.transpose(psum[:, 0:82], rows[:], core.ident[0:82, 0:82]).then_inc(rowsT, 1)

            def mod_chunks(layer):
                with pe.Fori(0, NCH // 2) as i:
                    for s in range(2):
                        pe.wait_ge(mw_in[s], i * 16 + (16 + 16 * layer * (NCH // 2)))
                        pe.wait_ge(mod_free, i * 2 + (layer * NCH + s + 1))
                        for b in range(2):
                            for k in range(KT):
                                last = pe.matmul(psum[:, 3072 + 512 * s + 2 * b:3072 + 512 * s + 2 * b + 2],
                                                 mw[s][:, k, b * P:(b + 1) * P], scond[:, k, :],
                                                 start=(k == 0), stop=(k == KT - 1))
                        last.then_inc(mw_used, 1)

            pe.wait_ge(cond_rdy, 2)
            mod_chunks(0)
            pe.wait_ge(tab_in, 64)
            pe.wait_ge(fold_rdy, 1)
            pe.wait_ge(odd_rdy, 2)
            pe.wait_ge(mod_free, 2 + NCH)
            for k in range(KT):
                b = 3 * (k % 2) * 512
                ch = slice(k * P, (k + 1) * P)
                if k >= 2:
                    pe.wait_ge(dft_free_a, k - 1)
                    pe.wait_ge(dft_free_v, k - 1)
                for t in range(4):
                    pe.matmul(psum[:, b:b + HL], ev[:, t, ch], cosL[:, t, :], start=(t == 0), stop=False)
                pe.matmul(psum[:, b:b + HL], b0[0:1, ch], altr[0:1, 0:HL], start=False, stop=True).then_inc(dft_mm, 1)
                pe.matmul(psum[:, b + 1024:b + 1024 + HC], ev[:, 4, ch], cosC, start=True, stop=False)
                pe.matmul(psum[:, b + 1024:b + 1024 + HC], b0[32:33, ch], altr[32:33, 0:HC],
                          start=False, stop=True)
                for t in range(4):
                    pe.matmul(psum[:, b + 512:b + 1024], xm[:, t, ch], sinL[:, t, :], start=(t == 0), stop=False,
                              skip_group_check=True)
                for t in range(4):
                    pe.matmul(psum[:, b + 512:b + 513], ev[:, t, ch], altc[:, 0:1], start=False, stop=False,
                              skip_group_check=True)
                pe.matmul(psum[:, b + 512:b + 513], b0[0:1, ch], altr[0:1, 0:1], start=False, stop=True,
                          skip_group_check=True)
                o = b + 1024 + HC
                pe.matmul(psum[:, o:o + HC], xm[:, 4, ch], sinC, start=True, stop=False, skip_group_check=True)
                pe.matmul(psum[:, o:o + 1], ev[:, 4, ch], altc[:, 1:2], start=False, stop=False, skip_group_check=True)
                pe.matmul(psum[:, o:o + 1], b0[32:33, ch], altr[32:33, 0:1], start=False, stop=True,
                          skip_group_check=True).then_inc(dft_mm, 1)
                for j, (t0, nt) in enumerate(((0, 4), (4, 4), (8, 2))):
                    g = 3 * k + j
                    bb = (6 + g % 2) * 512
                    if g >= 2:
                        pe.wait_ge(tr_free, g - 1)
                    for t in range(nt):
                        last = pe.transpose(psum[:, bb + t * P:bb + (t + 1) * P], xn[:, t0 + t, ch], core.ident[:])
                    last.then_inc(tr_mm, 1)
            pe.wait_ge(tr_free, 3 * KT)
            mod_chunks(1)


def fourier_phase(core, io):
    nc, psum = core.nc, core.psum
    pqT = core.at("pqT", [P, KT, TOK], 0)
    nT = core.at("nT", [P, KT, TOK], 40)
    wz = [core.at(f"wz{s}", [P, KT, FD], 80 + 8 * s) for s in range(2)]
    wu = [core.at(f"wu{s}", [P, KT, FD], 96 + 8 * s) for s in range(2)]
    wg = [core.at(f"wg{s}", [P, 2, FD], 112 + 2 * s) for s in range(2)]
    chd = core.at("chd", [P, 2, 2, FD], 116)
    csw = [core.at(f"csw{s}", [P, 2, 2, FD], 120 + 4 * s) for s in range(2)]
    zs = core.at("zs", [P, 2, TOK], 128)
    pq = core.at("pq", [P, 2, TOK], 148)
    es = core.at("es", [P, 2, HL + HC + 4], 168)
    f = core.at("f", [P, 2, TOK], 174)
    y = core.at("y", [P, 2, TOK], 184)
    w_in = io["fn_w_in"][0].rearrange("(k p) (n c) -> n p k c", p=P, c=FD)
    w_grp = io["fn_w_grp"][0].rearrange("g (k p) c -> g p k c", p=P)
    y_v = core.y_d.rearrange("(n p) t -> n p t", p=P)
    SET = [0, 1536]
    CW = 3072
    with ExitStack() as st:
        sem = sems(nc, st)
        chd_in = sem("chd_in")
        wu_in, wz_in, wg_in = ([sem(f"{n}_in{s}") for s in range(2)] for n in ("wu", "wz", "wg"))
        cw_mm, pq_mm, z_mm, eo_mm = sem("cw_mm"), sem("pq_mm"), sem("z_mm"), sem("eo_mm")
        cw_rdy, pq_rdy, zs_rdy = sem("cw_rdy"), sem("pq_rdy"), sem("zs_rdy")
        es_rdy, f_rdy, y_rdy, y_stored = sem("es_rdy"), sem("f_rdy"), sem("y_rdy"), [sem("y_stored0"), sem("y_stored1")]
        block = st.enter_context(nc.Block())

        @block.sync
        def _(sp):
            def load(g, s):
                sp.dma_start(wg[s][:], w_grp[g]).then_inc(wg_in[s], 16)
                sp.dma_start(wu[s][:], w_in[g]).then_inc(wu_in[s], 16)
                sp.dma_start(wz[s][:], w_in[g + FG]).then_inc(wz_in[s], 16)

            def store(g, gi):
                for m in range(2):
                    sp.wait_ge(y_rdy, g * 2 + (m + 3))
                    sp.dma_start(y_v[g * 2 + m], y[:, m, :]).then_inc(y_stored[m], 16)

            sp.dma_start(chd[:], io["ch_dft"]).then_inc(chd_in, 16)
            for m in range(2):
                sp.sem_inc(y_stored[m], 16)
            load(0, 0)
            load(1, 1)
            with sp.Fori(0, FG // 2 - 1) as i:
                for s in range(2):
                    store(i * 2 + s, i)
                    load(i * 2 + (s + 2), s)
            for g in range(FG - 2, FG):
                store(g, None)
            for m in range(2):
                sp.wait_ge(y_stored[m], 16 * (FG + 1))

        @block.tensor
        def _(pe):
            pe.wait_ge(chd_in, 16)
            with pe.Fori(0, FG // 2) as i:
                for s in range(2):
                    g = i * 2 + s
                    pe.wait_ge(wg_in[s], i * 16 + 16)
                    pe.wait_ge(cw_rdy, g + 1)
                    for t in range(2):
                        for ct in range(2):
                            for k in range(2):
                                last = pe.matmul(psum[:, CW + 512 * t + FD * ct:CW + 512 * t + FD * ct + FD],
                                                 chd[:, t, k, ct * P:(ct + 1) * P], wg[s][:, k, :],
                                                 start=(k == 0), stop=(k == 1))
                    last.then_inc(cw_mm, 1)
                    for w, rhs, w_in_sem, done, free in ((wu, pqT, wu_in, pq_mm, f_rdy), (wz, nT, wz_in, z_mm, pq_rdy)):
                        pe.wait_ge(w_in_sem[s], i * 16 + 16)
                        for m in range(2):
                            pe.wait_ge(free, g * 2 + (m + 1))
                            for lo, n in ((0, 512), (512, 512), (1024, 256)):
                                for k in range(KT):
                                    last = pe.matmul(psum[:, SET[m] + lo:SET[m] + lo + n],
                                                     w[s][:, k, m * P:(m + 1) * P], rhs[:, k, lo:lo + n],
                                                     start=(k == 0), stop=(k == KT - 1))
                            last.then_inc(done, 1)
                    pe.wait_ge(cw_rdy, g + 2)
                    pe.wait_ge(pq_rdy, g * 2 + 2)
                    for m in range(2):
                        pe.wait_ge(zs_rdy, g * 2 + (m + 1))
                        b, dc = SET[m], slice(m * P, (m + 1) * P)
                        for t, off, lo, n in ((0, 0, 0, HL), (1, 512, HL, HL), (0, 1024, LAT, HC),
                                              (1, 1024 + HC, LAT + HC, HC), (0, 1024 + 2 * HC, HL, 1),
                                              (0, 1024 + 2 * HC + 1, LAT + HC, 1)):
                            for k in range(2):
                                last = pe.matmul(psum[:, b + off:b + off + n], csw[s][:, t, k, dc],
                                                 pq[:, k, lo:lo + n], start=(k == 0), stop=(k == 1))
                        last.then_inc(eo_mm, 1)

        @block.scalar
        def _(act):
            act.sem_inc(cw_rdy, 1)
            with act.Fori(0, FG // 2) as i:
                for s in range(2):
                    g = i * 2 + s
                    act.wait_ge(cw_mm, g + 1)
                    act.activation(csw[s][:].rearrange("p a b c -> p (a b c)"), psum[:, CW:CW + 1024], ACT.Copy).then_inc(cw_rdy, 1)
                    for m in range(2):
                        act.wait_ge(z_mm, g * 2 + (m + 1))
                        act.wait_ge(y_rdy, g * 2 + (m + 1))
                        act.activation(zs[:, m, :], psum[:, SET[m]:SET[m] + TOK], ACT.Silu).then_inc(zs_rdy, 1)
                    for m in range(2):
                        b = SET[m]
                        act.wait_ge(eo_mm, g * 2 + (m + 1))
                        act.activation(es[:, m, 0:HL], psum[:, b:b + HL], ACT.Copy)
                        act.activation(es[:, m, HL:HL + HC], psum[:, b + 1024:b + 1024 + HC], ACT.Copy)
                        act.activation(f[:, m, 0:LAT + 1:LAT], psum[:, b:b + 1025:1024], ACT.Copy)
                        act.activation(f[:, m, HL:LAT + HC + 1:HL + HC], psum[:, b + 1024 + 2 * HC:b + 1026 + 2 * HC],
                                       ACT.Copy).then_inc(es_rdy, 1)

        @block.vector
        def _(dve):
            dve.sem_inc(f_rdy, 2)
            with dve.Fori(0, FG // 2) as i:
                for s in range(2):
                    g = i * 2 + s
                    for m in range(2):
                        dve.wait_ge(pq_mm, g * 2 + (m + 1))
                        dve.tensor_copy(pq[:, m, :], psum[:, SET[m]:SET[m] + TOK]).then_inc(pq_rdy, 1)
                    for m in range(2):
                        b = SET[m]
                        dve.wait_ge(es_rdy, g * 2 + (m + 1))
                        for o, lo, L in ((512, 0, LAT), (1024 + HC, HL, CTX)):
                            t0, h = (0 if L == LAT else LAT), L // 2
                            for op, dst in ((ALU.subtract, f[:, m, t0 + 1:t0 + h]), (ALU.add, f[:, m, t0 + L - 1:t0 + h:-1])):
                                last = dve.tensor_tensor(dst, es[:, m, lo + 1:lo + h], psum[:, b + o + 1:b + o + h], op)
                        last.then_inc(f_rdy, 1)

        @block.gpsimd
        def _(pool):
            pool.sem_inc(y_rdy, 2)
            with pool.Fori(0, FG // 2) as i:
                for s in range(2):
                    g = i * 2 + s
                    for m in range(2):
                        pool.wait_ge(f_rdy, g * 2 + (m + 3))
                        pool.wait_ge(y_stored[m], g * 16 + 16)
                        pool.tensor_tensor(y[:, m, :], f[:, m, :], zs[:, m, :], ALU.mult).then_inc(y_rdy, 1)


def output_phase(core, io, layer):
    nc, psum, ident = core.nc, core.psum, core.ident
    last_layer = layer == 1
    name = lambda n: f"{n}_o{layer}"
    n1T = None if last_layer else core.at("n1T", [P, KT, TOK], 0)
    wo = core.at(name("wo"), [P, 16, D], 40)
    yb = [core.at(name(f"yb{s}"), [P, 16, P], 104 + 8 * s) for s in range(2)]
    h = [core.at(name(f"h{s}"), [P, D], 120 + 4 * s) for s in range(2)]
    gx = [core.at(name(f"gx{s}"), [P, D], 128 + 4 * s) for s in range(2)]
    gate = core.at(name("gate"), [P, 2, D], 136)
    fg = core.at(name("fg"), [P, D], 144)
    junk = core.at(name("junk"), [P, D], 148)
    st_ = core.at(name("st"), [P, 2, 4], 152)
    nlat = NL
    y_v = (core.y2_d if last_layer else core.y_d).rearrange("(c p) (n t) -> n p c t", p=P, t=P)
    h_v = (core.h_d if last_layer else io["x"][0]).rearrange("(n p) d -> n p d", p=P)
    c_v = io["ctx"][0].rearrange("(n p) d -> n p d", p=P)
    dst_v = (io["out"][0] if last_layer else core.h_d).rearrange("(n p) d -> n p d", p=P)
    w_v = (io["dn_w_out"] if last_layer else io["fn_w_out"])[0].rearrange("(c p) d -> p c d", p=P)
    tiles = NL if last_layer else NT
    conds = 1 if last_layer else 2
    with ExitStack() as st:
        sem = sems(nc, st)
        wo_in = [sem(f"wo_in{q}") for q in range(4)]
        y_in, h_in, stored = ([sem(f"{n}{s}") for s in range(2)] for n in ("y_in", "h_in", "h_stored"))
        fg_in, g_mm, gate_rdy = sem("fg_in"), sem("g_mm"), sem("gate_rdy")
        o_mm, gx_rdy, h_rdy, ss_rdy, var_rdy = sem("o_mm"), sem("gx_rdy"), sem("h_rdy"), sem("ss_rdy"), sem("var_rdy")
        std_rdy, rstd_rdy, n_rdy, t_mm, t_free = sem("std_rdy"), sem("rstd_rdy"), sem("n_rdy"), sem("t_mm"), sem("t_free")
        block = st.enter_context(nc.Block())

        def tiles_loop(eng, body):
            with eng.Fori(0, NL // 2) as i:
                for s in range(2):
                    body(i * 2 + s, s, i, 0)
            for n in range(NL, tiles):
                body(n, n % 2, n // 2, 1)

        @block.sync
        def _(sp):
            def load(n, s, ctx_tile):
                sp.dma_start(yb[s][:], y_v[n]).then_inc(y_in[s], 16)
                sp.dma_start(h[s][:], c_v[n - NL] if ctx_tile else h_v[n]).then_inc(h_in[s], 16)

            for q in range(4):
                sp.dma_start(wo[:, 4 * q:4 * q + 4, :], w_v[:, 4 * q:4 * q + 4, :]).then_inc(wo_in[q], 16)
                if q == 0:
                    load(0, 0, 0)
            load(1, 1, 0)
            if last_layer:
                sp.dma_start(fg[:], io["final_g"].rearrange("(a n) -> a n", a=1).broadcast_to([P, D])).then_inc(fg_in, 16)

            def turn(n, s, i, store_it, load_ctx):
                if store_it:
                    sp.wait_ge(n_rdy if last_layer else h_rdy, n + 1)
                    sp.dma_start(dst_v[n], h[s][:]).then_inc(stored[s], 16)
                if load_ctx is not None:
                    sp.wait_ge(o_mm, n + 1)
                    sp.wait_ge(n_rdy, n + 1)
                    if store_it:
                        sp.wait_ge(stored[s], i * 16 + 16)
                    load(n + 2, s, load_ctx)

            with sp.Fori(0, NL // 2 - 1) as i:
                for s in range(2):
                    turn(i * 2 + s, s, i, True, 0)
            for n in range(NL - 2, NL):
                turn(n, n % 2, n // 2, True, 1 if tiles > NL else None)
            for s in range(2):
                sp.wait_ge(stored[s], 16 * NL // 2)

        @block.tensor
        def _(pe):
            for c in range(conds):
                for k in range(KT):
                    col = core.modT[:, 24 * layer + 16 + k, c:c + 1].broadcast_to([P, P])
                    last = pe.matmul(psum[:, 1024 * c + k * P:1024 * c + (k + 1) * P], col, ident[:], start=True, stop=True)
            last.then_inc(g_mm, 1)
            for q in range(4):
                pe.wait_ge(wo_in[q], 16)
            pe.wait_ge(gate_rdy, 1)

            def norm_transposes(n, s):
                pe.wait_ge(n_rdy, n + 1)
                pe.wait_ge(t_free, n + 1)
                b = 2048 + 1024 * s
                for k in range(KT):
                    last = pe.transpose(psum[:, b + k * P:b + (k + 1) * P], gx[s][:, k * P:(k + 1) * P], ident[:])
                last.then_inc(t_mm, 1)

            def body(n, s, i, c):
                pe.wait_ge(y_in[s], i * 16 + 16)
                pe.wait_ge(gx_rdy, n + 1)
                for half in range(2):
                    o = 1024 * s + 512 * half
                    for k in range(16):
                        last = pe.matmul(psum[:, o:o + 512], yb[s][:, k, :], wo[:, k, 512 * half:512 * half + 512],
                                         start=(k == 0), stop=(k == 15))
                last.then_inc(o_mm, 1)

            if last_layer:
                tiles_loop(pe, body)
            else:
                body(0, 0, 0, 0)
                with pe.Fori(0, NL // 2) as i:
                    for s in range(2):
                        n = i * 2 + s
                        pe.wait_ge(y_in[1 - s], i * 16 + (16 + 16 * s))
                        pe.wait_ge(gx_rdy, n + 2)
                        for half in range(2):
                            o = 1024 * (1 - s) + 512 * half
                            for k in range(16):
                                last = pe.matmul(psum[:, o:o + 512], yb[1 - s][:, k, :],
                                                 wo[:, k, 512 * half:512 * half + 512], start=(k == 0), stop=(k == 15))
                        last.then_inc(o_mm, 1)
                        norm_transposes(n, s)
                body(NL + 1, 1, NL // 2, 1)
                norm_transposes(NL, 0)
                norm_transposes(NL + 1, 1)

        @block.vector
        def _(dve):
            dve.sem_inc(gx_rdy, 2)
            dve.wait_ge(g_mm, 1)
            dve.tensor_copy(gate[:, 0:conds, :].rearrange("p c d -> p (c d)"), psum[:, 0:1024 * conds]).then_inc(gate_rdy, 1)
            dve.wait_ge(gate_rdy, 1)
            if last_layer:
                dve.wait_ge(fg_in, 16)

            def body(n, s, i, c):
                dve.wait_ge(o_mm, n + 1)
                if not last_layer:
                    dve.wait_ge(t_free, n + 1)
                dve.tensor_tensor(gx[s][:], psum[:, 1024 * s:1024 * s + 1024], gate[:, c, :], ALU.mult).then_inc(gx_rdy, 1)
                dve.wait_ge(gx_rdy, n + 3)
                dve.wait_ge(h_in[s], i * 16 + 16)
                dve.tensor_tensor(h[s][:], h[s][:], gx[s][:], ALU.add).then_inc(h_rdy, 1)
                dve.wait_ge(ss_rdy, n + 1)
                dve.tensor_scalar(st_[:, s, 1:2], st_[:, s, 0:1], 1.0 / D, EPS, ALU.mult, ALU.add).then_inc(var_rdy, 1)
                dve.wait_ge(std_rdy, n + 1)
                dve.reciprocal(st_[:, s, 3:4], st_[:, s, 2:3]).then_inc(rstd_rdy, 1)
                dve.wait_ge(rstd_rdy, n + 1)
                if last_layer:
                    dve.scalar_tensor_tensor(h[s][:], h[s][:], st_[:, s, 3:4], fg[:], ALU.mult, ALU.mult).then_inc(n_rdy, 1)
                else:
                    dve.tensor_scalar(gx[s][:], h[s][:], st_[:, s, 3:4], None, ALU.mult).then_inc(n_rdy, 1)

            tiles_loop(dve, body)

        @block.scalar
        def _(act):
            if not last_layer:
                act.sem_inc(t_free, 2)

            def stats(n, s, i, c):
                act.wait_ge(h_rdy, n + 1)
                act.activation(junk[:], h[s][:], ACT.Square, accum_out=st_[:, s, 0:1]).then_inc(ss_rdy, 1)
                act.wait_ge(var_rdy, n + 1)
                act.activation(st_[:, s, 2:3], st_[:, s, 1:2], ACT.Sqrt).then_inc(std_rdy, 1)

            def to_n1T(n, s, i, c):
                act.wait_ge(t_mm, n + 1)
                b = 2048 + 1024 * s
                for k in range(KT):
                    last = act.activation(n1T[:, k, bass.ts(n, P)], psum[:, b + k * P:b + (k + 1) * P], ACT.Identity,
                                          scale=core.acoef[:, 1, k, c:c + 1], bias=core.modT[:, 24 + k, c:c + 1])
                last.then_inc(t_free, 1)

            def body(n, s, i, c):
                stats(n, s, i, c)
                if not last_layer:
                    to_n1T(n, s, i, c)

            tiles_loop(act, body)


def project_phase(core, io):
    nc, psum, ident = core.nc, core.psum, core.ident
    n1T = core.at("n1T", [P, KT, TOK], 0)
    wq = core.at("wq", [P, KT, P], 40)
    wk = core.at("wk", [P, KT, P], 44)
    wv = core.at("wv", [P, KT, DV], 48)
    wz = core.at("wz_d", [P, KT, DV], 56)
    PADR, PADC = GR + 2, GW + 2
    NPAD = PADR * PADC + CTX + 2
    pad = [core.at(f"pad{s}", [P, NPAD], 64 + 6 * s) for s in range(2)]
    acc = [core.at(f"acc{s}", [P, TOK], 76 + 5 * s) for s in range(2)]
    sil = [core.at(f"sil{s}", [P, TOK], 86 + 5 * s) for s in range(2)]
    qt = core.at("qt", [P, NL, P], 96)
    kt = core.at("kt", [P, NT, P], 100)
    vt = [core.at(f"vt{s}", [P, NT, P], 105 + 5 * s) for s in range(2)]
    qT = core.at("qT", [P, LAT], 115)
    kT = core.at("kT", [P, TOK], 119)
    zs = [core.at(f"zs_d{s}", [P, LAT], 124 + 4 * s) for s in range(2)]
    sq = core.at("sq", [P, NT, P], 132)
    ssq = core.at("ssq", [P, 2, 3, 16], 137)
    wab = core.at("wab", [P, KT, 32], 138)
    crow = core.at("crow", [9, 4096], 139)
    cw = core.at("cw", [P, 32, 9], 155)
    cwh = core.at("cwh", [P, 4, 9], 157)
    ab = core.at("ab", [P, 2, 16], 158)
    gw = [core.at(f"gw{s}", [P, NT, 16], 159 + s) for s in range(4)]
    wi = io["dn_w_in"][0].rearrange("(k p) c -> p k c", p=P)
    QO, KO, VO, ZO, AO = 0, D, 2 * D, 2 * D + FW, 2 * D + 2 * FW
    k_v = core.k_d.rearrange("(n p) (h c) -> h p n c", p=P, c=P)
    v_v = core.v_d.rearrange("(n p) (h c) -> h p n c", p=P, c=P)
    z_v = core.z_d.rearrange("(n p) t -> n p t", p=P)
    SET = [0, 1536]
    FULL, LATO = ((0, 512), (512, 512), (1024, 256)), ((0, 512), (512, 512))
    with ExitStack() as st:
        sem = sems(nc, st)
        misc_in = sem("misc_in")
        w_in = {n: sem(f"w{n}_in") for n in "qkvz"}
        ab_mm, tap_mm, tap_rdy = sem("ab_mm"), sem("tap_mm"), sem("tap_rdy")
        gch, gact = sem("decay_vec"), sem("decay_act")
        mm = sem("proj_mm")
        evac = sem("proj_evac")
        conv = sem("conv_done")
        silu = sem("silu_done")
        tmm, tfree = sem("t_mm"), sem("t_free_d")
        sq_rdy, red, var, std, nrm = sem("sq_rdy"), sem("red"), sem("var"), sem("std"), sem("nrm")
        taps, taps_used = sem("taps"), sem("taps_used")
        vec = sem("conv_chain")
        out_s = {n: sem(f"{n}_stored") for n in ("qT", "k", "kT", "v0", "v1", "z0", "z1")}
        block = st.enter_context(nc.Block())
        T = {"q": 0, "k": 2, "qT": 5, "v0": 7, "kT": 10, "v1": 13}
        NB = 16

        @block.sync
        def _(sp):
            sp.dma_start(wab[:], wi[:, :, AO:AO + 32]).then_inc(misc_in, 16)
            sp.dma_start(ab[:, 0, :], io["dn_dt_bias"].rearrange("a b c -> a (b c)").broadcast_to([P, 16])).then_inc(misc_in, 16)
            sp.dma_start(ab[:, 1, :], io["dn_a_log"].rearrange("a b c -> a (b c)").broadcast_to([P, 16])).then_inc(misc_in, 16)
            sp.dma_start(crow[:], io["dn_conv"][0].rearrange("a b c -> (a b) c")).then_inc(misc_in, 16)
            wqv, wkv, wvv, wzv = (wi[:, :, o:o + n * H].rearrange("p k (h c) -> h p k c", c=n)
                                  for o, n in ((QO, DK), (KO, DK), (VO, DV), (ZO, DV)))
            src = {"q": (wq, wqv), "k": (wk, wkv), "v": (wv, wvv), "z": (wz, wzv)}

            def load(n, hh):
                sp.dma_start(src[n][0][:], src[n][1][hh]).then_inc(w_in[n], 16)

            for n in "qkvz":
                load(n, 0)
            for n in out_s:
                sp.sem_inc(out_s[n], 16)

            def turn(hh, more):
                sp.wait_ge(mm, hh * 6 + 1)
                if more:
                    load("q", hh + 1)
                sp.wait_ge(mm, hh * 6 + 2)
                if more:
                    load("k", hh + 1)
                sp.wait_ge(tfree, hh * NB + (2 + T["qT"] + 2))
                sp.dma_start(core.qT_d[hh], qT[:]).then_inc(out_s["qT"], 16)
                sp.wait_ge(mm, hh * 6 + 4)
                if more:
                    load("v", hh + 1)
                sp.wait_ge(tfree, hh * NB + (2 + T["v0"] + 3))
                sp.dma_start(v_v[hh * 2], vt[0][:]).then_inc(out_s["v0"], 16)
                sp.wait_ge(nrm, hh * 2 + 2)
                sp.dma_start(k_v[hh], kt[:]).then_inc(out_s["k"], 16)
                sp.wait_ge(tfree, hh * NB + (2 + T["kT"] + 3))
                sp.dma_start(core.kT_d[hh], kT[:]).then_inc(out_s["kT"], 16)
                sp.wait_ge(evac, hh * 6 + 7)
                sp.dma_start(z_v[hh * 2], zs[0][:]).then_inc(out_s["z0"], 16)
                sp.wait_ge(tfree, hh * NB + (2 + T["v1"] + 3))
                sp.dma_start(v_v[hh * 2 + 1], vt[1][:]).then_inc(out_s["v1"], 16)
                sp.wait_ge(evac, hh * 6 + 8)
                if more:
                    load("z", hh + 1)
                sp.dma_start(z_v[hh * 2 + 1], zs[1][:]).then_inc(out_s["z1"], 16)

            with sp.Fori(0, H - 1) as hh:
                turn(hh, True)
            turn(H - 1, False)
            for n in out_s:
                sp.wait_ge(out_s[n], 16 * (H + 1))

        @block.tensor
        def _(pe):
            pe.wait_ge(misc_in, 64)
            for n in range(NT):
                for k in range(KT):
                    last = pe.matmul(psum[:, n * 32:(n + 1) * 32], n1T[:, k, n * P:(n + 1) * P], wab[:, k, :],
                                     start=(k == 0), stop=(k == KT - 1))
            last.then_inc(ab_mm, 1)
            for t in range(32):
                last = pe.transpose(psum[:, 3072 + 9 * t:3072 + 9 * t + 9], crow[:, t * P:(t + 1) * P], ident[0:9, 0:9])
            last.then_inc(tap_mm, 1)
            pe.wait_ge(gch, 2)
            pe.wait_ge(tap_rdy, 1)

            with pe.Fori(0, H) as hh:
                def product(j, w, cols, groups):
                    pe.wait_ge(evac, hh * 6 + (j + 1))
                    for lo, n in groups:
                        for k in range(KT):
                            last = pe.matmul(psum[:, SET[j % 2] + lo:SET[j % 2] + lo + n], w[:, k, cols],
                                             n1T[:, k, lo:lo + n], start=(k == 0), stop=(k == KT - 1))
                    last.then_inc(mm, 1)

                def transposes(what, src, tiles):
                    for j, t0 in enumerate(range(0, tiles, 4)):
                        b = T[what] + j
                        pe.wait_ge(tfree, hh * NB + (b + 1))
                        for t in range(t0, min(t0 + 4, tiles)):
                            o = 3072 + 512 * (b % 2) + (t - t0) * P
                            last = pe.transpose(psum[:, o:o + P], src(t), ident[:])
                        last.then_inc(tmm, 1)

                chan = lambda s: (lambda t: sil[s][:, t * P:(t + 1) * P])
                pe.wait_ge(w_in["q"], hh * 16 + 16)
                product(0, wq, slice(0, P), LATO)
                pe.wait_ge(w_in["k"], hh * 16 + 16)
                product(1, wk, slice(0, P), FULL)
                pe.wait_ge(silu, hh * 4 + 1)
                transposes("q", chan(0), NL)
                pe.wait_ge(w_in["v"], hh * 16 + 16)
                product(2, wv, slice(0, P), FULL)
                pe.wait_ge(silu, hh * 4 + 2)
                transposes("k", chan(1), NT)
                pe.wait_ge(nrm, hh * 2 + 1)
                transposes("qT", lambda t: qt[:, t, :], NL)
                product(3, wv, slice(P, 2 * P), FULL)
                pe.wait_ge(silu, hh * 4 + 3)
                transposes("v0", chan(0), NT)
                pe.wait_ge(nrm, hh * 2 + 2)
                transposes("kT", lambda t: kt[:, t, :], NT)
                pe.wait_ge(w_in["z"], hh * 16 + 16)
                product(4, wz, slice(0, P), LATO)
                pe.wait_ge(silu, hh * 4 + 4)
                transposes("v1", chan(1), NT)
                product(5, wz, slice(P, 2 * P), LATO)

        def inner(s):
            g = pad[s][:, 0:PADR * PADC].rearrange("p (r c) -> p r c", c=PADC)
            return g, pad[s][:, PADR * PADC:NPAD]

        @block.scalar
        def _(act):
            act.sem_inc(evac, 2)
            act.sem_inc(tfree, 2)
            act.wait_ge(tap_mm, 1)
            act.activation(cw[:].rearrange("p t n -> p (t n)"), psum[:, 3072:3072 + 288], ACT.Copy).then_inc(tap_rdy, 1)
            act.wait_ge(gch, 8)
            act.activation(gw[1][:], gw[1][:], ACT.Exp, scale=-1.0).then_inc(gact, 1)
            act.activation(gw[3][:], gw[3][:], ACT.Exp, scale=-1.0).then_inc(gact, 1)
            act.activation(gw[2][:], gw[2][:], ACT.Exp).then_inc(gact, 1)
            act.activation(ab[:, 1, :], ab[:, 1, :], ACT.Exp).then_inc(gact, 1)
            act.wait_ge(gch, 10)
            act.activation(gw[1][:], gw[1][:], ACT.Ln).then_inc(gact, 1)
            act.wait_ge(vec, 1)

            with act.Fori(0, H) as hh:
                def to_pad(j):
                    act.wait_ge(mm, hh * 6 + (j + 1))
                    s, b = j % 2, SET[j % 2]
                    g, c = inner(s)
                    last = act.activation(g[:, 1:GR + 1, 1:GW + 1], psum[:, b:b + LAT].rearrange("p (r c) -> p r c", c=GW), ACT.Copy)
                    if j:
                        last = act.activation(c[:, 1:CTX + 1], psum[:, b + LAT:b + TOK], ACT.Copy)
                    last.then_inc(evac, 1)

                def do_silu(j):
                    act.wait_ge(conv, hh * 4 + (j + 1))
                    n = TOK if j else LAT
                    act.activation(sil[j % 2][:, 0:n], acc[j % 2][:, 0:n], ACT.Silu).then_inc(silu, 1)

                def tokens(what, dst, tiles, squares):
                    for j, t0 in enumerate(range(0, tiles, 4)):
                        b, n = T[what] + j, min(4, tiles - t0)
                        src = psum[:, 3072 + 512 * (b % 2):3072 + 512 * (b % 2) + n * P].rearrange("p (t c) -> p t c", c=P)
                        act.wait_ge(tmm, hh * NB + (b + 1))
                        if squares:
                            act.activation(sq[:, t0:t0 + n, :], src, ACT.Square).then_inc(sq_rdy, 1)
                        act.activation(dst[:, t0:t0 + n, :], src, ACT.Copy).then_inc(tfree, 1)

                def std_of(j):
                    act.wait_ge(var, hh * 2 + (j + 1))
                    act.activation(ssq[:, j, 1, 0:NT], ssq[:, j, 0, 0:NT], ACT.Sqrt).then_inc(std, 1)

                act.wait_ge(taps_used, hh + 1)
                for j, lo in ((0, hh), (1, hh + 8), (2, hh * 2 + 16), (3, hh * 2 + 17)):
                    last = act.activation(cwh[:, j, :], cw[:, bass.ds(lo, 1), :].rearrange("p a n -> p (a n)"), ACT.Copy)
                last.then_inc(taps, 1)
                cm = lambda t: t[:].rearrange("p (t c) -> p t c", c=P)
                to_pad(0)
                do_silu(0)
                to_pad(1)
                tokens("q", qt, NL, True)
                do_silu(1)
                std_of(0)
                to_pad(2)
                act.wait_ge(out_s["k"], hh * 16 + 16)
                tokens("k", kt, NT, True)
                act.wait_ge(out_s["qT"], hh * 16 + 16)
                tokens("qT", cm(qT), NL, False)
                do_silu(2)
                std_of(1)
                to_pad(3)
                act.wait_ge(out_s["v0"], hh * 16 + 16)
                tokens("v0", vt[0], NT, False)
                act.wait_ge(out_s["kT"], hh * 16 + 16)
                tokens("kT", cm(kT), NT, False)
                do_silu(3)
                for m in range(2):
                    act.wait_ge(mm, hh * 6 + (5 + m))
                    act.wait_ge(out_s[f"z{m}"], hh * 16 + 16)
                    act.activation(zs[m][:], psum[:, SET[m]:SET[m] + LAT], ACT.Silu).then_inc(evac, 1)
                    if m == 0:
                        act.wait_ge(out_s["v1"], hh * 16 + 16)
                        tokens("v1", vt[1], NT, False)

        @block.vector
        def _(dve):
            dve.sem_inc(taps_used, 1)
            dve.memset(pad[0][:], 0.0)
            dve.memset(pad[1][:], 0.0).then_inc(vec, 1)
            dve.memset(ssq[:], 1.0).then_inc(vec, 1)
            dve.wait_ge(ab_mm, 1)
            ga = psum[:, 0:320].rearrange("p (n c) -> p n c", c=32)
            dt = ab[:, 0, :].unsqueeze(1).broadcast_to([P, NT, 16])
            n = [0]

            def link(ins):
                n[0] += 1
                ins.then_inc(gch, 1)
                dve.wait_ge(gch, n[0])

            link(dve.tensor_copy(gw[3][:], ga[:, :, 16:32]))
            link(dve.tensor_tensor(gw[0][:], ga[:, :, 0:16], dt, ALU.add))
            link(dve.tensor_scalar(gw[1][:], gw[0][:], -1.0, None, ALU.mult))
            link(dve.tensor_tensor(gw[1][:], gw[1][:], gw[0][:], ALU.max))
            link(dve.tensor_scalar(gw[0][:], gw[0][:], 0.0, None, ALU.max))
            link(dve.tensor_scalar(gw[2][:], gw[3][:], -1.0, None, ALU.mult))
            link(dve.tensor_tensor(gw[3][:], gw[3][:], gw[2][:], ALU.max))
            link(dve.tensor_scalar(gw[2][:], gw[2][:], 0.0, -1.0, ALU.max, ALU.mult))
            dve.wait_ge(gact, 4)
            link(dve.tensor_scalar(gw[3][:], gw[3][:], 1.0, None, ALU.add))
            link(dve.tensor_scalar(gw[1][:], gw[1][:], 1.0, None, ALU.add))
            link(dve.reciprocal(gw[3][:], gw[3][:]))
            link(dve.tensor_tensor(core.beta[:], gw[2][:], gw[3][:], ALU.mult))
            link(dve.tensor_scalar(core.nbeta[:], core.beta[:], -1.0, None, ALU.mult))
            dve.wait_ge(gact, 5)
            link(dve.tensor_tensor(gw[0][:], gw[0][:], gw[1][:], ALU.add))
            link(dve.scalar_tensor_tensor(core.gtok[:], gw[0][:], -1.0,
                                          ab[:, 1, :].unsqueeze(1).broadcast_to([P, NT, 16]), ALU.mult, ALU.mult))

            with dve.Fori(0, H) as hh:
                NV = 8 + 3 * 10
                at = [0]

                def chain(ins):
                    at[0] += 1
                    ins.then_inc(vec, 1)
                    dve.wait_ge(vec, hh * NV + (2 + at[0]))

                def convolve(j):
                    s = j % 2
                    dve.wait_ge(evac, hh * 6 + (j + 3))
                    g, c = inner(s)
                    a = acc[s][:, 0:LAT].rearrange("p (r c) -> p r c", c=GW)
                    ac = acc[s][:, LAT:TOK]
                    tap = lambda t: cwh[:, j, t:t + 1]
                    if j:
                        dve.tensor_scalar(ac, c[:, 0:CTX], tap(3), None, ALU.mult)
                    chain(dve.tensor_scalar(a, g[:, 0:GR, 0:GW], tap(0), None, ALU.mult))
                    for t in range(1, 9):
                        last = dve.scalar_tensor_tensor(a, g[:, t // 3:t // 3 + GR, t % 3:t % 3 + GW], tap(t), a, ALU.mult, ALU.add)
                        if t < 8:
                            chain(last)
                        if j and t in (4, 5):
                            last = dve.scalar_tensor_tensor(ac, c[:, t - 3:t - 3 + CTX], tap(t), ac, ALU.mult, ALU.add)
                            chain(last)
                    return last

                def norm(j, x, tiles, scale):
                    nb = (tiles + 3) // 4
                    dve.wait_ge(sq_rdy, hh * 5 + (2 if j == 0 else 5))
                    dve.reduce_sum(ssq[:, j, 2, 0:tiles], sq[:, 0:tiles, :], AXX).then_inc(red, 1)
                    dve.wait_ge(red, hh * 4 + (2 * j + 1))
                    dve.tensor_scalar(ssq[:, j, 0, 0:tiles], ssq[:, j, 2, 0:tiles], EPS, 1.0 / scale ** 2, ALU.add, ALU.mult).then_inc(var, 1)
                    dve.wait_ge(std, hh * 2 + (j + 1))
                    dve.reciprocal(ssq[:, j, 2, 0:tiles], ssq[:, j, 1, 0:tiles]).then_inc(red, 1)
                    dve.wait_ge(red, hh * 4 + (2 * j + 2))
                    dve.wait_ge(tfree, hh * NB + (2 + T["qk"[j]] + nb))
                    dve.tensor_tensor(x[:], x[:], ssq[:, j, 2, 0:tiles].unsqueeze(2).broadcast_to([P, tiles, P]),
                                      ALU.mult).then_inc(nrm, 1)

                dve.wait_ge(taps, hh + 1)
                convolve(0).then_inc(conv, 1)
                convolve(1).then_inc(conv, 1)
                norm(0, qt, NL, DK ** -0.5)
                convolve(2).then_inc(conv, 1)
                norm(1, kt, NT, 1.0)
                convolve(3).then_inc(conv, 1)
                dve.wait_ge(conv, hh * 4 + 4)
                dve.sem_inc(taps_used, 1)
                assert at[0] == NV


class Steps:

    def __init__(self, names):
        self.names = names.split()
        self.n = len(self.names)

    def done(self, step, name):
        return step * self.n + (self.names.index(name) + 1)


LV = range(LEVELS)
PE_EV = Steps("gb gp kk0 kk1 kk2 kk3 x0 " + " ".join(f"x{l} d{l} t{l}" for l in LV[1:-1]) + " x6 t6 "
              + " ".join(f"{w}{p}" for w in ("ks", "vn", "o", "su") for p in range(4)))
ACT_EV = Steps("eg el tl dt " + " ".join(f"x{l}" for l in LV[1:]) + " vn0 vn1 vn2 vn3")
DVE_EV = Steps("gps td gm na0 na1 na2 na3 pt " + " ".join(f"tu{l} tt{l}" for l in LV[:-1]) + " tt6 "
               + " ".join(f"{w}{p}" for w in ("r", "oa", "su") for p in range(4)))
POOL_EV = Steps("gc ti gms db qg kg kta")


def delta_phase(core, io):
    nc, psum, ident = core.nc, core.psum, core.ident
    o = core.at("o", [P, NL, FW], 0)
    per = lambda n, shape, kb: [core.at(f"{n}_{d}", shape, 64 + 64 * d + kb) for d in range(2)]
    S = per("S", [P, H, DV], 0)
    kq = per("kq", [P, H, 2, P], 8)
    kk = per("kk", [P, H, P], 16)
    v = per("v", [P, H, DV], 20)
    T = per("T", [P, H, P], 28)
    TT = per("TT", [P, H, P], 32)
    X = per("X", [P, H, P], 36)
    nA = per("nA", [P, H, P], 40)
    DT = per("DT", [P, H, P], 44)
    EG = per("EG", [P, H, P], 48)
    QG = per("QG", [P, H, P], 52)
    vn = per("vn", [P, H, DV], 56)
    U = core.at("U", [P, 2, P], 192)
    NM = core.at("NM", [P, 2, P], 193)
    lm = core.at("lm", [P, LEVELS, 2, 64], 194, I32)
    small = lambda n, kb: [core.at(f"{n}_{d}", [P, H], kb + d / 32) for d in range(2)]
    gc, bc, nb = small("gc", 197.5), small("bc", 197.5 + 1 / 16), small("nb", 197.5 + 2 / 16)
    gps, td, tl, el = (small(n, 197.5 + (3 + j) / 16) for j, n in enumerate(("gps", "td", "tl", "el")))
    kT_v = core.kT_d.rearrange("h p (n t) -> n p h t", t=P)
    qT_v = core.qT_d.rearrange("h p (n t) -> n p h t", t=P)
    k_v = core.k_d.rearrange("(n p) (h c) -> n p h c", p=P, h=H)
    v_v = core.v_d.rearrange("(n p) (h c) -> n p h c", p=P, h=H)
    LAST = (P - 1, 0)
    DIR = (0, 1)

    def half(t, l, which):
        return t[:].rearrange("p h (n two s) -> p h n two s", two=2, s=1 << l)[:, :, :, which, :]

    def packed(bank, l):
        return bank.rearrange("p (h n s) -> p h n s", h=H, s=1 << l)

    def mask(l, which):
        m = lm[:, l, which, :].rearrange("p (n s) -> p n s", s=1 << l)
        return m.unsqueeze(1).broadcast_to([P, H, 64 >> l, 1 << l])

    with ExitStack() as st:
        sem = sems(nc, st)
        tab_in, nm_rdy, init_rdy = sem("tab_in5"), sem("nm_rdy"), sem("init_rdy")
        kT_in, qT_in, k_in, v_in = ([sem(f"{n}{d}") for d in DIR] for n in ("kT_in", "qT_in", "k_in", "v_in"))
        pe_done = [sem("pe_fwd"), sem("pe_bwd")]
        act_done = [sem("act_fwd"), sem("act_bwd")]
        dve_done = [sem("dve_fwd"), sem("dve_bwd")]
        pool_done = [sem("pool_fwd"), sem("pool_bwd")]
        merges = sem("merges")
        block = st.enter_context(nc.Block())

        def bank(d, b):
            return psum[:, (4 * d + b) * 512:(4 * d + b + 1) * 512]

        def head2(d, p):
            return bank(d, p).rearrange("p (a c) -> p a c", a=2)

        def all_steps(eng, body):
            for s in range(2):
                body(s, (NL + s, NL + 1 - s), False)
            down = eng.alloc_register("down")
            eng.reg_mov(down, NL - 1)
            with eng.Fori(0, NL) as i:
                body(i + 2, (i, eng.snap(down, min_val=0, max_val=NL - 1)), True)
                eng.reg_sub(down, down, 1)

        @block.sync
        def _(sp):
            sp.dma_start(U[:], io["tri"]).then_inc(tab_in, 16)
            sp.dma_start(lm[:], io["level_mask"]).then_inc(tab_in, 16)

            def load(step, chunk, lat):
                for d in DIR:
                    first = isinstance(step, int) and step == 0
                    if not first:
                        sp.wait_ge(pe_done[d], PE_EV.done(step - 1, "kk3"))
                        sp.wait_ge(pool_done[d], POOL_EV.done(step - 1, "kg"))
                    sp.dma_start(kq[d][:, :, 0, :], kT_v[chunk[d]]).then_inc(kT_in[d], 16)
                    if lat:
                        sp.dma_start(kq[d][:, :, 1, :], qT_v[chunk[d]]).then_inc(qT_in[d], 16)
                for d in DIR:
                    if not first:
                        sp.wait_ge(pe_done[d], PE_EV.done(step - 1, "vn3"))
                    sp.dma_start(v[d][:], v_v[chunk[d]]).then_inc(v_in[d], 16)
                for d in DIR:
                    if not first:
                        sp.wait_ge(pe_done[d], PE_EV.done(step - 1, "su3"))
                    sp.dma_start(kk[d][:], k_v[chunk[d]]).then_inc(k_in[d], 16)

            all_steps(sp, load)

        @block.tensor
        def _(pe):
            pe.wait_ge(tab_in, 32)

            def body(step, chunk, lat):
                first = isinstance(step, int) and step == 0
                for d in DIR:
                    pe.wait_ge(pool_done[d], POOL_EV.done(step, "gc"))
                    if not first:
                        pe.wait_ge(dve_done[d], DVE_EV.done(step - 1, "su3"))
                    for h in range(H):
                        last = pe.matmul(bank(d, h // 4)[:, (h % 4) * P:(h % 4 + 1) * P],
                                         gc[d][:, h:h + 1].broadcast_to([P, P]), U[:, d, :], start=True, stop=True)
                    last.then_inc(pe_done[d], 1)
                    pe.matmul(bank(d, 2)[:, 0:H], U[:, d, :], gc[d][:], start=True, stop=True).then_inc(pe_done[d], 1)
                for d in DIR:
                    pe.wait_ge(kT_in[d], step * 16 + 16)
                    if lat:
                        pe.wait_ge(qT_in[d], step * 16 - 16)
                    pe.wait_ge(dve_done[d], DVE_EV.done(step, "gm"))
                    pe.wait_ge(act_done[d], ACT_EV.done(step, "el"))
                    for p in range(4):
                        for h in (2 * p, 2 * p + 1):
                            out = head2(d, p)[:, h % 2, :]
                            if lat:
                                last = pe.matmul(out, kq[d][:, h, 0, :], kq[d][:, h, :, :].rearrange("p a c -> p (a c)"), start=True, stop=True)
                            else:
                                last = pe.matmul(out[:, 0:P], kq[d][:, h, 0, :], kq[d][:, h, 0, :], start=True, stop=True)
                        last.then_inc(pe_done[d], 1)
                for l in LV:
                    for d in DIR:
                        xc = d
                        if l == 0:
                            pe.wait_ge(dve_done[d], DVE_EV.done(step, "pt"))
                            pe.wait_ge(pool_done[d], POOL_EV.done(step, "ti"))
                        else:
                            pe.wait_ge(dve_done[d], DVE_EV.done(step, f"tt{l - 1}"))
                        for h in range(H):
                            last = pe.matmul(packed(bank(d, 0), l)[:, h], nA[d][:, h, :], half(T[d], l, xc)[:, h],
                                             start=True, stop=True)
                        last.then_inc(pe_done[d], 1)
                    if l == 0:
                        continue
                    for d in DIR:
                        xc = d
                        pe.wait_ge(act_done[d], ACT_EV.done(step, f"x{l}"))
                        if l < LEVELS - 1:
                            for h in range(H):
                                last = pe.matmul(packed(bank(d, 1), l)[:, h], TT[d][:, h, :], half(X[d], l, xc)[:, h],
                                                 start=True, stop=True)
                            last.then_inc(pe_done[d], 1)
                        for h in range(H):
                            last = pe.matmul(packed(bank(d, 2), l)[:, h], X[d][:, h, :], half(TT[d], l, 1 - xc)[:, h],
                                             start=True, stop=True)
                        last.then_inc(pe_done[d], 1)
                for d in DIR:
                    pe.wait_ge(pool_done[d], POOL_EV.done(step, "kg"))
                    pe.wait_ge(dve_done[d], DVE_EV.done(step, "tt6"))
                    if first:
                        pe.wait_ge(init_rdy, 1)
                    for p in range(4):
                        for h in (2 * p, 2 * p + 1):
                            last = pe.matmul(head2(d, p)[:, h % 2, :], EG[d][:, h, :], S[d][:, h, :], start=True, stop=True)
                        last.then_inc(pe_done[d], 1)
                for d in DIR:
                    for p in range(4):
                        pe.wait_ge(dve_done[d], DVE_EV.done(step, f"r{p}"))
                        for h in (2 * p, 2 * p + 1):
                            last = pe.matmul(head2(d, p)[:, h % 2, :], TT[d][:, h, :], v[d][:, h, :], start=True, stop=True)
                        last.then_inc(pe_done[d], 1)
                for d in DIR:
                    if lat:
                        pe.wait_ge(pool_done[d], POOL_EV.done(step, "qg"))
                        for p in range(4):
                            pe.wait_ge(act_done[d], ACT_EV.done(step, f"vn{p}"))
                            for h in (2 * p, 2 * p + 1):
                                out = head2(d, p)[:, h % 2, :]
                                pe.matmul(out, QG[d][:, h, :], S[d][:, h, :], start=True, stop=False)
                                last = pe.matmul(out, DT[d][:, h, :], vn[d][:, h, :], start=False, stop=True)
                            last.then_inc(pe_done[d], 1)
                    else:
                        pe.wait_ge(pe_done[d], PE_EV.done(step, "vn3"))
                        pe.sem_inc(pe_done[d], 4)
                for d in DIR:
                    pe.wait_ge(pool_done[d], POOL_EV.done(step, "kta"))
                    for p in range(4):
                        if lat:
                            pe.wait_ge(dve_done[d], DVE_EV.done(step, f"oa{p}"))
                        else:
                            pe.wait_ge(act_done[d], ACT_EV.done(step, f"vn{p}"))
                        for h in (2 * p, 2 * p + 1):
                            last = pe.matmul(head2(d, p)[:, h % 2, :], kk[d][:, h, :], vn[d][:, h, :], start=True, stop=True)
                        last.then_inc(pe_done[d], 1)

            all_steps(pe, body)

        @block.scalar
        def _(act):
            def body(step, chunk, lat):
                for d in DIR:
                    gb = psum[:, 2048 * d:2048 * d + 1024].rearrange("p (h c) -> p h c", h=H)
                    act.wait_ge(dve_done[d], DVE_EV.done(step, "gm"))
                    act.activation(EG[d][:], gb, ACT.Exp).then_inc(act_done[d], 1)
                    act.activation(el[d][:].unsqueeze(2), gb[:, :, LAST[d]:LAST[d] + 1], ACT.Exp).then_inc(act_done[d], 1)
                    act.activation(tl[d][:], td[d][:], ACT.Exp).then_inc(act_done[d], 1)
                for d in DIR:
                    act.wait_ge(pool_done[d], POOL_EV.done(step, "gms"))
                    act.activation(DT[d][:], nA[d][:], ACT.Exp).then_inc(act_done[d], 1)
                for l in LV[1:]:
                    for d in DIR:
                        act.wait_ge(pe_done[d], PE_EV.done(step, f"x{l}"))
                        act.activation(half(X[d], l, d), packed(bank(d, 0), l), ACT.Copy).then_inc(act_done[d], 1)
                for d in DIR:
                    for p in range(4):
                        act.wait_ge(pe_done[d], PE_EV.done(step, f"vn{p}"))
                        for h in (2 * p, 2 * p + 1):
                            last = act.activation(vn[d][:, h, :], head2(d, p)[:, h % 2, :], ACT.Copy, scale=bc[d][:, h:h + 1])
                        last.then_inc(act_done[d], 1)

            act.wait_ge(init_rdy, 1)
            all_steps(act, body)

        @block.vector
        def _(dve):
            for d in DIR:
                dve.memset(X[d][:], 0.0)
                dve.memset(S[d][:], 0.0)
            dve.memset(o[:], 0.0).then_inc(init_rdy, 1)
            dve.wait_ge(init_rdy, 1)
            dve.wait_ge(nm_rdy, 1)

            def body(step, chunk, lat):
                for d in DIR:
                    sig = dve_done[d]
                    gb = psum[:, 2048 * d:2048 * d + 1024].rearrange("p (h c) -> p h c", h=H)
                    dve.wait_ge(pe_done[d], PE_EV.done(step, "gp"))
                    dve.tensor_copy(gps[d][:], bank(d, 2)[:, 0:H]).then_inc(sig, 1)
                    dve.wait_ge(sig, DVE_EV.done(step, "gps"))
                    dve.tensor_tensor(td[d][:], gb[:, :, LAST[d]], gps[d][:], ALU.subtract).then_inc(sig, 1)
                    dve.tensor_tensor(nA[d][:], gb, NM[:, d, :].unsqueeze(1).broadcast_to([P, H, P]), ALU.add).then_inc(sig, 1)
                for d in DIR:
                    sig = dve_done[d]
                    dve.wait_ge(pool_done[d], POOL_EV.done(step, "db"))
                    for p in range(4):
                        dve.wait_ge(pe_done[d], PE_EV.done(step, f"kk{p}"))
                        hs = slice(2 * p, 2 * p + 2)
                        dve.tensor_tensor(nA[d][:, hs, :], head2(d, p)[:, :, 0:P], nA[d][:, hs, :], ALU.mult).then_inc(sig, 1)
                        if lat:
                            last = dve.tensor_tensor(DT[d][:, hs, :], head2(d, p)[:, :, P:2 * P], DT[d][:, hs, :], ALU.mult)
                    if lat:
                        last.then_inc(sig, 1)
                    else:
                        dve.wait_ge(sig, DVE_EV.done(step, "na3"))
                        dve.sem_inc(sig, 1)
                for l in LV:
                    for d in DIR:
                        sig = dve_done[d]
                        xc, tc = d, 1 - d
                        if l == 0:
                            dve.wait_ge(pe_done[d], PE_EV.done(step, "x0"))
                            dve.sem_inc(merges, 1)
                            dve.copy_predicated(half(T[d], 0, xc), mask(0, 1 - d), packed(bank(d, 0), 0)).then_inc(sig, 1)
                            dve.wait_ge(sig, DVE_EV.done(step, "pt"))
                            dve.sem_inc(merges, 1)
                            dve.copy_predicated(half(TT[d], 0, tc), mask(0, d), half(nA[d], 0, tc)).then_inc(sig, 1)
                            continue
                        if l < LEVELS - 1:
                            dve.wait_ge(pe_done[d], PE_EV.done(step, f"d{l}"))
                            dve.sem_inc(merges, 1)
                            dve.copy_predicated(half(T[d], l, xc), mask(l, 1 - d), packed(bank(d, 1), l)).then_inc(sig, 1)
                        dve.wait_ge(pe_done[d], PE_EV.done(step, f"t{l}"))
                        dve.sem_inc(merges, 1)
                        dve.copy_predicated(half(TT[d], l, tc), mask(l, d), packed(bank(d, 2), l)).then_inc(sig, 1)
                for d in DIR:
                    dve.wait_ge(v_in[d], step * 16 + 16)
                    for p in range(4):
                        hs = slice(2 * p, 2 * p + 2)
                        dve.wait_ge(pe_done[d], PE_EV.done(step, f"ks{p}"))
                        dve.tensor_tensor(v[d][:, hs, :], v[d][:, hs, :], head2(d, p), ALU.subtract).then_inc(dve_done[d], 1)
                for d in DIR:
                    if lat:
                        for p in range(4):
                            dve.wait_ge(pe_done[d], PE_EV.done(step, f"o{p}"))
                            oc = o[:, bass.ds(chunk[d], 1), 512 * p:512 * p + 512].rearrange("p a c -> p (a c)")
                            dve.tensor_tensor(oc, oc, bank(d, p), ALU.add).then_inc(dve_done[d], 1)
                    else:
                        dve.wait_ge(dve_done[d], DVE_EV.done(step, "r3"))
                        dve.sem_inc(dve_done[d], 4)
                for d in DIR:
                    dve.wait_ge(act_done[d], ACT_EV.done(step, "el"))
                    for p in range(4):
                        dve.wait_ge(pe_done[d], PE_EV.done(step, f"su{p}"))
                        for h in (2 * p, 2 * p + 1):
                            last = dve.scalar_tensor_tensor(S[d][:, h, :], S[d][:, h, :], el[d][:, h:h + 1],
                                                            head2(d, p)[:, h % 2, :], ALU.mult, ALU.add)
                        last.then_inc(dve_done[d], 1)

            all_steps(dve, body)

        @block.gpsimd
        def _(pool):
            pool.wait_ge(tab_in, 32)
            pool.tensor_scalar(NM[:], U[:], -1.0, -BIG, ALU.add, ALU.mult).then_inc(nm_rdy, 1)

            def body(step, chunk, lat):
                first = isinstance(step, int) and step == 0
                for d in DIR:
                    if not first:
                        pool.wait_ge(pe_done[d], PE_EV.done(step - 1, "su3"))
                    hs = slice(8 * d, 8 * d + 8)
                    for dst, src in ((gc, core.gtok), (bc, core.beta), (nb, core.nbeta)):
                        last = pool.tensor_copy(dst[d][:], src[:, bass.ds(chunk[d], 1), hs].rearrange("p a h -> p (a h)"))
                    last.then_inc(pool_done[d], 1)
                    for t in (T, TT):
                        last = pool.tensor_copy(t[d][:], ident[:].unsqueeze(1).broadcast_to([P, H, P]))
                    last.then_inc(pool_done[d], 1)
                for d in DIR:
                    b3 = lambda a: a[:].unsqueeze(2).broadcast_to([P, H, P])
                    pool.wait_ge(dve_done[d], DVE_EV.done(step, "gm"))
                    pool.tensor_tensor(nA[d][:], nA[d][:], b3(gps[d]), ALU.subtract).then_inc(pool_done[d], 1)
                    pool.wait_ge(act_done[d], ACT_EV.done(step, "dt"))
                    pool.tensor_tensor(nA[d][:], DT[d][:], b3(nb[d]), ALU.mult).then_inc(pool_done[d], 1)
                for d in DIR:
                    b3 = lambda a: a[:].unsqueeze(2).broadcast_to([P, H, P])
                    pool.wait_ge(kT_in[d], step * 16 + 16)
                    if lat:
                        pool.wait_ge(qT_in[d], step * 16 - 16)
                        pool.tensor_tensor(QG[d][:], kq[d][:, :, 1, :], EG[d][:], ALU.mult).then_inc(pool_done[d], 1)
                        pool.wait_ge(pool_done[d], POOL_EV.done(step, "qg"))
                    else:
                        pool.wait_ge(pool_done[d], POOL_EV.done(step, "db"))
                        pool.sem_inc(pool_done[d], 1)
                    pool.tensor_tensor(EG[d][:], kq[d][:, :, 0, :], EG[d][:], ALU.mult).then_inc(pool_done[d], 1)
                    pool.wait_ge(k_in[d], step * 16 + 16)
                    pool.tensor_tensor(kk[d][:], kk[d][:], b3(tl[d]), ALU.mult).then_inc(pool_done[d], 1)

            all_steps(pool, body)


def gate_phase(core, io):
    nc, psum, ident = core.nc, core.psum, core.ident
    o = core.at("o", [P, NL, FW], 0)
    zt = [core.at(f"zt{s}", [P, LAT], 64 + 4 * s) for s in range(2)]
    y = [core.at(f"y_g{s}", [P, LAT], 72 + 4 * s) for s in range(2)]
    sq = core.at("sq_g", [P, NL, FW], 80)
    st_ = core.at("st_g", [P, 3, NL * H], 144)
    cols = core.cols
    z_v = core.z_d.rearrange("(n p) t -> n p t", p=P)
    y_v = core.y2_d.rearrange("(n p) t -> n p t", p=P)
    with ExitStack() as st:
        sem = sems(nc, st)
        z_in = [sem("zt_in0"), sem("zt_in1")]
        stored = [sem("yg_stored0"), sem("yg_stored1")]
        sq_rdy, red, std, rstd, on = sem("sqg_rdy"), sem("red_g"), sem("std_g"), sem("rstd_g"), sem("on_rdy")
        t_mm, y_rdy = sem("tg_mm"), sem("yg_rdy")
        block = st.enter_context(nc.Block())
        NCT = 16

        @block.sync
        def _(sp):
            for s in range(2):
                sp.dma_start(zt[s][:], z_v[s]).then_inc(z_in[s], 16)
                sp.sem_inc(stored[s], 16)

            def turn(n, s, more):
                sp.wait_ge(y_rdy, n + 3)
                sp.dma_start(y_v[n], y[s][:]).then_inc(stored[s], 16)
                if more:
                    sp.dma_start(zt[s][:], z_v[n + 2]).then_inc(z_in[s], 16)

            with sp.Fori(0, NCT // 2 - 1) as i:
                for s in range(2):
                    turn(i * 2 + s, s, True)
            for s in range(2):
                turn(NCT - 2 + s, s, False)
            for s in range(2):
                sp.wait_ge(stored[s], 16 + 16 * NCT // 2)

        @block.scalar
        def _(act):
            for n in range(NL):
                act.activation(sq[:, n, :], o[:, n, :], ACT.Square).then_inc(sq_rdy, 1)
            act.wait_ge(red, 2)
            act.activation(st_[:, 1, :], st_[:, 0, :], ACT.Sqrt).then_inc(std, 1)

        @block.vector
        def _(dve):
            dve.sem_inc(y_rdy, 2)
            for n in range(NL):
                dve.wait_ge(sq_rdy, n + 1)
                last = dve.reduce_sum(st_[:, 2, n * H:(n + 1) * H], sq[:, n, :].rearrange("p (h c) -> p h c", h=H), AXX)
            last.then_inc(red, 1)
            dve.wait_ge(red, 1)
            dve.tensor_scalar(st_[:, 0, :], st_[:, 2, :], 1.0 / DV, EPS, ALU.mult, ALU.add).then_inc(red, 1)
            dve.wait_ge(std, 1)
            dve.reciprocal(st_[:, 2, :], st_[:, 1, :]).then_inc(rstd, 1)
            dve.wait_ge(rstd, 1)
            for n in range(NL):
                on_ = o[:, n, :].rearrange("p (h c) -> p h c", h=H)
                r = st_[:, 2, n * H:(n + 1) * H].unsqueeze(2).broadcast_to([P, H, DV])
                dve.tensor_tensor(on_, on_, r, ALU.mult).then_inc(on, 1)
            with dve.Fori(0, NCT // 2) as i:
                for s in range(2):
                    n = i * 2 + s
                    dve.wait_ge(t_mm, n + 1)
                    dve.wait_ge(z_in[s], i * 16 + 16)
                    dve.wait_ge(stored[s], i * 16 + 16)
                    dve.scalar_tensor_tensor(y[s][:], psum[:, 1024 * s:1024 * s + 1024], cols[:, COL_DN + s:COL_DN + s + 1],
                                             zt[s][:], ALU.mult, ALU.mult).then_inc(y_rdy, 1)

        @block.tensor
        def _(pe):
            pe.wait_ge(on, NL)
            for n in range(NCT):
                pe.wait_ge(y_rdy, n + 1)
                for t in range(NL):
                    o_ = 1024 * (n % 2) + t * P
                    last = pe.transpose(psum[:, o_:o_ + P], o[:, t, n * P:(n + 1) * P], ident[:])
                last.then_inc(t_mm, 1)


def tables():
    t = {}
    k = np.arange(HL)
    f = lambda L: 2 * np.pi / L * np.outer(np.arange(L // 2), np.arange(L // 2))
    lat = [m.reshape(4, P, HL).transpose(1, 0, 2).reshape(P, -1) for m in (np.cos(f(LAT)), np.sin(f(LAT)))]
    t["dft_tab"] = np.concatenate([m / LAT ** 0.5 for m in lat] + [np.cos(f(CTX)) / CTX ** 0.5, np.sin(f(CTX)) / CTX ** 0.5], 1)
    alt = 1.0 - 2.0 * (np.arange(P) % 2)
    t["alt_col"] = np.stack([alt / LAT ** 0.5, alt / CTX ** 0.5], 1)
    t["alt_row"] = np.concatenate([np.tile(alt, 4) / LAT ** 0.5, alt / CTX ** 0.5])[None]
    a = 2 * np.pi / FD * np.outer(np.arange(FD), np.arange(FD))
    t["ch_dft"] = np.stack([m.reshape(2, P, FD).transpose(1, 0, 2) for m in (np.cos(a) / FD ** 0.5, np.sin(a) / FD ** 0.5)], 1)
    t["ident"] = np.eye(P)
    i = np.arange(P)
    t["tri"] = np.stack([i[:, None] <= i[None], i[:, None] >= i[None]], 1)
    t = {n: np.ascontiguousarray(v, np.float32) for n, v in t.items()}
    lm = np.zeros((P, LEVELS, 2, 64), np.int32)
    for l in range(LEVELS):
        s = 1 << l
        c = np.arange(64)
        for half in range(2):
            lm[:, l, half] = (i[:, None] // (2 * s) == c[None] // s) & ((i[:, None] % (2 * s)) // s == half)
    t["level_mask"] = lm
    return t


def program(nc, io):
    core = Core(nc)
    input_phase(core, io)
    fourier_phase(core, io)
    output_phase(core, io, 0)
    project_phase(core, io)
    delta_phase(core, io)
    gate_phase(core, io)
    output_phase(core, io, 1)


INPUTS = ("x", "c", "ctx", "c_ctx", "mod_w", "mod_b", "norm_g", "final_g", "fn_w_in", "fn_w_grp", "fn_w_out",
          "dn_w_in", "dn_conv", "dn_a_log", "dn_dt_bias", "dn_norm_g", "dn_w_out")


def kernel(**inputs):
    import concourse.bacc as _bacc
    from concourse.bass_utils import run_bass_kernel_spmd as _run

    nc = _bacc.Bacc("TRN2", target_bir_lowering=False, num_devices=1)
    arrays = {n: np.ascontiguousarray(inputs[n]) for n in INPUTS}
    x, ctx = arrays["x"][0], arrays["ctx"][0]
    arrays["x_mirror"] = np.ascontiguousarray(np.concatenate([x[HL:HL + 1], x[:HL:-1]]))
    arrays["ctx_mirror"] = np.ascontiguousarray(np.concatenate([ctx[HC:HC + 1], ctx[:HC:-1]]))
    arrays.update(tables())
    io = {n: nc.dram_tensor(f"in_{n}", a.shape, mybir.dt.from_np(a.dtype), kind="ExternalInput").ap() for n, a in arrays.items()}
    io["out"] = nc.dram_tensor("out", (1, LAT, D), F32, kind="ExternalOutput").ap()
    program(nc, io)
    r = _run(nc, [{f"in_{n}": a for n, a in arrays.items()}], core_ids=[0])
    return r.results[0]["out"]
```

```python
from contextlib import ExitStack

import numpy as np
import concourse.bass as bass
from concourse import mybir

F32 = mybir.dt.float32
I32 = mybir.dt.int32
ACT = mybir.ActivationFunctionType
ALU = mybir.AluOpType
AXX = mybir.AxisListType.X

P = 128
D = 1024
KT = D // P
LAT, CTX = 1024, 256
TOK = LAT + CTX
NL, NC_ = LAT // P, CTX // P
NT = NL + NC_
HL, HC = LAT // 2, CTX // 2
GW = 64
GR = LAT // GW
EPS = 1e-6
FG, FD = 8, 256
FW = FG * FD
H, DK, DV = 8, 128, 256
BIG = -1.0e30
KB = 1024


def bcast(ap, shape):
    return ap.broadcast_to(shape)


class Core:

    def __init__(self, nc):
        self.nc = nc
        self.placed = {}
        sb = nc.alloc_sbuf_tensor
        self.ident = sb("ident", [P, P], F32)
        self.cols = sb("cols", [P, 82], F32)
        self.modT = sb("modT", [P, 48, 2], F32)
        self.acoef = sb("acoef", [P, 2, KT, 2], F32)
        self.gtok = sb("gtok", [P, NT, 16], F32)
        self.beta = sb("beta", [P, NT, 16], F32)
        self.nbeta = sb("nbeta", [P, NT, 16], F32)
        self.epst = sb("epst", [P, 1], F32)
        self.base = (nc.sbuf_base + 63) // 64 * 64
        self.psum = nc.alloc_psum_tensor("psum", [P, 8 * 512], F32)
        dr = lambda n, s: nc.dram_tensor(n, s, F32, kind="Internal").ap()
        self.y_d = dr("y_scr", (FW, TOK))
        self.y2_d = dr("y2_scr", (FW, LAT))
        self.h_d = dr("h_scr", (LAT, D))
        self.z_d = dr("z_scr", (FW, LAT))
        self.qT_d = dr("qT_scr", (H, P, LAT))
        self.kT_d = dr("kT_scr", (H, P, TOK))
        self.k_d = dr("k_scr", (TOK, D))
        self.v_d = dr("v_scr", (TOK, FW))

    def at(self, name, shape, kb, dt=F32):
        if name not in self.placed:
            self.placed[name] = self.nc.alloc_sbuf_tensor_at(name, shape, dt, offset=self.base + int(kb * KB))
        return self.placed[name]


def sems(nc, stack):
    return lambda name: stack.enter_context(nc.semaphore(name))


COL_MODB, COL_G, COL_C, COL_CC, COL_DN = 0, 48, 64, 72, 80


def input_phase(core, io):
    nc = core.nc
    pqT = core.at("pqT", [P, KT, TOK], 0)
    nT = core.at("nT", [P, KT, TOK], 40)
    xn = core.at("xn", [P, NT, D], 80)
    xm = core.at("xm", [P, 5, D], 120)
    ev = core.at("ev", [P, 5, D], 140)
    mw = [core.at(f"mw{s}", [P, KT, 256], 160 + 8 * s) for s in range(2)]
    dft = core.at("dft", [P, 2 * 4 * HL + 2 * HC], 176)
    b0 = core.at("b0", [64, D], 193)
    junk = core.at("junk", [P, D], 0)
    rows = core.at("rows", [82, P], 40)
    scond = core.at("scond", [P, KT, 2], 199)
    ss = core.at("ss", [P, 16], 199.25)
    altc = core.at("altc", [P, 2], 199.5)
    shs = core.at("shs", [P, KT, 2], 199.75)
    altr = core.at("altr", [64, HL], 197)
    cosL = dft[:, 0:4 * HL].rearrange("p (t k) -> p t k", t=4)
    sinL = dft[:, 4 * HL:8 * HL].rearrange("p (t k) -> p t k", t=4)
    cosC = dft[:, 8 * HL:8 * HL + HC]
    sinC = dft[:, 8 * HL + HC:8 * HL + 2 * HC]
    psum, cols, modT = core.psum, core.cols, core.modT
    NCH = 12
    with ExitStack() as st:
        sem = sems(nc, st)
        x_in = [sem(f"x_in{n}") for n in range(5)]
        rows_in, tab_in, id_in = sem("rows_in"), sem("tab_in"), sem("id_in")
        mw_in = [sem("mw_in0"), sem("mw_in1")]
        mw_used = sem("mw_used")
        rowsT, cols_rdy, cond_rdy = sem("rowsT"), sem("cols_rdy"), sem("cond_rdy")
        ss_rdy, var_rdy, std_rdy, eps_rdy = sem("ss_rdy"), sem("var_rdy"), sem("std_rdy"), sem("eps_rdy")
        vec = sem("vec_chain")
        xhat_rdy, fold_rdy, odd_rdy, mod_free = sem("xhat_rdy"), sem("fold_rdy"), sem("odd_rdy"), sem("mod_free")
        coef_rdy = sem("coef_rdy")
        dft_mm, dft_free_a, dft_free_v = sem("dft_mm"), sem("dft_free_a"), sem("dft_free_v")
        tr_mm, tr_free = sem("tr_mm"), sem("tr_free")
        block = st.enter_context(nc.Block())

        @block.sync
        def _(sp):
            sp.dma_start(core.ident[:], io["ident"]).then_inc(id_in, 16)
            r = lambda a: a.rearrange("(n p) -> n p", p=P)
            for lo, src in ((COL_MODB, io["mod_b"].rearrange("l (n p) -> (l n) p", p=P)),
                            (COL_G, io["norm_g"].rearrange("l (n p) -> (l n) p", p=P)),
                            (COL_C, io["c"].rearrange("l (n p) -> (l n) p", p=P)),
                            (COL_CC, r(io["c_ctx"])),
                            (COL_DN, io["dn_norm_g"].rearrange("l (n p) -> (l n) p", p=P))):
                sp.dma_start(rows[lo:lo + src.shape[0], :], src).then_inc(rows_in, 16)
            xv = io["x"][0].rearrange("(n p) d -> p n d", p=P)
            sp.dma_start(xn[:, 0:4, :], xv[:, 0:4, :]).then_inc(x_in[0], 16)
            sp.dma_start(xn[:, 4:8, :], xv[:, 4:8, :]).then_inc(x_in[1], 16)
            sp.dma_start(xn[:, 8:10, :], io["ctx"][0].rearrange("(n p) d -> p n d", p=P)).then_inc(x_in[2], 16)
            sp.dma_start(xm[:, 0:4, :], io["x_mirror"].rearrange("(n p) d -> p n d", p=P)).then_inc(x_in[3], 16)
            sp.dma_start(xm[:, 4, :], io["ctx_mirror"]).then_inc(x_in[4], 16)
            mv = [io["mod_w"][l].rearrange("(k p) (n c) -> n p k c", p=P, c=256) for l in range(2)]
            for s in range(2):
                sp.dma_start(mw[s][:], mv[0][s]).then_inc(mw_in[s], 16)
            sp.dma_start(dft[:], io["dft_tab"]).then_inc(tab_in, 16)
            sp.dma_start(altc[:], io["alt_col"]).then_inc(tab_in, 16)
            sp.dma_start(altr[0:1, :], io["alt_row"][:, 0:HL]).then_inc(tab_in, 16)
            sp.dma_start(altr[32:33, 0:HC], io["alt_row"][:, HL:HL + HC]).then_inc(tab_in, 16)
            with sp.Fori(0, NCH // 2 - 1) as i:
                for s in range(2):
                    sp.wait_ge(mw_used, i * 2 + (s + 1))
                    sp.dma_start(mw[s][:], mv[0][i * 2 + (s + 2)]).then_inc(mw_in[s], 16)
            with sp.Fori(0, NCH // 2) as i:
                for s in range(2):
                    sp.wait_ge(mw_used, i * 2 + (s + NCH - 1))
                    sp.dma_start(mw[s][:], mv[1][i * 2 + s]).then_inc(mw_in[s], 16)

        @block.scalar
        def _(act):
            for n in range(15):
                src = xn[:, n, :] if n < NT else xm[:, n - NT, :]
                act.wait_ge(x_in[0 if n < 4 else 1 if n < 8 else 2 if n < 10 else 3 if n < 14 else 4], 16)
                if n:
                    act.wait_ge(ss_rdy, n)
                act.activation(junk[:], src, ACT.Square, accum_out=ss[:, n:n + 1]).then_inc(ss_rdy, 1)
            act.wait_ge(var_rdy, 1)
            act.activation(ss[:, 0:15], ss[:, 0:15], ACT.Sqrt).then_inc(std_rdy, 1)
            act.wait_ge(cols_rdy, 1)
            for c in range(2):
                act.activation(scond[:, :, c], cols[:, COL_C + 8 * c:COL_C + 8 * c + 8], ACT.Silu).then_inc(cond_rdy, 1)
            act.wait_ge(coef_rdy, 3)
            for k in range(KT):
                b = 3 * (k % 2) * 512
                act.wait_ge(dft_mm, 2 * k + 1)
                a = core.acoef[:, 0, k, 0:1]
                act.activation(pqT[:, k, 1:HL], psum[:, b + 1:b + HL], ACT.Identity, scale=a)
                act.activation(pqT[:, k, 0:1], psum[:, b:b + 1], ACT.Identity,
                               scale=a, bias=shs[:, k, 0:1]).then_inc(dft_free_a, 1)
                for j, (t0, nt) in enumerate(((0, 4), (4, 4), (8, 2))):
                    g = 3 * k + j
                    bb = (6 + g % 2) * 512
                    c = int(j == 2)
                    act.wait_ge(tr_mm, g + 1)
                    act.activation(nT[:, k, t0 * P:(t0 + nt) * P], psum[:, bb:bb + nt * P], ACT.Identity,
                                   scale=core.acoef[:, 0, k, c:c + 1], bias=modT[:, k, c:c + 1]).then_inc(tr_free, 1)

        @block.vector
        def _(dve):
            chain = [0]

            def link(ins):
                chain[0] += 1
                ins.then_inc(vec, 1)
                dve.wait_ge(vec, chain[0])

            dve.memset(core.epst[:], EPS).then_inc(eps_rdy, 1)
            dve.sem_inc(mod_free, 2)
            dve.wait_ge(rowsT, 1)
            dve.tensor_copy(cols[:], psum[:, 0:82]).then_inc(cols_rdy, 1)
            dve.wait_ge(ss_rdy, 15)
            dve.tensor_scalar(ss[:, 0:15], ss[:, 0:15], 1.0 / D, EPS, ALU.mult, ALU.add).then_inc(var_rdy, 1)
            dve.wait_ge(std_rdy, 1)
            link(dve.reciprocal(ss[:, 0:15], ss[:, 0:15]))
            for n in range(15):
                x = xn[:, n, :] if n < NT else xm[:, n - NT, :]
                dve.tensor_scalar(x, x, ss[:, n:n + 1], None, ALU.mult).then_inc(xhat_rdy, 1)
            dve.wait_ge(xhat_rdy, 15)
            link(dve.tensor_tensor(ev[:, 0:4, :], xn[:, 0:4, :], xm[:, 0:4, :], ALU.add))
            link(dve.tensor_tensor(ev[:, 4, :], xn[:, 8, :], xm[:, 4, :], ALU.add))
            dve.tensor_copy(ev[0:1, 0, :], xn[0:1, 0, :])
            dve.tensor_copy(ev[0:1, 4, :], xn[0:1, 8, :])
            dve.tensor_copy(b0[0:1, :], xm[0:1, 0, :])
            dve.tensor_copy(b0[32:33, :], xm[0:1, 4, :]).then_inc(fold_rdy, 1)

            def mod_chunks(layer):
                with dve.Fori(0, NCH // 2) as i:
                    for s in range(2):
                        dve.wait_ge(mw_used, i * 2 + (layer * NCH + s + 1))
                        blk = i * 4 + (layer * 24 + 2 * s)
                        dve.tensor_tensor(modT[:, bass.ds(blk, 2), :],
                                          psum[:, 3072 + 512 * s:3072 + 512 * s + 4].rearrange("p (a b) -> p a b", a=2),
                                          cols[:, bass.ds(blk, 2)].unsqueeze(2).broadcast_to([P, 2, 2]),
                                          ALU.add).then_inc(mod_free, 1)

            def coefs(layer):
                dve.wait_ge(mod_free, 2 + NCH * (layer + 1))
                g = cols[:, COL_G + 8 * layer:COL_G + 8 * layer + 8].unsqueeze(2).broadcast_to([P, KT, 2])
                link(dve.tensor_scalar(core.acoef[:, layer], modT[:, 24 * layer + 8:24 * layer + 16, :], 1.0, None, ALU.add))
                dve.tensor_tensor(core.acoef[:, layer], core.acoef[:, layer], g, ALU.mult).then_inc(coef_rdy, 1)

            dve.wait_ge(cols_rdy, 1)
            mod_chunks(0)
            coefs(0)
            dve.tensor_scalar(shs[:, :, 0], modT[:, 0:8, 0], float(LAT) ** 0.5, None, ALU.mult).then_inc(coef_rdy, 1)
            dve.tensor_scalar(shs[:, :, 1], modT[:, 0:8, 1], float(CTX) ** 0.5, None, ALU.mult).then_inc(coef_rdy, 1)
            dve.wait_ge(coef_rdy, 3)
            for k in range(KT):
                b = 3 * (k % 2) * 512
                dve.wait_ge(dft_mm, 2 * k + 2)
                dve.tensor_scalar(pqT[:, k, HL:2 * HL], psum[:, b + 512:b + 1024],
                                  core.acoef[:, 0, k, 0:1], None, ALU.mult)
                dve.tensor_scalar(pqT[:, k, LAT + 1:TOK], psum[:, b + 1025:b + 1024 + 2 * HC],
                                  core.acoef[:, 0, k, 1:2], None, ALU.mult)
                dve.tensor_scalar(pqT[:, k, LAT:LAT + 1], psum[:, b + 1024:b + 1025],
                                  core.acoef[:, 0, k, 1:2], shs[:, k, 1:2], ALU.mult, ALU.add).then_inc(dft_free_v, 1)
            mod_chunks(1)
            coefs(1)

        @block.gpsimd
        def _(pool):
            pool.wait_ge(fold_rdy, 1)
            pool.tensor_tensor(xm[:, 0:4, :], xn[:, 0:4, :], xm[:, 0:4, :], ALU.subtract).then_inc(odd_rdy, 1)
            pool.tensor_tensor(xm[:, 4, :], xn[:, 8, :], xm[:, 4, :], ALU.subtract).then_inc(odd_rdy, 1)

        @block.tensor
        def _(pe):
            pe.wait_ge(id_in, 16)
            pe.wait_ge(rows_in, 80)
            pe.transpose(psum[:, 0:82], rows[:], core.ident[0:82, 0:82]).then_inc(rowsT, 1)

            def mod_chunks(layer):
                with pe.Fori(0, NCH // 2) as i:
                    for s in range(2):
                        pe.wait_ge(mw_in[s], i * 16 + (16 + 16 * layer * (NCH // 2)))
                        pe.wait_ge(mod_free, i * 2 + (layer * NCH + s + 1))
                        for b in range(2):
                            for k in range(KT):
                                last = pe.matmul(psum[:, 3072 + 512 * s + 2 * b:3072 + 512 * s + 2 * b + 2],
                                                 mw[s][:, k, b * P:(b + 1) * P], scond[:, k, :],
                                                 start=(k == 0), stop=(k == KT - 1))
                        last.then_inc(mw_used, 1)

            pe.wait_ge(cond_rdy, 2)
            mod_chunks(0)
            pe.wait_ge(tab_in, 64)
            pe.wait_ge(fold_rdy, 1)
            pe.wait_ge(odd_rdy, 2)
            pe.wait_ge(mod_free, 2 + NCH)
            for k in range(KT):
                b = 3 * (k % 2) * 512
                ch = slice(k * P, (k + 1) * P)
                if k >= 2:
                    pe.wait_ge(dft_free_a, k - 1)
                    pe.wait_ge(dft_free_v, k - 1)
                for t in range(4):
                    pe.matmul(psum[:, b:b + HL], ev[:, t, ch], cosL[:, t, :], start=(t == 0), stop=False)
                pe.matmul(psum[:, b:b + HL], b0[0:1, ch], altr[0:1, 0:HL], start=False, stop=True).then_inc(dft_mm, 1)
                pe.matmul(psum[:, b + 1024:b + 1024 + HC], ev[:, 4, ch], cosC, start=True, stop=False)
                pe.matmul(psum[:, b + 1024:b + 1024 + HC], b0[32:33, ch], altr[32:33, 0:HC],
                          start=False, stop=True)
                for t in range(4):
                    pe.matmul(psum[:, b + 512:b + 1024], xm[:, t, ch], sinL[:, t, :], start=(t == 0), stop=False,
                              skip_group_check=True)
                for t in range(4):
                    pe.matmul(psum[:, b + 512:b + 513], ev[:, t, ch], altc[:, 0:1], start=False, stop=False,
                              skip_group_check=True)
                pe.matmul(psum[:, b + 512:b + 513], b0[0:1, ch], altr[0:1, 0:1], start=False, stop=True,
                          skip_group_check=True)
                o = b + 1024 + HC
                pe.matmul(psum[:, o:o + HC], xm[:, 4, ch], sinC, start=True, stop=False, skip_group_check=True)
                pe.matmul(psum[:, o:o + 1], ev[:, 4, ch], altc[:, 1:2], start=False, stop=False, skip_group_check=True)
                pe.matmul(psum[:, o:o + 1], b0[32:33, ch], altr[32:33, 0:1], start=False, stop=True,
                          skip_group_check=True).then_inc(dft_mm, 1)
                for j, (t0, nt) in enumerate(((0, 4), (4, 4), (8, 2))):
                    g = 3 * k + j
                    bb = (6 + g % 2) * 512
                    if g >= 2:
                        pe.wait_ge(tr_free, g - 1)
                    for t in range(nt):
                        last = pe.transpose(psum[:, bb + t * P:bb + (t + 1) * P], xn[:, t0 + t, ch], core.ident[:])
                    last.then_inc(tr_mm, 1)
            pe.wait_ge(tr_free, 3 * KT)
            mod_chunks(1)


def fourier_phase(core, io):
    nc, psum = core.nc, core.psum
    pqT = core.at("pqT", [P, KT, TOK], 0)
    nT = core.at("nT", [P, KT, TOK], 40)
    wz = [core.at(f"wz{s}", [P, KT, FD], 80 + 8 * s) for s in range(2)]
    wu = [core.at(f"wu{s}", [P, KT, FD], 96 + 8 * s) for s in range(2)]
    wg = [core.at(f"wg{s}", [P, 2, FD], 112 + 2 * s) for s in range(2)]
    chd = core.at("chd", [P, 2, 2, FD], 116)
    csw = [core.at(f"csw{s}", [P, 2, 2, FD], 120 + 4 * s) for s in range(2)]
    zs = core.at("zs", [P, 2, TOK], 128)
    pq = core.at("pq", [P, 2, TOK], 148)
    es = core.at("es", [P, 2, HL + HC + 4], 168)
    f = core.at("f", [P, 2, TOK], 174)
    y = core.at("y", [P, 2, TOK], 184)
    w_in = io["fn_w_in"][0].rearrange("(k p) (n c) -> n p k c", p=P, c=FD)
    w_grp = io["fn_w_grp"][0].rearrange("g (k p) c -> g p k c", p=P)
    y_v = core.y_d.rearrange("(n p) t -> n p t", p=P)
    SET = [0, 1536]
    CW = 3072
    with ExitStack() as st:
        sem = sems(nc, st)
        chd_in = sem("chd_in")
        wu_in, wz_in, wg_in = ([sem(f"{n}_in{s}") for s in range(2)] for n in ("wu", "wz", "wg"))
        cw_mm, pq_mm, z_mm, eo_mm = sem("cw_mm"), sem("pq_mm"), sem("z_mm"), sem("eo_mm")
        cw_rdy, pq_rdy, zs_rdy = sem("cw_rdy"), sem("pq_rdy"), sem("zs_rdy")
        es_rdy, f_rdy, y_rdy, y_stored = sem("es_rdy"), sem("f_rdy"), sem("y_rdy"), [sem("y_stored0"), sem("y_stored1")]
        block = st.enter_context(nc.Block())

        @block.sync
        def _(sp):
            def load(g, s):
                sp.dma_start(wg[s][:], w_grp[g]).then_inc(wg_in[s], 16)
                sp.dma_start(wu[s][:], w_in[g]).then_inc(wu_in[s], 16)
                sp.dma_start(wz[s][:], w_in[g + FG]).then_inc(wz_in[s], 16)

            def store(g, gi):
                for m in range(2):
                    sp.wait_ge(y_rdy, g * 2 + (m + 3))
                    sp.dma_start(y_v[g * 2 + m], y[:, m, :]).then_inc(y_stored[m], 16)

            sp.dma_start(chd[:], io["ch_dft"]).then_inc(chd_in, 16)
            for m in range(2):
                sp.sem_inc(y_stored[m], 16)
            load(0, 0)
            load(1, 1)
            with sp.Fori(0, FG // 2 - 1) as i:
                for s in range(2):
                    store(i * 2 + s, i)
                    load(i * 2 + (s + 2), s)
            for g in range(FG - 2, FG):
                store(g, None)
            for m in range(2):
                sp.wait_ge(y_stored[m], 16 * (FG + 1))

        @block.tensor
        def _(pe):
            pe.wait_ge(chd_in, 16)
            with pe.Fori(0, FG // 2) as i:
                for s in range(2):
                    g = i * 2 + s
                    pe.wait_ge(wg_in[s], i * 16 + 16)
                    pe.wait_ge(cw_rdy, g + 1)
                    for t in range(2):
                        for ct in range(2):
                            for k in range(2):
                                last = pe.matmul(psum[:, CW + 512 * t + FD * ct:CW + 512 * t + FD * ct + FD],
                                                 chd[:, t, k, ct * P:(ct + 1) * P], wg[s][:, k, :],
                                                 start=(k == 0), stop=(k == 1))
                    last.then_inc(cw_mm, 1)
                    for w, rhs, w_in_sem, done, free in ((wu, pqT, wu_in, pq_mm, f_rdy), (wz, nT, wz_in, z_mm, pq_rdy)):
                        pe.wait_ge(w_in_sem[s], i * 16 + 16)
                        for m in range(2):
                            pe.wait_ge(free, g * 2 + (m + 1))
                            for lo, n in ((0, 512), (512, 512), (1024, 256)):
                                for k in range(KT):
                                    last = pe.matmul(psum[:, SET[m] + lo:SET[m] + lo + n],
                                                     w[s][:, k, m * P:(m + 1) * P], rhs[:, k, lo:lo + n],
                                                     start=(k == 0), stop=(k == KT - 1))
                            last.then_inc(done, 1)
                    pe.wait_ge(cw_rdy, g + 2)
                    pe.wait_ge(pq_rdy, g * 2 + 2)
                    for m in range(2):
                        pe.wait_ge(zs_rdy, g * 2 + (m + 1))
                        b, dc = SET[m], slice(m * P, (m + 1) * P)
                        for t, off, lo, n in ((0, 0, 0, HL), (1, 512, HL, HL), (0, 1024, LAT, HC),
                                              (1, 1024 + HC, LAT + HC, HC), (0, 1024 + 2 * HC, HL, 1),
                                              (0, 1024 + 2 * HC + 1, LAT + HC, 1)):
                            for k in range(2):
                                last = pe.matmul(psum[:, b + off:b + off + n], csw[s][:, t, k, dc],
                                                 pq[:, k, lo:lo + n], start=(k == 0), stop=(k == 1))
                        last.then_inc(eo_mm, 1)

        @block.scalar
        def _(act):
            act.sem_inc(cw_rdy, 1)
            with act.Fori(0, FG // 2) as i:
                for s in range(2):
                    g = i * 2 + s
                    act.wait_ge(cw_mm, g + 1)
                    act.activation(csw[s][:].rearrange("p a b c -> p (a b c)"), psum[:, CW:CW + 1024], ACT.Copy).then_inc(cw_rdy, 1)
                    for m in range(2):
                        act.wait_ge(z_mm, g * 2 + (m + 1))
                        act.wait_ge(y_rdy, g * 2 + (m + 1))
                        act.activation(zs[:, m, :], psum[:, SET[m]:SET[m] + TOK], ACT.Silu).then_inc(zs_rdy, 1)
                    for m in range(2):
                        b = SET[m]
                        act.wait_ge(eo_mm, g * 2 + (m + 1))
                        act.activation(es[:, m, 0:HL], psum[:, b:b + HL], ACT.Copy)
                        act.activation(es[:, m, HL:HL + HC], psum[:, b + 1024:b + 1024 + HC], ACT.Copy)
                        act.activation(f[:, m, 0:LAT + 1:LAT], psum[:, b:b + 1025:1024], ACT.Copy)
                        act.activation(f[:, m, HL:LAT + HC + 1:HL + HC], psum[:, b + 1024 + 2 * HC:b + 1026 + 2 * HC],
                                       ACT.Copy).then_inc(es_rdy, 1)

        @block.vector
        def _(dve):
            dve.sem_inc(f_rdy, 2)
            with dve.Fori(0, FG // 2) as i:
                for s in range(2):
                    g = i * 2 + s
                    for m in range(2):
                        dve.wait_ge(pq_mm, g * 2 + (m + 1))
                        dve.tensor_copy(pq[:, m, :], psum[:, SET[m]:SET[m] + TOK]).then_inc(pq_rdy, 1)
                    for m in range(2):
                        b = SET[m]
                        dve.wait_ge(es_rdy, g * 2 + (m + 1))
                        for o, lo, L in ((512, 0, LAT), (1024 + HC, HL, CTX)):
                            t0, h = (0 if L == LAT else LAT), L // 2
                            for op, dst in ((ALU.subtract, f[:, m, t0 + 1:t0 + h]), (ALU.add, f[:, m, t0 + L - 1:t0 + h:-1])):
                                last = dve.tensor_tensor(dst, es[:, m, lo + 1:lo + h], psum[:, b + o + 1:b + o + h], op)
                        last.then_inc(f_rdy, 1)

        @block.gpsimd
        def _(pool):
            pool.sem_inc(y_rdy, 2)
            with pool.Fori(0, FG // 2) as i:
                for s in range(2):
                    g = i * 2 + s
                    for m in range(2):
                        pool.wait_ge(f_rdy, g * 2 + (m + 3))
                        pool.wait_ge(y_stored[m], g * 16 + 16)
                        pool.tensor_tensor(y[:, m, :], f[:, m, :], zs[:, m, :], ALU.mult).then_inc(y_rdy, 1)


def output_phase(core, io, layer):
    nc, psum, ident = core.nc, core.psum, core.ident
    last_layer = layer == 1
    name = lambda n: f"{n}_o{layer}"
    n1T = None if last_layer else core.at("n1T", [P, KT, TOK], 0)
    wo = core.at(name("wo"), [P, 16, D], 40)
    yb = [core.at(name(f"yb{s}"), [P, 16, P], 104 + 8 * s) for s in range(2)]
    h = [core.at(name(f"h{s}"), [P, D], 120 + 4 * s) for s in range(2)]
    gx = [core.at(name(f"gx{s}"), [P, D], 128 + 4 * s) for s in range(2)]
    gate = core.at(name("gate"), [P, 2, D], 136)
    fg = core.at(name("fg"), [P, D], 144)
    junk = core.at(name("junk"), [P, D], 148)
    st_ = core.at(name("st"), [P, 2, 4], 152)
    nlat = NL
    y_v = (core.y2_d if last_layer else core.y_d).rearrange("(c p) (n t) -> n p c t", p=P, t=P)
    h_v = (core.h_d if last_layer else io["x"][0]).rearrange("(n p) d -> n p d", p=P)
    c_v = io["ctx"][0].rearrange("(n p) d -> n p d", p=P)
    dst_v = (io["out"][0] if last_layer else core.h_d).rearrange("(n p) d -> n p d", p=P)
    w_v = (io["dn_w_out"] if last_layer else io["fn_w_out"])[0].rearrange("(c p) d -> p c d", p=P)
    tiles = NL if last_layer else NT
    conds = 1 if last_layer else 2
    with ExitStack() as st:
        sem = sems(nc, st)
        wo_in = [sem(f"wo_in{q}") for q in range(4)]
        y_in, h_in, stored = ([sem(f"{n}{s}") for s in range(2)] for n in ("y_in", "h_in", "h_stored"))
        fg_in, g_mm, gate_rdy = sem("fg_in"), sem("g_mm"), sem("gate_rdy")
        o_mm, gx_rdy, h_rdy, ss_rdy, var_rdy = sem("o_mm"), sem("gx_rdy"), sem("h_rdy"), sem("ss_rdy"), sem("var_rdy")
        std_rdy, rstd_rdy, n_rdy, t_mm, t_free = sem("std_rdy"), sem("rstd_rdy"), sem("n_rdy"), sem("t_mm"), sem("t_free")
        block = st.enter_context(nc.Block())

        def tiles_loop(eng, body):
            with eng.Fori(0, NL // 2) as i:
                for s in range(2):
                    body(i * 2 + s, s, i, 0)
            for n in range(NL, tiles):
                body(n, n % 2, n // 2, 1)

        @block.sync
        def _(sp):
            def load(n, s, ctx_tile):
                sp.dma_start(yb[s][:], y_v[n]).then_inc(y_in[s], 16)
                sp.dma_start(h[s][:], c_v[n - NL] if ctx_tile else h_v[n]).then_inc(h_in[s], 16)

            for q in range(4):
                sp.dma_start(wo[:, 4 * q:4 * q + 4, :], w_v[:, 4 * q:4 * q + 4, :]).then_inc(wo_in[q], 16)
                if q == 0:
                    load(0, 0, 0)
            load(1, 1, 0)
            if last_layer:
                sp.dma_start(fg[:], io["final_g"].rearrange("(a n) -> a n", a=1).broadcast_to([P, D])).then_inc(fg_in, 16)

            def turn(n, s, i, store_it, load_ctx):
                if store_it:
                    sp.wait_ge(n_rdy if last_layer else h_rdy, n + 1)
                    sp.dma_start(dst_v[n], h[s][:]).then_inc(stored[s], 16)
                if load_ctx is not None:
                    sp.wait_ge(o_mm, n + 1)
                    sp.wait_ge(n_rdy, n + 1)
                    if store_it:
                        sp.wait_ge(stored[s], i * 16 + 16)
                    load(n + 2, s, load_ctx)

            with sp.Fori(0, NL // 2 - 1) as i:
                for s in range(2):
                    turn(i * 2 + s, s, i, True, 0)
            for n in range(NL - 2, NL):
                turn(n, n % 2, n // 2, True, 1 if tiles > NL else None)
            for s in range(2):
                sp.wait_ge(stored[s], 16 * NL // 2)

        @block.tensor
        def _(pe):
            for c in range(conds):
                for k in range(KT):
                    col = core.modT[:, 24 * layer + 16 + k, c:c + 1].broadcast_to([P, P])
                    last = pe.matmul(psum[:, 1024 * c + k * P:1024 * c + (k + 1) * P], col, ident[:], start=True, stop=True)
            last.then_inc(g_mm, 1)
            for q in range(4):
                pe.wait_ge(wo_in[q], 16)
            pe.wait_ge(gate_rdy, 1)

            def norm_transposes(n, s):
                pe.wait_ge(n_rdy, n + 1)
                pe.wait_ge(t_free, n + 1)
                b = 2048 + 1024 * s
                for k in range(KT):
                    last = pe.transpose(psum[:, b + k * P:b + (k + 1) * P], gx[s][:, k * P:(k + 1) * P], ident[:])
                last.then_inc(t_mm, 1)

            def body(n, s, i, c):
                pe.wait_ge(y_in[s], i * 16 + 16)
                pe.wait_ge(gx_rdy, n + 1)
                for half in range(2):
                    o = 1024 * s + 512 * half
                    for k in range(16):
                        last = pe.matmul(psum[:, o:o + 512], yb[s][:, k, :], wo[:, k, 512 * half:512 * half + 512],
                                         start=(k == 0), stop=(k == 15))
                last.then_inc(o_mm, 1)

            if last_layer:
                tiles_loop(pe, body)
            else:
                body(0, 0, 0, 0)
                with pe.Fori(0, NL // 2) as i:
                    for s in range(2):
                        n = i * 2 + s
                        pe.wait_ge(y_in[1 - s], i * 16 + (16 + 16 * s))
                        pe.wait_ge(gx_rdy, n + 2)
                        for half in range(2):
                            o = 1024 * (1 - s) + 512 * half
                            for k in range(16):
                                last = pe.matmul(psum[:, o:o + 512], yb[1 - s][:, k, :],
                                                 wo[:, k, 512 * half:512 * half + 512], start=(k == 0), stop=(k == 15))
                        last.then_inc(o_mm, 1)
                        norm_transposes(n, s)
                body(NL + 1, 1, NL // 2, 1)
                norm_transposes(NL, 0)
                norm_transposes(NL + 1, 1)

        @block.vector
        def _(dve):
            dve.sem_inc(gx_rdy, 2)
            dve.wait_ge(g_mm, 1)
            dve.tensor_copy(gate[:, 0:conds, :].rearrange("p c d -> p (c d)"), psum[:, 0:1024 * conds]).then_inc(gate_rdy, 1)
            dve.wait_ge(gate_rdy, 1)
            if last_layer:
                dve.wait_ge(fg_in, 16)

            def body(n, s, i, c):
                dve.wait_ge(o_mm, n + 1)
                if not last_layer:
                    dve.wait_ge(t_free, n + 1)
                dve.tensor_tensor(gx[s][:], psum[:, 1024 * s:1024 * s + 1024], gate[:, c, :], ALU.mult).then_inc(gx_rdy, 1)
                dve.wait_ge(gx_rdy, n + 3)
                dve.wait_ge(h_in[s], i * 16 + 16)
                dve.tensor_tensor(h[s][:], h[s][:], gx[s][:], ALU.add).then_inc(h_rdy, 1)
                dve.wait_ge(ss_rdy, n + 1)
                dve.tensor_scalar(st_[:, s, 1:2], st_[:, s, 0:1], 1.0 / D, EPS, ALU.mult, ALU.add).then_inc(var_rdy, 1)
                dve.wait_ge(std_rdy, n + 1)
                dve.reciprocal(st_[:, s, 3:4], st_[:, s, 2:3]).then_inc(rstd_rdy, 1)
                dve.wait_ge(rstd_rdy, n + 1)
                if last_layer:
                    dve.scalar_tensor_tensor(h[s][:], h[s][:], st_[:, s, 3:4], fg[:], ALU.mult, ALU.mult).then_inc(n_rdy, 1)
                else:
                    dve.tensor_scalar(gx[s][:], h[s][:], st_[:, s, 3:4], None, ALU.mult).then_inc(n_rdy, 1)

            tiles_loop(dve, body)

        @block.scalar
        def _(act):
            if not last_layer:
                act.sem_inc(t_free, 2)

            def stats(n, s, i, c):
                act.wait_ge(h_rdy, n + 1)
                act.activation(junk[:], h[s][:], ACT.Square, accum_out=st_[:, s, 0:1]).then_inc(ss_rdy, 1)
                act.wait_ge(var_rdy, n + 1)
                act.activation(st_[:, s, 2:3], st_[:, s, 1:2], ACT.Sqrt).then_inc(std_rdy, 1)

            def to_n1T(n, s, i, c):
                act.wait_ge(t_mm, n + 1)
                b = 2048 + 1024 * s
                for k in range(KT):
                    last = act.activation(n1T[:, k, bass.ts(n, P)], psum[:, b + k * P:b + (k + 1) * P], ACT.Identity,
                                          scale=core.acoef[:, 1, k, c:c + 1], bias=core.modT[:, 24 + k, c:c + 1])
                last.then_inc(t_free, 1)

            def body(n, s, i, c):
                stats(n, s, i, c)
                if not last_layer:
                    to_n1T(n, s, i, c)

            tiles_loop(act, body)


def project_phase(core, io):
    nc, psum, ident = core.nc, core.psum, core.ident
    n1T = core.at("n1T", [P, KT, TOK], 0)
    wq = core.at("wq", [P, KT, P], 40)
    wk = core.at("wk", [P, KT, P], 44)
    wv = core.at("wv", [P, KT, DV], 48)
    wz = core.at("wz_d", [P, KT, DV], 56)
    PADR, PADC = GR + 2, GW + 2
    NPAD = PADR * PADC + CTX + 2
    pad = [core.at(f"pad{s}", [P, NPAD], 64 + 6 * s) for s in range(2)]
    acc = [core.at(f"acc{s}", [P, TOK], 76 + 5 * s) for s in range(2)]
    sil = [core.at(f"sil{s}", [P, TOK], 86 + 5 * s) for s in range(2)]
    qt = core.at("qt", [P, NL, P], 96)
    kt = core.at("kt", [P, NT, P], 100)
    vt = [core.at(f"vt{s}", [P, NT, P], 105 + 5 * s) for s in range(2)]
    qT = core.at("qT", [P, LAT], 115)
    kT = core.at("kT", [P, TOK], 119)
    zs = [core.at(f"zs_d{s}", [P, LAT], 124 + 4 * s) for s in range(2)]
    sq = core.at("sq", [P, NT, P], 132)
    ssq = core.at("ssq", [P, 2, 3, 16], 137)
    wab = core.at("wab", [P, KT, 32], 138)
    crow = core.at("crow", [9, 4096], 139)
    cw = core.at("cw", [P, 32, 9], 155)
    cwh = core.at("cwh", [P, 4, 9], 157)
    ab = core.at("ab", [P, 2, 16], 158)
    gw = [core.at(f"gw{s}", [P, NT, 16], 159 + s) for s in range(4)]
    wi = io["dn_w_in"][0].rearrange("(k p) c -> p k c", p=P)
    QO, KO, VO, ZO, AO = 0, D, 2 * D, 2 * D + FW, 2 * D + 2 * FW
    k_v = core.k_d.rearrange("(n p) (h c) -> h p n c", p=P, c=P)
    v_v = core.v_d.rearrange("(n p) (h c) -> h p n c", p=P, c=P)
    z_v = core.z_d.rearrange("(n p) t -> n p t", p=P)
    SET = [0, 1536]
    FULL, LATO = ((0, 512), (512, 512), (1024, 256)), ((0, 512), (512, 512))
    with ExitStack() as st:
        sem = sems(nc, st)
        misc_in = sem("misc_in")
        w_in = {n: sem(f"w{n}_in") for n in "qkvz"}
        ab_mm, tap_mm, tap_rdy = sem("ab_mm"), sem("tap_mm"), sem("tap_rdy")
        gch, gact = sem("decay_vec"), sem("decay_act")
        mm = sem("proj_mm")
        evac = sem("proj_evac")
        conv = sem("conv_done")
        silu = sem("silu_done")
        tmm, tfree = sem("t_mm"), sem("t_free_d")
        sq_rdy, red, var, std, nrm = sem("sq_rdy"), sem("red"), sem("var"), sem("std"), sem("nrm")
        taps, taps_used = sem("taps"), sem("taps_used")
        vec = sem("conv_chain")
        out_s = {n: sem(f"{n}_stored") for n in ("qT", "k", "kT", "v0", "v1", "z0", "z1")}
        block = st.enter_context(nc.Block())
        T = {"q": 0, "k": 2, "qT": 5, "v0": 7, "kT": 10, "v1": 13}
        NB = 16

        @block.sync
        def _(sp):
            sp.dma_start(wab[:], wi[:, :, AO:AO + 32]).then_inc(misc_in, 16)
            sp.dma_start(ab[:, 0, :], io["dn_dt_bias"].rearrange("a b c -> a (b c)").broadcast_to([P, 16])).then_inc(misc_in, 16)
            sp.dma_start(ab[:, 1, :], io["dn_a_log"].rearrange("a b c -> a (b c)").broadcast_to([P, 16])).then_inc(misc_in, 16)
            sp.dma_start(crow[:], io["dn_conv"][0].rearrange("a b c -> (a b) c")).then_inc(misc_in, 16)
            wqv, wkv, wvv, wzv = (wi[:, :, o:o + n * H].rearrange("p k (h c) -> h p k c", c=n)
                                  for o, n in ((QO, DK), (KO, DK), (VO, DV), (ZO, DV)))
            src = {"q": (wq, wqv), "k": (wk, wkv), "v": (wv, wvv), "z": (wz, wzv)}

            def load(n, hh):
                sp.dma_start(src[n][0][:], src[n][1][hh]).then_inc(w_in[n], 16)

            for n in "qkvz":
                load(n, 0)
            for n in out_s:
                sp.sem_inc(out_s[n], 16)

            def turn(hh, more):
                sp.wait_ge(mm, hh * 6 + 1)
                if more:
                    load("q", hh + 1)
                sp.wait_ge(mm, hh * 6 + 2)
                if more:
                    load("k", hh + 1)
                sp.wait_ge(tfree, hh * NB + (2 + T["qT"] + 2))
                sp.dma_start(core.qT_d[hh], qT[:]).then_inc(out_s["qT"], 16)
                sp.wait_ge(mm, hh * 6 + 4)
                if more:
                    load("v", hh + 1)
                sp.wait_ge(tfree, hh * NB + (2 + T["v0"] + 3))
                sp.dma_start(v_v[hh * 2], vt[0][:]).then_inc(out_s["v0"], 16)
                sp.wait_ge(nrm, hh * 2 + 2)
                sp.dma_start(k_v[hh], kt[:]).then_inc(out_s["k"], 16)
                sp.wait_ge(tfree, hh * NB + (2 + T["kT"] + 3))
                sp.dma_start(core.kT_d[hh], kT[:]).then_inc(out_s["kT"], 16)
                sp.wait_ge(evac, hh * 6 + 7)
                sp.dma_start(z_v[hh * 2], zs[0][:]).then_inc(out_s["z0"], 16)
                sp.wait_ge(tfree, hh * NB + (2 + T["v1"] + 3))
                sp.dma_start(v_v[hh * 2 + 1], vt[1][:]).then_inc(out_s["v1"], 16)
                sp.wait_ge(evac, hh * 6 + 8)
                if more:
                    load("z", hh + 1)
                sp.dma_start(z_v[hh * 2 + 1], zs[1][:]).then_inc(out_s["z1"], 16)

            with sp.Fori(0, H - 1) as hh:
                turn(hh, True)
            turn(H - 1, False)
            for n in out_s:
                sp.wait_ge(out_s[n], 16 * (H + 1))

        @block.tensor
        def _(pe):
            pe.wait_ge(misc_in, 64)
            for n in range(NT):
                for k in range(KT):
                    last = pe.matmul(psum[:, n * 32:(n + 1) * 32], n1T[:, k, n * P:(n + 1) * P], wab[:, k, :],
                                     start=(k == 0), stop=(k == KT - 1))
            last.then_inc(ab_mm, 1)
            for t in range(32):
                last = pe.transpose(psum[:, 3072 + 9 * t:3072 + 9 * t + 9], crow[:, t * P:(t + 1) * P], ident[0:9, 0:9])
            last.then_inc(tap_mm, 1)
            pe.wait_ge(gch, 2)
            pe.wait_ge(tap_rdy, 1)

            with pe.Fori(0, H) as hh:
                def product(j, w, cols, groups):
                    pe.wait_ge(evac, hh * 6 + (j + 1))
                    for lo, n in groups:
                        for k in range(KT):
                            last = pe.matmul(psum[:, SET[j % 2] + lo:SET[j % 2] + lo + n], w[:, k, cols],
                                             n1T[:, k, lo:lo + n], start=(k == 0), stop=(k == KT - 1))
                    last.then_inc(mm, 1)

                def transposes(what, src, tiles):
                    for j, t0 in enumerate(range(0, tiles, 4)):
                        b = T[what] + j
                        pe.wait_ge(tfree, hh * NB + (b + 1))
                        for t in range(t0, min(t0 + 4, tiles)):
                            o = 3072 + 512 * (b % 2) + (t - t0) * P
                            last = pe.transpose(psum[:, o:o + P], src(t), ident[:])
                        last.then_inc(tmm, 1)

                chan = lambda s: (lambda t: sil[s][:, t * P:(t + 1) * P])
                pe.wait_ge(w_in["q"], hh * 16 + 16)
                product(0, wq, slice(0, P), LATO)
                pe.wait_ge(w_in["k"], hh * 16 + 16)
                product(1, wk, slice(0, P), FULL)
                pe.wait_ge(silu, hh * 4 + 1)
                transposes("q", chan(0), NL)
                pe.wait_ge(w_in["v"], hh * 16 + 16)
                product(2, wv, slice(0, P), FULL)
                pe.wait_ge(silu, hh * 4 + 2)
                transposes("k", chan(1), NT)
                pe.wait_ge(nrm, hh * 2 + 1)
                transposes("qT", lambda t: qt[:, t, :], NL)
                product(3, wv, slice(P, 2 * P), FULL)
                pe.wait_ge(silu, hh * 4 + 3)
                transposes("v0", chan(0), NT)
                pe.wait_ge(nrm, hh * 2 + 2)
                transposes("kT", lambda t: kt[:, t, :], NT)
                pe.wait_ge(w_in["z"], hh * 16 + 16)
                product(4, wz, slice(0, P), LATO)
                pe.wait_ge(silu, hh * 4 + 4)
                transposes("v1", chan(1), NT)
                product(5, wz, slice(P, 2 * P), LATO)

        def inner(s):
            g = pad[s][:, 0:PADR * PADC].rearrange("p (r c) -> p r c", c=PADC)
            return g, pad[s][:, PADR * PADC:NPAD]

        @block.scalar
        def _(act):
            act.sem_inc(evac, 2)
            act.sem_inc(tfree, 2)
            act.wait_ge(tap_mm, 1)
            act.activation(cw[:].rearrange("p t n -> p (t n)"), psum[:, 3072:3072 + 288], ACT.Copy).then_inc(tap_rdy, 1)
            act.wait_ge(gch, 8)
            act.activation(gw[1][:], gw[1][:], ACT.Exp, scale=-1.0).then_inc(gact, 1)
            act.activation(gw[3][:], gw[3][:], ACT.Exp, scale=-1.0).then_inc(gact, 1)
            act.activation(gw[2][:], gw[2][:], ACT.Exp).then_inc(gact, 1)
            act.activation(ab[:, 1, :], ab[:, 1, :], ACT.Exp).then_inc(gact, 1)
            act.wait_ge(gch, 10)
            act.activation(gw[1][:], gw[1][:], ACT.Ln).then_inc(gact, 1)
            act.wait_ge(vec, 1)

            with act.Fori(0, H) as hh:
                def to_pad(j):
                    act.wait_ge(mm, hh * 6 + (j + 1))
                    s, b = j % 2, SET[j % 2]
                    g, c = inner(s)
                    last = act.activation(g[:, 1:GR + 1, 1:GW + 1], psum[:, b:b + LAT].rearrange("p (r c) -> p r c", c=GW), ACT.Copy)
                    if j:
                        last = act.activation(c[:, 1:CTX + 1], psum[:, b + LAT:b + TOK], ACT.Copy)
                    last.then_inc(evac, 1)

                def do_silu(j):
                    act.wait_ge(conv, hh * 4 + (j + 1))
                    n = TOK if j else LAT
                    act.activation(sil[j % 2][:, 0:n], acc[j % 2][:, 0:n], ACT.Silu).then_inc(silu, 1)

                def tokens(what, dst, tiles, squares):
                    for j, t0 in enumerate(range(0, tiles, 4)):
                        b, n = T[what] + j, min(4, tiles - t0)
                        src = psum[:, 3072 + 512 * (b % 2):3072 + 512 * (b % 2) + n * P].rearrange("p (t c) -> p t c", c=P)
                        act.wait_ge(tmm, hh * NB + (b + 1))
                        if squares:
                            act.activation(sq[:, t0:t0 + n, :], src, ACT.Square).then_inc(sq_rdy, 1)
                        act.activation(dst[:, t0:t0 + n, :], src, ACT.Copy).then_inc(tfree, 1)

                def std_of(j):
                    act.wait_ge(var, hh * 2 + (j + 1))
                    act.activation(ssq[:, j, 1, 0:NT], ssq[:, j, 0, 0:NT], ACT.Sqrt).then_inc(std, 1)

                act.wait_ge(taps_used, hh + 1)
                for j, lo in ((0, hh), (1, hh + 8), (2, hh * 2 + 16), (3, hh * 2 + 17)):
                    last = act.activation(cwh[:, j, :], cw[:, bass.ds(lo, 1), :].rearrange("p a n -> p (a n)"), ACT.Copy)
                last.then_inc(taps, 1)
                cm = lambda t: t[:].rearrange("p (t c) -> p t c", c=P)
                to_pad(0)
                do_silu(0)
                to_pad(1)
                tokens("q", qt, NL, True)
                do_silu(1)
                std_of(0)
                to_pad(2)
                act.wait_ge(out_s["k"], hh * 16 + 16)
                tokens("k", kt, NT, True)
                act.wait_ge(out_s["qT"], hh * 16 + 16)
                tokens("qT", cm(qT), NL, False)
                do_silu(2)
                std_of(1)
                to_pad(3)
                act.wait_ge(out_s["v0"], hh * 16 + 16)
                tokens("v0", vt[0], NT, False)
                act.wait_ge(out_s["kT"], hh * 16 + 16)
                tokens("kT", cm(kT), NT, False)
                do_silu(3)
                for m in range(2):
                    act.wait_ge(mm, hh * 6 + (5 + m))
                    act.wait_ge(out_s[f"z{m}"], hh * 16 + 16)
                    act.activation(zs[m][:], psum[:, SET[m]:SET[m] + LAT], ACT.Silu).then_inc(evac, 1)
                    if m == 0:
                        act.wait_ge(out_s["v1"], hh * 16 + 16)
                        tokens("v1", vt[1], NT, False)

        @block.vector
        def _(dve):
            dve.sem_inc(taps_used, 1)
            dve.memset(pad[0][:], 0.0)
            dve.memset(pad[1][:], 0.0).then_inc(vec, 1)
            dve.memset(ssq[:], 1.0).then_inc(vec, 1)
            dve.wait_ge(ab_mm, 1)
            ga = psum[:, 0:320].rearrange("p (n c) -> p n c", c=32)
            dt = ab[:, 0, :].unsqueeze(1).broadcast_to([P, NT, 16])
            n = [0]

            def link(ins):
                n[0] += 1
                ins.then_inc(gch, 1)
                dve.wait_ge(gch, n[0])

            link(dve.tensor_copy(gw[3][:], ga[:, :, 16:32]))
            link(dve.tensor_tensor(gw[0][:], ga[:, :, 0:16], dt, ALU.add))
            link(dve.tensor_scalar(gw[1][:], gw[0][:], -1.0, None, ALU.mult))
            link(dve.tensor_tensor(gw[1][:], gw[1][:], gw[0][:], ALU.max))
            link(dve.tensor_scalar(gw[0][:], gw[0][:], 0.0, None, ALU.max))
            link(dve.tensor_scalar(gw[2][:], gw[3][:], -1.0, None, ALU.mult))
            link(dve.tensor_tensor(gw[3][:], gw[3][:], gw[2][:], ALU.max))
            link(dve.tensor_scalar(gw[2][:], gw[2][:], 0.0, -1.0, ALU.max, ALU.mult))
            dve.wait_ge(gact, 4)
            link(dve.tensor_scalar(gw[3][:], gw[3][:], 1.0, None, ALU.add))
            link(dve.tensor_scalar(gw[1][:], gw[1][:], 1.0, None, ALU.add))
            link(dve.reciprocal(gw[3][:], gw[3][:]))
            link(dve.tensor_tensor(core.beta[:], gw[2][:], gw[3][:], ALU.mult))
            link(dve.tensor_scalar(core.nbeta[:], core.beta[:], -1.0, None, ALU.mult))
            dve.wait_ge(gact, 5)
            link(dve.tensor_tensor(gw[0][:], gw[0][:], gw[1][:], ALU.add))
            link(dve.scalar_tensor_tensor(core.gtok[:], gw[0][:], -1.0,
                                          ab[:, 1, :].unsqueeze(1).broadcast_to([P, NT, 16]), ALU.mult, ALU.mult))

            with dve.Fori(0, H) as hh:
                NV = 8 + 3 * 10
                at = [0]

                def chain(ins):
                    at[0] += 1
                    ins.then_inc(vec, 1)
                    dve.wait_ge(vec, hh * NV + (2 + at[0]))

                def convolve(j):
                    s = j % 2
                    dve.wait_ge(evac, hh * 6 + (j + 3))
                    g, c = inner(s)
                    a = acc[s][:, 0:LAT].rearrange("p (r c) -> p r c", c=GW)
                    ac = acc[s][:, LAT:TOK]
                    tap = lambda t: cwh[:, j, t:t + 1]
                    if j:
                        dve.tensor_scalar(ac, c[:, 0:CTX], tap(3), None, ALU.mult)
                    chain(dve.tensor_scalar(a, g[:, 0:GR, 0:GW], tap(0), None, ALU.mult))
                    for t in range(1, 9):
                        last = dve.scalar_tensor_tensor(a, g[:, t // 3:t // 3 + GR, t % 3:t % 3 + GW], tap(t), a, ALU.mult, ALU.add)
                        if t < 8:
                            chain(last)
                        if j and t in (4, 5):
                            last = dve.scalar_tensor_tensor(ac, c[:, t - 3:t - 3 + CTX], tap(t), ac, ALU.mult, ALU.add)
                            chain(last)
                    return last

                def norm(j, x, tiles, scale):
                    nb = (tiles + 3) // 4
                    dve.wait_ge(sq_rdy, hh * 5 + (2 if j == 0 else 5))
                    dve.reduce_sum(ssq[:, j, 2, 0:tiles], sq[:, 0:tiles, :], AXX).then_inc(red, 1)
                    dve.wait_ge(red, hh * 4 + (2 * j + 1))
                    dve.tensor_scalar(ssq[:, j, 0, 0:tiles], ssq[:, j, 2, 0:tiles], EPS, 1.0 / scale ** 2, ALU.add, ALU.mult).then_inc(var, 1)
                    dve.wait_ge(std, hh * 2 + (j + 1))
                    dve.reciprocal(ssq[:, j, 2, 0:tiles], ssq[:, j, 1, 0:tiles]).then_inc(red, 1)
                    dve.wait_ge(red, hh * 4 + (2 * j + 2))
                    dve.wait_ge(tfree, hh * NB + (2 + T["qk"[j]] + nb))
                    dve.tensor_tensor(x[:], x[:], ssq[:, j, 2, 0:tiles].unsqueeze(2).broadcast_to([P, tiles, P]),
                                      ALU.mult).then_inc(nrm, 1)

                dve.wait_ge(taps, hh + 1)
                convolve(0).then_inc(conv, 1)
                convolve(1).then_inc(conv, 1)
                norm(0, qt, NL, DK ** -0.5)
                convolve(2).then_inc(conv, 1)
                norm(1, kt, NT, 1.0)
                convolve(3).then_inc(conv, 1)
                dve.wait_ge(conv, hh * 4 + 4)
                dve.sem_inc(taps_used, 1)
                assert at[0] == NV


class Steps:

    def __init__(self, names):
        self.names = names.split()
        self.n = len(self.names)

    def done(self, step, name):
        return step * self.n + (self.names.index(name) + 1)


NB = 32
TOP = (5, 6)
SUBST = " ".join(f"m{k} a{k}" for k in range(NB - 1))
PE_EV = Steps("gb gp kk0 kk1 kk2 kk3 " + " ".join(f"rp{r}" for r in range(NB // 2)) + " x5 d5 t5 x6 t6 "
              + " ".join(f"{w}{p}" for w in ("ks", "vn", "o", "su") for p in range(4)))
ACT_EV = Steps("eg el tl dt hi tt x5 x6 vn0 vn1 vn2 vn3")
DVE_EV = Steps("gps td gm na0 na1 na2 na3 pt lo " + SUBST + " tr tu5 tt5 tt6 "
               + " ".join(f"{w}{p}" for w in ("r", "oa", "su") for p in range(4)))
POOL_EV = Steps("gc gms db bc z qg kg kta")


def delta_phase(core, io):
    nc, psum, ident = core.nc, core.psum, core.ident
    F32R = mybir.dt.float32r
    o = core.at("o", [P, NL, FW], 0)
    per = lambda n, shape, kb, dt=F32: [core.at(f"{n}_{d}", shape, 64 + 60 * d + kb, dt) for d in range(2)]
    S = per("S", [P, H, DV], 0)
    kq = per("kq", [P, H, 2, P], 8)
    kk = per("kk", [P, H, P], 16)
    v = per("v", [P, H, DV], 20)
    T = per("T", [P, H, P], 28)
    TT = per("TT", [P, H, P], 32)
    X = per("X", [P, H, P], 36)
    nA = per("nA", [P, H, P], 40)
    DT = per("DT", [P, H, P], 44)
    EG = per("EG", [P, H, P], 48)
    QG = per("QG", [P, H, P], 52)
    R = per("R", [P, H, NB], 56)
    tmp = per("tmp", [P, H, NB], 57)
    ahi = per("ahi", [P, H, NB], 58, F32R)
    alo = per("alo", [P, H, NB], 59, F32R)
    U = core.at("U", [P, 2, P], 184)
    NM = core.at("NM", [P, 2, P], 185)
    lm = core.at("lm", [P, 2, 2, 64], 186, I32)
    sel = core.at("sel", [P, NB, P], 187, F32R)
    selst = core.at("selst", [P, NB, P], 0)
    eye = core.at("eye", [P, NB], 203)
    small = lambda n, k: [core.at(f"{n}_{d}", [P, H], 203.125 + (2 * k + d) / 32) for d in range(2)]
    gc, bc, nb, gps, td, tl, el = (small(n, k) for k, n in enumerate(("gc", "bc", "nb", "gps", "td", "tl", "el")))
    kT_v = core.kT_d.rearrange("h p (n t) -> n p h t", t=P)
    qT_v = core.qT_d.rearrange("h p (n t) -> n p h t", t=P)
    k_v = core.k_d.rearrange("(n p) (h c) -> n p h c", p=P, h=H)
    v_v = core.v_d.rearrange("(n p) (h c) -> n p h c", p=P, h=H)
    LAST = (P - 1, 0)
    b3 = lambda a: a[:].unsqueeze(2).broadcast_to([P, H, P])
    quad = [slice(NB * q, NB * (q + 1)) for q in range(4)]

    def half(t, l, which):
        return t[:].rearrange("p h (n two s) -> p h n two s", two=2, s=1 << l)[:, :, :, which, :]

    def packed(bank, l):
        return bank.rearrange("p (h n s) -> p h n s", h=H, s=1 << l)

    def mask(l, which):
        m = lm[:, l - TOP[0], which, :].rearrange("p (n s) -> p n s", s=1 << l)
        return m.unsqueeze(1).broadcast_to([P, H, 64 >> l, 1 << l])

    with ExitStack() as st:
        sem = sems(nc, st)
        tab_in, nm_rdy, init_rdy, sel_rdy = sem("tab_in5"), sem("nm_rdy"), sem("init_rdy"), sem("sel_rdy")
        kT_in, qT_in, k_in, v_in = ([sem(f"{n}{d}") for d in (0, 1)] for n in ("kT_in", "qT_in", "k_in", "v_in"))
        pe_done = [sem("pe_fwd"), sem("pe_bwd")]
        act_done = [sem("act_fwd"), sem("act_bwd")]
        dve_done = [sem("dve_fwd"), sem("dve_bwd")]
        pool_done = [sem("pool_fwd"), sem("pool_bwd")]
        merges = sem("merges")
        block = st.enter_context(nc.Block())

        def bank(d, b):
            return psum[:, (4 * d + b) * 512:(4 * d + b + 1) * 512]

        def head2(d, p):
            return bank(d, p).rearrange("p (a c) -> p a c", a=2)

        class At:

            def __init__(self, d, step, chunk, lat):
                self.d, self.step, self.chunk, self.lat = d, step, chunk, lat
                self.first = isinstance(step, int) and step == 0

        def ctx_at(d, step):
            return At(d, step, NL + step if d == 0 else NL + 1 - step, False)

        def all_halves(eng, half_step, start, end):
            c = ctx_at
            lat = lambda d, n: At(d, n + 2, n if d == 0 else NL - 1 - n, True)
            start(c(0, 0))
            half_step(c(0, 0), None, c(1, 0))
            half_step(c(1, 0), c(0, 0), c(0, 1))
            half_step(c(0, 1), c(1, 0), c(1, 1))
            half_step(c(1, 1), c(0, 1), lat(0, 0))
            half_step(lat(0, 0), c(1, 1), lat(1, 0))
            regs = [eng.alloc_register(n) for n in ("up", "up1", "down", "down1")]
            for r, n in zip(regs, (0, 1, NL - 1, NL - 2)):
                eng.reg_mov(r, n)
            with eng.Fori(0, NL - 1) as i:
                up, up1, down, down1 = (eng.snap(r, min_val=0, max_val=NL - 1) for r in regs)
                half_step(At(1, i + 2, down, True), At(0, i + 2, up, True), At(0, i + 3, up1, True))
                half_step(At(0, i + 3, up1, True), At(1, i + 2, down, True), At(1, i + 3, down1, True))
                for r in regs[:2]:
                    eng.reg_add(r, r, 1)
                for r in regs[2:]:
                    eng.reg_sub(r, r, 1)
            half_step(lat(1, NL - 1), lat(0, NL - 1), None)
            end(lat(1, NL - 1))

        @block.sync
        def _(sp):
            sp.dma_start(U[:], io["tri"]).then_inc(tab_in, 16)
            sp.dma_start(lm[:], io["level_mask"]).then_inc(tab_in, 16)
            sp.dma_start(eye[:], io["block_eye"]).then_inc(tab_in, 16)
            sp.dma_start(selst[:], io["block_sel"]).then_inc(tab_in, 16)

            def load_kq(a):
                if not a.first:
                    sp.wait_ge(pe_done[a.d], PE_EV.done(a.step - 1, "kk3"))
                    sp.wait_ge(pool_done[a.d], POOL_EV.done(a.step - 1, "kg"))
                sp.dma_start(kq[a.d][:, :, 0, :], kT_v[a.chunk]).then_inc(kT_in[a.d], 16)
                if a.lat:
                    sp.dma_start(kq[a.d][:, :, 1, :], qT_v[a.chunk]).then_inc(qT_in[a.d], 16)

            def load_kv(a):
                if not a.first:
                    sp.wait_ge(pe_done[a.d], PE_EV.done(a.step - 1, "su3"))
                sp.dma_start(kk[a.d][:], k_v[a.chunk]).then_inc(k_in[a.d], 16)
                sp.dma_start(v[a.d][:], v_v[a.chunk]).then_inc(v_in[a.d], 16)

            def start(a):
                load_kq(a)
                load_kv(a)

            def half_step(a, other, nxt):
                if nxt is not None:
                    load_kq(nxt)
                    load_kv(nxt)

            all_halves(sp, half_step, start, lambda a: None)

        @block.tensor
        def _(pe):
            def decays(a):
                d = a.d
                pe.wait_ge(pool_done[d], POOL_EV.done(a.step, "gc"))
                if not a.first:
                    pe.wait_ge(dve_done[d], DVE_EV.done(a.step - 1, "su3"))
                for h in range(H):
                    last = pe.matmul(bank(d, h // 4)[:, (h % 4) * P:(h % 4 + 1) * P],
                                     gc[d][:, h:h + 1].broadcast_to([P, P]), U[:, d, :], start=True, stop=True)
                last.then_inc(pe_done[d], 1)
                pe.matmul(bank(d, 2)[:, 0:H], U[:, d, :], gc[d][:], start=True, stop=True).then_inc(pe_done[d], 1)

            def products(a):
                d = a.d
                pe.wait_ge(kT_in[d], a.step * 16 + 16)
                if a.lat:
                    pe.wait_ge(qT_in[d], a.step * 16 - 16)
                pe.wait_ge(act_done[d], ACT_EV.done(a.step, "el"))
                for p in range(4):
                    for h in (2 * p, 2 * p + 1):
                        out = head2(d, p)[:, h % 2, :]
                        if a.lat:
                            last = pe.matmul(out, kq[d][:, h, 0, :], kq[d][:, h, :, :].rearrange("p a c -> p (a c)"),
                                             start=True, stop=True)
                        else:
                            last = pe.matmul(out[:, 0:P], kq[d][:, h, 0, :], kq[d][:, h, 0, :], start=True, stop=True)
                    last.then_inc(pe_done[d], 1)

            def replicate(a, r):
                d = a.d
                if r == 0:
                    pe.wait_ge(dve_done[d], DVE_EV.done(a.step, "lo"))
                if r >= 4:
                    pe.wait_ge(dve_done[d], DVE_EV.done(a.step, f"a{2 * (r - 4) + 1}"))
                for k in (2 * r, 2 * r + 1):
                    if k == NB - 1:
                        continue
                    j = k if d == 0 else NB - 1 - k
                    out = head2(d, r % 4)[:, k % 2, :]
                    pe.matmul(out, sel[:, j, :], ahi[d][:].rearrange("p h i -> p (h i)"), start=True, stop=False)
                    last = pe.matmul(out, sel[:, j, :], alo[d][:].rearrange("p h i -> p (h i)"), start=False, stop=True)
                last.then_inc(pe_done[d], 1)

            def double(a, l):
                d, xc = a.d, a.d
                if l == 5:
                    pe.wait_ge(dve_done[d], DVE_EV.done(a.step, "tr"))
                    pe.wait_ge(act_done[d], ACT_EV.done(a.step, "tt"))
                else:
                    pe.wait_ge(dve_done[d], DVE_EV.done(a.step, "tt5"))
                for h in range(H):
                    last = pe.matmul(packed(bank(d, 0), l)[:, h], nA[d][:, h, :], half(T[d], l, xc)[:, h], start=True, stop=True)
                last.then_inc(pe_done[d], 1)
                pe.wait_ge(act_done[d], ACT_EV.done(a.step, f"x{l}"))
                if l == 5:
                    for h in range(H):
                        last = pe.matmul(packed(bank(d, 1), l)[:, h], TT[d][:, h, :], half(X[d], l, xc)[:, h], start=True, stop=True)
                    last.then_inc(pe_done[d], 1)
                for h in range(H):
                    last = pe.matmul(packed(bank(d, 2), l)[:, h], X[d][:, h, :], half(TT[d], l, 1 - xc)[:, h], start=True, stop=True)
                last.then_inc(pe_done[d], 1)

            def scan(a, n):
                d, p = a.d, n % 4
                heads = (2 * p, 2 * p + 1)
                out = lambda h: head2(d, p)[:, h % 2, :]
                if n < 4:
                    if n == 0:
                        pe.wait_ge(pool_done[d], POOL_EV.done(a.step, "kg"))
                        pe.wait_ge(dve_done[d], DVE_EV.done(a.step, "tt6"))
                        if a.first:
                            pe.wait_ge(init_rdy, 1)
                    for h in heads:
                        last = pe.matmul(out(h), EG[d][:, h, :], S[d][:, h, :], start=True, stop=True)
                elif n < 8:
                    pe.wait_ge(dve_done[d], DVE_EV.done(a.step, f"r{p}"))
                    for h in heads:
                        last = pe.matmul(out(h), TT[d][:, h, :], v[d][:, h, :], start=True, stop=True)
                elif n < 12:
                    if not a.lat:
                        if p == 3:
                            pe.wait_ge(pe_done[d], PE_EV.done(a.step, "vn3"))
                            pe.sem_inc(pe_done[d], 4)
                        return
                    pe.wait_ge(pool_done[d], POOL_EV.done(a.step, "qg"))
                    pe.wait_ge(act_done[d], ACT_EV.done(a.step, f"vn{p}"))
                    for h in heads:
                        pe.matmul(out(h), QG[d][:, h, :], S[d][:, h, :], start=True, stop=False)
                        last = pe.matmul(out(h), DT[d][:, h, :], v[d][:, h, :], start=False, stop=True)
                else:
                    pe.wait_ge(pool_done[d], POOL_EV.done(a.step, "kta"))
                    if a.lat:
                        pe.wait_ge(dve_done[d], DVE_EV.done(a.step, f"oa{p}"))
                    else:
                        pe.wait_ge(act_done[d], ACT_EV.done(a.step, f"vn{p}"))
                    for h in heads:
                        last = pe.matmul(out(h), kk[d][:, h, :], v[d][:, h, :], start=True, stop=True)
                last.then_inc(pe_done[d], 1)

            def start(a):
                pe.wait_ge(tab_in, 64)
                pe.wait_ge(sel_rdy, 1)
                decays(a)
                products(a)

            def half_step(a, other, nxt):
                for t in range(20):
                    if t < 16 and other is not None:
                        scan(other, t)
                    if t >= 4:
                        replicate(a, t - 4)
                if nxt is not None:
                    decays(nxt)
                double(a, 5)
                if nxt is not None:
                    products(nxt)
                double(a, 6)

            def end(a):
                for t in range(16):
                    scan(a, t)

            all_halves(pe, half_step, start, end)

        @block.scalar
        def _(act):
            def decays(a):
                d = a.d
                gb = psum[:, 2048 * d:2048 * d + 1024].rearrange("p (h c) -> p h c", h=H)
                act.wait_ge(dve_done[d], DVE_EV.done(a.step, "gm"))
                act.activation(EG[d][:], gb, ACT.Exp).then_inc(act_done[d], 1)
                act.activation(el[d][:].unsqueeze(2), gb[:, :, LAST[d]:LAST[d] + 1], ACT.Exp).then_inc(act_done[d], 1)
                act.activation(tl[d][:], td[d][:], ACT.Exp).then_inc(act_done[d], 1)
                act.wait_ge(pool_done[d], POOL_EV.done(a.step, "gms"))
                act.activation(DT[d][:], nA[d][:], ACT.Exp).then_inc(act_done[d], 1)

            def high_parts(a):
                d = a.d
                act.wait_ge(dve_done[d], DVE_EV.done(a.step, "na3"))
                for q in quad:
                    last = act.activation(ahi[d][q], nA[d][q, :, q], ACT.Copy)
                last.then_inc(act_done[d], 1)

            def to_TT(a):
                d = a.d
                act.wait_ge(dve_done[d], DVE_EV.done(a.step, f"a{NB - 2}"))
                act.wait_ge(pool_done[d], POOL_EV.done(a.step, "z"))
                for q in quad:
                    last = act.activation(TT[d][q, :, q], R[d][q], ACT.Copy)
                last.then_inc(act_done[d], 1)

            def x_out(a, l):
                d = a.d
                act.wait_ge(pe_done[d], PE_EV.done(a.step, f"x{l}"))
                act.activation(half(X[d], l, d), packed(bank(d, 0), l), ACT.Copy).then_inc(act_done[d], 1)

            def v_new(a, p):
                d = a.d
                act.wait_ge(pe_done[d], PE_EV.done(a.step, f"vn{p}"))
                for h in (2 * p, 2 * p + 1):
                    last = act.activation(v[d][:, h, :], head2(d, p)[:, h % 2, :], ACT.Copy, scale=bc[d][:, h:h + 1])
                last.then_inc(act_done[d], 1)

            def half_step(a, other, nxt):
                high_parts(a)
                if other is not None:
                    for p in range(4):
                        v_new(other, p)
                to_TT(a)
                if nxt is not None:
                    decays(nxt)
                x_out(a, 5)
                x_out(a, 6)

            def end(a):
                for p in range(4):
                    v_new(a, p)

            act.wait_ge(tab_in, 64)
            act.activation(sel[:], selst[:], ACT.Copy).then_inc(sel_rdy, 1)
            act.wait_ge(init_rdy, 1)
            all_halves(act, half_step, decays, end)

        @block.vector
        def _(dve):
            for d in (0, 1):
                dve.memset(X[d][:], 0.0)
                dve.memset(S[d][:], 0.0)
            dve.wait_ge(sel_rdy, 1)
            dve.memset(o[:], 0.0).then_inc(init_rdy, 1)
            dve.wait_ge(init_rdy, 1)
            dve.wait_ge(nm_rdy, 1)

            def decays(a):
                d, sig = a.d, dve_done[a.d]
                gb = psum[:, 2048 * d:2048 * d + 1024].rearrange("p (h c) -> p h c", h=H)
                dve.wait_ge(pe_done[d], PE_EV.done(a.step, "gp"))
                dve.tensor_copy(gps[d][:], bank(d, 2)[:, 0:H]).then_inc(sig, 1)
                dve.wait_ge(sig, DVE_EV.done(a.step, "gps"))
                dve.tensor_tensor(td[d][:], gb[:, :, LAST[d]], gps[d][:], ALU.subtract).then_inc(sig, 1)
                dve.tensor_tensor(nA[d][:], gb, NM[:, d, :].unsqueeze(1).broadcast_to([P, H, P]), ALU.add).then_inc(sig, 1)

            def products(a):
                d, sig = a.d, dve_done[a.d]
                dve.wait_ge(pool_done[d], POOL_EV.done(a.step, "db"))
                for p in range(4):
                    dve.wait_ge(pe_done[d], PE_EV.done(a.step, f"kk{p}"))
                    hs = slice(2 * p, 2 * p + 2)
                    dve.tensor_tensor(nA[d][:, hs, :], head2(d, p)[:, :, 0:P], nA[d][:, hs, :], ALU.mult).then_inc(sig, 1)
                    if a.lat:
                        last = dve.tensor_tensor(DT[d][:, hs, :], head2(d, p)[:, :, P:2 * P], DT[d][:, hs, :], ALU.mult)
                if a.lat:
                    last.then_inc(sig, 1)
                else:
                    dve.wait_ge(sig, DVE_EV.done(a.step, "na3"))
                    dve.sem_inc(sig, 1)

            def low_parts(a):
                d = a.d
                dve.wait_ge(act_done[d], ACT_EV.done(a.step, "hi"))
                for q in quad:
                    last = dve.tensor_tensor(alo[d][q], nA[d][q, :, q], ahi[d][q].bitcast(F32), ALU.subtract)
                last.then_inc(dve_done[d], 1)

            def substitute(a, r):
                d, sig = a.d, dve_done[a.d]
                dve.wait_ge(pe_done[d], PE_EV.done(a.step, f"rp{r}"))
                for k in (2 * r, 2 * r + 1):
                    if k == NB - 1:
                        continue
                    if k:
                        dve.wait_ge(sig, DVE_EV.done(a.step, f"a{k - 1}"))
                    else:
                        dve.wait_ge(pool_done[d], POOL_EV.done(a.step, "z"))
                    j = k if d == 0 else NB - 1 - k
                    i = slice(j + 1, NB) if d == 0 else slice(0, j)
                    n = NB - 1 - k
                    row = head2(d, r % 4)[:, k % 2, :].rearrange("p (h i) -> p h i", h=H)[:, :, i]
                    dve.tensor_tensor(tmp[d][:, :, 0:n], row, R[d][:, :, j:j + 1].broadcast_to([P, H, n]), ALU.mult).then_inc(sig, 1)
                    dve.wait_ge(sig, DVE_EV.done(a.step, f"m{k}"))
                    dve.tensor_tensor(R[d][:, :, i], R[d][:, :, i], tmp[d][:, :, 0:n], ALU.add).then_inc(sig, 1)

            def to_T(a):
                d, sig = a.d, dve_done[a.d]
                dve.wait_ge(sig, DVE_EV.done(a.step, f"a{NB - 2}"))
                for q in quad:
                    last = dve.transpose(T[d][q, :, q], R[d][q])
                last.then_inc(sig, 1)

            def merge(a, l):
                d, sig = a.d, dve_done[a.d]
                xc, tc = d, 1 - d
                if l == 5:
                    dve.wait_ge(pe_done[d], PE_EV.done(a.step, "d5"))
                    dve.sem_inc(merges, 1)
                    dve.copy_predicated(half(T[d], l, xc), mask(l, 1 - d), packed(bank(d, 1), l)).then_inc(sig, 1)
                dve.wait_ge(pe_done[d], PE_EV.done(a.step, f"t{l}"))
                dve.sem_inc(merges, 1)
                dve.copy_predicated(half(TT[d], l, tc), mask(l, d), packed(bank(d, 2), l)).then_inc(sig, 1)

            def scan(a, n):
                d, p, sig = a.d, n % 4, dve_done[a.d]
                hs = slice(2 * p, 2 * p + 2)
                if n < 4:
                    if n == 0:
                        dve.wait_ge(v_in[d], a.step * 16 + 16)
                    dve.wait_ge(pe_done[d], PE_EV.done(a.step, f"ks{p}"))
                    dve.tensor_tensor(v[d][:, hs, :], v[d][:, hs, :], head2(d, p), ALU.subtract).then_inc(sig, 1)
                elif 8 <= n < 12:
                    if a.lat:
                        dve.wait_ge(pe_done[d], PE_EV.done(a.step, f"o{p}"))
                        oc = o[:, bass.ds(a.chunk, 1), 512 * p:512 * p + 512].rearrange("p a c -> p (a c)")
                        dve.tensor_tensor(oc, oc, bank(d, p), ALU.add).then_inc(sig, 1)
                    elif p == 3:
                        dve.wait_ge(sig, DVE_EV.done(a.step, "r3"))
                        dve.sem_inc(sig, 4)
                elif n >= 12:
                    dve.wait_ge(pe_done[d], PE_EV.done(a.step, f"su{p}"))
                    if n == 12:
                        dve.wait_ge(act_done[d], ACT_EV.done(a.step, "el"))
                    for h in (2 * p, 2 * p + 1):
                        last = dve.scalar_tensor_tensor(S[d][:, h, :], S[d][:, h, :], el[d][:, h:h + 1],
                                                        head2(d, p)[:, h % 2, :], ALU.mult, ALU.add)
                    last.then_inc(sig, 1)

            def start(a):
                decays(a)
                products(a)

            def half_step(a, other, nxt):
                for t in range(20):
                    if t < 16 and other is not None:
                        scan(other, t)
                    if t == 3:
                        low_parts(a)
                    if t >= 4:
                        substitute(a, t - 4)
                to_T(a)
                if nxt is not None:
                    decays(nxt)
                merge(a, 5)
                if nxt is not None:
                    products(nxt)
                merge(a, 6)

            def end(a):
                for t in range(16):
                    scan(a, t)

            all_halves(dve, half_step, start, end)

        @block.gpsimd
        def _(pool):
            pool.wait_ge(tab_in, 64)
            pool.tensor_scalar(NM[:], U[:], -1.0, -BIG, ALU.add, ALU.mult).then_inc(nm_rdy, 1)

            def chunk_cols(a, dst, src):
                return pool.tensor_copy(dst[a.d][:], src[:, bass.ds(a.chunk, 1), 8 * a.d:8 * a.d + 8].rearrange("p a h -> p (a h)"))

            def decays(a):
                d, sig = a.d, pool_done[a.d]
                if not a.first:
                    pool.wait_ge(pe_done[d], PE_EV.done(a.step - 1, "gp"))
                chunk_cols(a, gc, core.gtok)
                chunk_cols(a, nb, core.nbeta).then_inc(sig, 1)
                pool.wait_ge(dve_done[d], DVE_EV.done(a.step, "gm"))
                pool.tensor_tensor(nA[d][:], nA[d][:], b3(gps[d]), ALU.subtract).then_inc(sig, 1)
                pool.wait_ge(act_done[d], ACT_EV.done(a.step, "dt"))
                pool.tensor_tensor(nA[d][:], DT[d][:], b3(nb[d]), ALU.mult).then_inc(sig, 1)

            def half_step(a, other, nxt):
                d, sig = a.d, pool_done[a.d]
                if not a.first:
                    pool.wait_ge(pe_done[d], PE_EV.done(a.step - 1, "su3"))
                chunk_cols(a, bc, core.beta).then_inc(sig, 1)
                pool.memset(T[d][:], 0.0)
                pool.memset(TT[d][:], 0.0)
                pool.tensor_copy(R[d][:], eye[:].unsqueeze(1).broadcast_to([P, H, NB])).then_inc(sig, 1)
                pool.wait_ge(kT_in[d], a.step * 16 + 16)
                if a.lat:
                    pool.wait_ge(qT_in[d], a.step * 16 - 16)
                    pool.tensor_tensor(QG[d][:], kq[d][:, :, 1, :], EG[d][:], ALU.mult).then_inc(sig, 1)
                    pool.wait_ge(sig, POOL_EV.done(a.step, "qg"))
                else:
                    pool.wait_ge(sig, POOL_EV.done(a.step, "z"))
                    pool.sem_inc(sig, 1)
                pool.tensor_tensor(EG[d][:], kq[d][:, :, 0, :], EG[d][:], ALU.mult).then_inc(sig, 1)
                pool.wait_ge(k_in[d], a.step * 16 + 16)
                pool.tensor_tensor(kk[d][:], kk[d][:], b3(tl[d]), ALU.mult).then_inc(sig, 1)
                if nxt is not None:
                    decays(nxt)

            all_halves(pool, half_step, decays, lambda a: None)


def gate_phase(core, io):
    nc, psum, ident = core.nc, core.psum, core.ident
    o = core.at("o", [P, NL, FW], 0)
    zt = [core.at(f"zt{s}", [P, LAT], 64 + 4 * s) for s in range(2)]
    y = [core.at(f"y_g{s}", [P, LAT], 72 + 4 * s) for s in range(2)]
    sq = core.at("sq_g", [P, NL, FW], 80)
    st_ = core.at("st_g", [P, 3, NL * H], 144)
    cols = core.cols
    z_v = core.z_d.rearrange("(n p) t -> n p t", p=P)
    y_v = core.y2_d.rearrange("(n p) t -> n p t", p=P)
    with ExitStack() as st:
        sem = sems(nc, st)
        z_in = [sem("zt_in0"), sem("zt_in1")]
        stored = [sem("yg_stored0"), sem("yg_stored1")]
        sq_rdy, red, std, rstd, on = sem("sqg_rdy"), sem("red_g"), sem("std_g"), sem("rstd_g"), sem("on_rdy")
        t_mm, y_rdy = sem("tg_mm"), sem("yg_rdy")
        block = st.enter_context(nc.Block())
        NCT = 16

        @block.sync
        def _(sp):
            for s in range(2):
                sp.dma_start(zt[s][:], z_v[s]).then_inc(z_in[s], 16)
                sp.sem_inc(stored[s], 16)

            def turn(n, s, more):
                sp.wait_ge(y_rdy, n + 3)
                sp.dma_start(y_v[n], y[s][:]).then_inc(stored[s], 16)
                if more:
                    sp.dma_start(zt[s][:], z_v[n + 2]).then_inc(z_in[s], 16)

            with sp.Fori(0, NCT // 2 - 1) as i:
                for s in range(2):
                    turn(i * 2 + s, s, True)
            for s in range(2):
                turn(NCT - 2 + s, s, False)
            for s in range(2):
                sp.wait_ge(stored[s], 16 + 16 * NCT // 2)

        @block.scalar
        def _(act):
            for n in range(NL):
                act.activation(sq[:, n, :], o[:, n, :], ACT.Square).then_inc(sq_rdy, 1)
            act.wait_ge(red, 2)
            act.activation(st_[:, 1, :], st_[:, 0, :], ACT.Sqrt).then_inc(std, 1)

        @block.vector
        def _(dve):
            dve.sem_inc(y_rdy, 2)
            for n in range(NL):
                dve.wait_ge(sq_rdy, n + 1)
                last = dve.reduce_sum(st_[:, 2, n * H:(n + 1) * H], sq[:, n, :].rearrange("p (h c) -> p h c", h=H), AXX)
            last.then_inc(red, 1)
            dve.wait_ge(red, 1)
            dve.tensor_scalar(st_[:, 0, :], st_[:, 2, :], 1.0 / DV, EPS, ALU.mult, ALU.add).then_inc(red, 1)
            dve.wait_ge(std, 1)
            dve.reciprocal(st_[:, 2, :], st_[:, 1, :]).then_inc(rstd, 1)
            dve.wait_ge(rstd, 1)
            for n in range(NL):
                on_ = o[:, n, :].rearrange("p (h c) -> p h c", h=H)
                r = st_[:, 2, n * H:(n + 1) * H].unsqueeze(2).broadcast_to([P, H, DV])
                dve.tensor_tensor(on_, on_, r, ALU.mult).then_inc(on, 1)
            with dve.Fori(0, NCT // 2) as i:
                for s in range(2):
                    n = i * 2 + s
                    dve.wait_ge(t_mm, n + 1)
                    dve.wait_ge(z_in[s], i * 16 + 16)
                    dve.wait_ge(stored[s], i * 16 + 16)
                    dve.scalar_tensor_tensor(y[s][:], psum[:, 1024 * s:1024 * s + 1024], cols[:, COL_DN + s:COL_DN + s + 1],
                                             zt[s][:], ALU.mult, ALU.mult).then_inc(y_rdy, 1)

        @block.tensor
        def _(pe):
            pe.wait_ge(on, NL)
            for n in range(NCT):
                pe.wait_ge(y_rdy, n + 1)
                for t in range(NL):
                    o_ = 1024 * (n % 2) + t * P
                    last = pe.transpose(psum[:, o_:o_ + P], o[:, t, n * P:(n + 1) * P], ident[:])
                last.then_inc(t_mm, 1)


def tables():
    t = {}
    k = np.arange(HL)
    f = lambda L: 2 * np.pi / L * np.outer(np.arange(L // 2), np.arange(L // 2))
    lat = [m.reshape(4, P, HL).transpose(1, 0, 2).reshape(P, -1) for m in (np.cos(f(LAT)), np.sin(f(LAT)))]
    t["dft_tab"] = np.concatenate([m / LAT ** 0.5 for m in lat] + [np.cos(f(CTX)) / CTX ** 0.5, np.sin(f(CTX)) / CTX ** 0.5], 1)
    alt = 1.0 - 2.0 * (np.arange(P) % 2)
    t["alt_col"] = np.stack([alt / LAT ** 0.5, alt / CTX ** 0.5], 1)
    t["alt_row"] = np.concatenate([np.tile(alt, 4) / LAT ** 0.5, alt / CTX ** 0.5])[None]
    a = 2 * np.pi / FD * np.outer(np.arange(FD), np.arange(FD))
    t["ch_dft"] = np.stack([m.reshape(2, P, FD).transpose(1, 0, 2) for m in (np.cos(a) / FD ** 0.5, np.sin(a) / FD ** 0.5)], 1)
    t["ident"] = np.eye(P)
    i = np.arange(P)
    t["tri"] = np.stack([i[:, None] <= i[None], i[:, None] >= i[None]], 1)
    t = {n: np.ascontiguousarray(v, np.float32) for n, v in t.items()}
    t["block_eye"] = np.ascontiguousarray(np.eye(NB, dtype=np.float32)[i % NB])
    j = np.arange(NB)
    t["block_sel"] = np.ascontiguousarray((i[:, None, None] == (i[None, None] // NB * NB + j[None, :, None])), np.float32)
    lm = np.zeros((P, 2, 2, 64), np.int32)
    for n, l in enumerate(TOP):
        s = 1 << l
        c = np.arange(64)
        for half in range(2):
            lm[:, n, half] = (i[:, None] // (2 * s) == c[None] // s) & ((i[:, None] % (2 * s)) // s == half)
    t["level_mask"] = lm
    return t


def program(nc, io):
    core = Core(nc)
    input_phase(core, io)
    fourier_phase(core, io)
    output_phase(core, io, 0)
    project_phase(core, io)
    delta_phase(core, io)
    gate_phase(core, io)
    output_phase(core, io, 1)


INPUTS = ("x", "c", "ctx", "c_ctx", "mod_w", "mod_b", "norm_g", "final_g", "fn_w_in", "fn_w_grp", "fn_w_out",
          "dn_w_in", "dn_conv", "dn_a_log", "dn_dt_bias", "dn_norm_g", "dn_w_out")


def kernel(**inputs):
    import concourse.bacc as _bacc
    from concourse.bass_utils import run_bass_kernel_spmd as _run

    nc = _bacc.Bacc("TRN2", target_bir_lowering=False, num_devices=1)
    arrays = {n: np.ascontiguousarray(inputs[n]) for n in INPUTS}
    x, ctx = arrays["x"][0], arrays["ctx"][0]
    arrays["x_mirror"] = np.ascontiguousarray(np.concatenate([x[HL:HL + 1], x[:HL:-1]]))
    arrays["ctx_mirror"] = np.ascontiguousarray(np.concatenate([ctx[HC:HC + 1], ctx[:HC:-1]]))
    arrays.update(tables())
    io = {n: nc.dram_tensor(f"in_{n}", a.shape, mybir.dt.from_np(a.dtype), kind="ExternalInput").ap() for n, a in arrays.items()}
    io["out"] = nc.dram_tensor("out", (1, LAT, D), F32, kind="ExternalOutput").ap()
    program(nc, io)
    r = _run(nc, [{f"in_{n}": a for n, a in arrays.items()}], core_ids=[0])
    return r.results[0]["out"]
```

```python
from contextlib import ExitStack

import numpy as np
import concourse.bass as bass
from concourse import mybir

F32 = mybir.dt.float32
I32 = mybir.dt.int32
F32R = mybir.dt.float32r
ACT = mybir.ActivationFunctionType
ALU = mybir.AluOpType
AXX = mybir.AxisListType.X

P = 128
D = 1024
KT = D // P
LAT, CTX = 1024, 256
TOK = LAT + CTX
NL, NC_ = LAT // P, CTX // P
NT = NL + NC_
HL, HC = LAT // 2, CTX // 2
GW = 64
GR = LAT // GW
EPS = 1e-6
FG, FD = 8, 256
FW = FG * FD
H, DK, DV = 8, 128, 256
BIG = -1.0e30
KB = 1024


class Core:

    def __init__(self, nc):
        self.nc = nc
        self.placed = {}
        self.early_sems = []
        sb = nc.alloc_sbuf_tensor
        self.ident = sb("ident", [P, P], F32)
        self.cols = sb("cols", [P, 82], F32)
        self.modT = sb("modT", [P, 48, 2], F32)
        self.acoef = sb("acoef", [P, 2, KT, 2], F32)
        self.scond = sb("scond", [P, KT, 2], F32)
        self.gtok = sb("gtok", [P, NT, 16], F32)
        self.beta = sb("beta", [P, NT, 16], F32)
        self.nbeta = sb("nbeta", [P, NT, 16], F32)
        self.base = (nc.sbuf_base + 63) // 64 * 64
        self.psum = nc.alloc_psum_tensor("psum", [P, 8 * 512], F32)
        dr = lambda n, s: nc.dram_tensor(n, s, F32, kind="Internal").ap()
        self.y_d = dr("y_scr", (FW, TOK))
        self.zf_d = dr("zf_scr", (FW, TOK))
        self.h_d = dr("h_scr", (LAT, D))
        self.z_d = dr("z_scr", (FW, LAT))
        self.qT_d = dr("qT_scr", (H, P, LAT))
        self.kT_d = dr("kT_scr", (H, P, TOK))
        self.k_d = dr("k_scr", (TOK, D))
        self.v_d = dr("v_scr", (TOK, FW))

    def at(self, name, shape, kb, dt=F32):
        if name not in self.placed:
            self.placed[name] = self.nc.alloc_sbuf_tensor_at(name, shape, dt, offset=self.base + int(kb * KB))
        return self.placed[name]


def split_parts(eng, hi, lo, x, signal, value):
    eng.tensor_copy(hi, x).then_inc(signal, 1)
    eng.wait_ge(signal, value)
    return eng.tensor_tensor(lo, x, hi.bitcast(F32), ALU.subtract)


def product3(pe, out, w, x, start, stop):
    pe.matmul(out, w[0], x[0], start=start, stop=False)
    pe.matmul(out, w[0], x[1], start=False, stop=False)
    return pe.matmul(out, w[1], x[0], start=False, stop=stop)


def sems(nc, stack, kept=None):
    def sem(name):
        handle = stack.enter_context(nc.semaphore(name))
        if kept is not None:
            kept.append(handle)
        return handle
    return sem


COL_MODB, COL_G, COL_C, COL_CC, COL_DN = 0, 48, 64, 72, 80


def norm_coefs(core, dve, layer, step):
    a = core.acoef[:, layer]
    if step == 0:
        return dve.tensor_scalar(a, core.modT[:, 24 * layer + 8:24 * layer + 16, :], 1.0, None, ALU.add)
    g = core.cols[:, COL_G + 8 * layer:COL_G + 8 * layer + 8].unsqueeze(2).broadcast_to([P, KT, 2])
    return dve.tensor_tensor(a, a, g, ALU.mult)


def input_phase(core, io):
    nc = core.nc
    pqT = core.at("pqT", [P, KT, TOK], 0)
    nT = core.at("nT", [P, KT, TOK], 40)
    nTh = core.at("nT_hi", [P, KT, TOK], 120, F32R)
    nTl = core.at("nT_lo", [P, KT, TOK], 40, F32R)
    xn = core.at("xn", [P, NT, D], 80)
    xm = core.at("xm", [P, 5, D], 120)
    ev = core.at("ev", [P, 5, D], 140)
    mw = [core.at(f"mw{s}", [P, KT, 256], 160 + 8 * s) for s in range(2)]
    dft = core.at("dft", [P, 2 * 4 * HL + 2 * HC], 176)
    b0 = core.at("b0", [64, D], 193)
    junk = core.at("junk", [P, D], 0)
    rows = core.at("rows", [82, P], 40)
    scond = core.scond
    ss = core.at("ss", [P, 16], 199.25)
    altc = core.at("altc", [P, 2], 199.5)
    shs = core.at("shs", [P, KT, 2], 199.75)
    altr = core.at("altr", [64, HL], 197)
    cosL = dft[:, 0:4 * HL].rearrange("p (t k) -> p t k", t=4)
    sinL = dft[:, 4 * HL:8 * HL].rearrange("p (t k) -> p t k", t=4)
    cosC = dft[:, 8 * HL:8 * HL + HC]
    sinC = dft[:, 8 * HL + HC:8 * HL + 2 * HC]
    psum, cols, modT = core.psum, core.cols, core.modT
    NCH = 12
    with ExitStack() as st:
        sem = sems(nc, st, core.early_sems)
        x_in = [sem(f"x_in{n}") for n in range(5)]
        rows_in, tab_in, id_in = sem("rows_in"), sem("tab_in"), sem("id_in")
        mw_in = [sem("mw_in0"), sem("mw_in1")]
        mw_used = sem("mw_used")
        rowsT, cols_rdy, cond_rdy = sem("rowsT"), sem("cols_rdy"), sem("cond_rdy")
        ss_rdy, var_rdy, std_rdy = sem("ss_rdy"), sem("var_rdy"), sem("std_rdy")
        vec = sem("vec_chain")
        xhat_rdy, fold_rdy, odd_rdy, mod_free = sem("xhat_rdy"), sem("fold_rdy"), sem("odd_rdy"), sem("mod_free")
        coef_rdy = sem("coef_rdy")
        dft_mm, dft_free_a, dft_free_v = sem("dft_mm"), sem("dft_free_a"), sem("dft_free_v")
        tr_mm, tr_free, nT_hi = sem("tr_mm"), sem("tr_free"), sem("nT_hi_rdy")
        block = st.enter_context(nc.Block())

        @block.sync
        def _(sp):
            sp.dma_start(core.ident[:], io["ident"]).then_inc(id_in, 16)
            r = lambda a: a.rearrange("(n p) -> n p", p=P)
            for lo, src in ((COL_MODB, io["mod_b"].rearrange("l (n p) -> (l n) p", p=P)),
                            (COL_G, io["norm_g"].rearrange("l (n p) -> (l n) p", p=P)),
                            (COL_C, io["c"].rearrange("l (n p) -> (l n) p", p=P)),
                            (COL_CC, r(io["c_ctx"])),
                            (COL_DN, io["dn_norm_g"].rearrange("l (n p) -> (l n) p", p=P))):
                sp.dma_start(rows[lo:lo + src.shape[0], :], src).then_inc(rows_in, 16)
            xv = io["x"][0].rearrange("(n p) d -> p n d", p=P)
            sp.dma_start(xn[:, 0:4, :], xv[:, 0:4, :]).then_inc(x_in[0], 16)
            sp.dma_start(xn[:, 4:8, :], xv[:, 4:8, :]).then_inc(x_in[1], 16)
            sp.dma_start(xn[:, 8:10, :], io["ctx"][0].rearrange("(n p) d -> p n d", p=P)).then_inc(x_in[2], 16)
            sp.dma_start(xm[:, 0:4, :], io["x_mirror"].rearrange("(n p) d -> p n d", p=P)).then_inc(x_in[3], 16)
            sp.dma_start(xm[:, 4, :], io["ctx_mirror"]).then_inc(x_in[4], 16)
            mv = io["mod_w"][0].rearrange("(k p) (n c) -> n p k c", p=P, c=256)
            for s in range(2):
                sp.dma_start(mw[s][:], mv[s]).then_inc(mw_in[s], 16)
            sp.dma_start(dft[:], io["dft_tab"]).then_inc(tab_in, 16)
            sp.dma_start(altc[:], io["alt_col"]).then_inc(tab_in, 16)
            sp.dma_start(altr[0:1, :], io["alt_row"][:, 0:HL]).then_inc(tab_in, 16)
            sp.dma_start(altr[32:33, 0:HC], io["alt_row"][:, HL:HL + HC]).then_inc(tab_in, 16)
            with sp.Fori(0, NCH // 2 - 1) as i:
                for s in range(2):
                    sp.wait_ge(mw_used, i * 2 + (s + 1))
                    sp.dma_start(mw[s][:], mv[i * 2 + (s + 2)]).then_inc(mw_in[s], 16)

        @block.scalar
        def _(act):
            for n in range(15):
                src = xn[:, n, :] if n < NT else xm[:, n - NT, :]
                act.wait_ge(x_in[0 if n < 4 else 1 if n < 8 else 2 if n < 10 else 3 if n < 14 else 4], 16)
                if n:
                    act.wait_ge(ss_rdy, n)
                act.activation(junk[:], src, ACT.Square, accum_out=ss[:, n:n + 1]).then_inc(ss_rdy, 1)
            act.wait_ge(var_rdy, 1)
            act.activation(ss[:, 0:15], ss[:, 0:15], ACT.Sqrt).then_inc(std_rdy, 1)
            act.wait_ge(cols_rdy, 1)
            for c in range(2):
                act.activation(scond[:, :, c], cols[:, COL_C + 8 * c:COL_C + 8 * c + 8], ACT.Silu).then_inc(cond_rdy, 1)
            act.wait_ge(coef_rdy, 3)
            for k in range(KT):
                b = 3 * (k % 2) * 512
                act.wait_ge(dft_mm, 2 * k + 1)
                a = core.acoef[:, 0, k, 0:1]
                act.activation(pqT[:, k, 1:HL], psum[:, b + 1:b + HL], ACT.Identity, scale=a)
                act.activation(pqT[:, k, 0:1], psum[:, b:b + 1], ACT.Identity,
                               scale=a, bias=shs[:, k, 0:1]).then_inc(dft_free_a, 1)
                for j, (t0, nt) in enumerate(((0, 4), (4, 4), (8, 2))):
                    g = 3 * k + j
                    bb = (6 + g % 2) * 512
                    c = int(j == 2)
                    act.wait_ge(tr_mm, g + 1)
                    act.activation(nT[:, k, t0 * P:(t0 + nt) * P], psum[:, bb:bb + nt * P], ACT.Identity,
                                   scale=core.acoef[:, 0, k, c:c + 1], bias=modT[:, k, c:c + 1]).then_inc(tr_free, 1)

            act.wait_ge(tr_mm, 3 * KT)
            for k in range(KT):
                act.wait_ge(tr_free, 3 * (k + 1))
                act.activation(nTh[:, k, :], nT[:, k, :], ACT.Copy).then_inc(nT_hi, 1)

        @block.vector
        def _(dve):
            chain = [0]

            def link(ins):
                chain[0] += 1
                ins.then_inc(vec, 1)
                dve.wait_ge(vec, chain[0])

            dve.sem_inc(mod_free, 2)
            dve.wait_ge(rowsT, 1)
            dve.tensor_copy(cols[:], psum[:, 0:82]).then_inc(cols_rdy, 1)
            dve.wait_ge(ss_rdy, 15)
            dve.tensor_scalar(ss[:, 0:15], ss[:, 0:15], 1.0 / D, EPS, ALU.mult, ALU.add).then_inc(var_rdy, 1)
            dve.wait_ge(std_rdy, 1)
            link(dve.reciprocal(ss[:, 0:15], ss[:, 0:15]))
            for n in range(15):
                x = xn[:, n, :] if n < NT else xm[:, n - NT, :]
                dve.tensor_scalar(x, x, ss[:, n:n + 1], None, ALU.mult).then_inc(xhat_rdy, 1)
            dve.wait_ge(xhat_rdy, 15)
            link(dve.tensor_tensor(ev[:, 0:4, :], xn[:, 0:4, :], xm[:, 0:4, :], ALU.add))
            link(dve.tensor_tensor(ev[:, 4, :], xn[:, 8, :], xm[:, 4, :], ALU.add))
            dve.tensor_copy(ev[0:1, 0, :], xn[0:1, 0, :])
            dve.tensor_copy(ev[0:1, 4, :], xn[0:1, 8, :])
            dve.tensor_copy(b0[0:1, :], xm[0:1, 0, :])
            dve.tensor_copy(b0[32:33, :], xm[0:1, 4, :]).then_inc(fold_rdy, 1)

            def mod_chunks(c0, n):
                with dve.Fori(0, n // 2) as i:
                    for s in range(2):
                        dve.wait_ge(mw_used, i * 2 + (c0 + s + 1))
                        blk = i * 4 + 2 * (c0 + s)
                        dve.tensor_tensor(modT[:, bass.ds(blk, 2), :],
                                          psum[:, 3072 + 512 * s:3072 + 512 * s + 4].rearrange("p (a b) -> p a b", a=2),
                                          cols[:, bass.ds(blk, 2)].unsqueeze(2).broadcast_to([P, 2, 2]),
                                          ALU.add).then_inc(mod_free, 1)

            dve.wait_ge(cols_rdy, 1)
            mod_chunks(0, 8)
            dve.wait_ge(mod_free, 2 + 8)
            link(norm_coefs(core, dve, 0, 0))
            norm_coefs(core, dve, 0, 1).then_inc(coef_rdy, 1)
            dve.tensor_scalar(shs[:, :, 0], modT[:, 0:8, 0], float(LAT) ** 0.5, None, ALU.mult).then_inc(coef_rdy, 1)
            dve.tensor_scalar(shs[:, :, 1], modT[:, 0:8, 1], float(CTX) ** 0.5, None, ALU.mult).then_inc(coef_rdy, 1)
            dve.wait_ge(coef_rdy, 3)
            for k in range(KT):
                b = 3 * (k % 2) * 512
                dve.wait_ge(dft_mm, 2 * k + 2)
                dve.tensor_scalar(pqT[:, k, HL:2 * HL], psum[:, b + 512:b + 1024],
                                  core.acoef[:, 0, k, 0:1], None, ALU.mult)
                dve.tensor_scalar(pqT[:, k, LAT + 1:TOK], psum[:, b + 1025:b + 1024 + 2 * HC],
                                  core.acoef[:, 0, k, 1:2], None, ALU.mult)
                dve.tensor_scalar(pqT[:, k, LAT:LAT + 1], psum[:, b + 1024:b + 1025],
                                  core.acoef[:, 0, k, 1:2], shs[:, k, 1:2], ALU.mult, ALU.add).then_inc(dft_free_v, 1)
            for k in range(KT):
                dve.wait_ge(nT_hi, k + 1)
                dve.tensor_tensor(nTl[:, k, :], nT[:, k, :], nTh[:, k, :].bitcast(F32), ALU.subtract)
            mod_chunks(8, 4)

        @block.gpsimd
        def _(pool):
            pool.wait_ge(fold_rdy, 1)
            pool.tensor_tensor(xm[:, 0:4, :], xn[:, 0:4, :], xm[:, 0:4, :], ALU.subtract).then_inc(odd_rdy, 1)
            pool.tensor_tensor(xm[:, 4, :], xn[:, 8, :], xm[:, 4, :], ALU.subtract).then_inc(odd_rdy, 1)

        @block.tensor
        def _(pe):
            pe.wait_ge(id_in, 16)
            pe.wait_ge(rows_in, 80)
            pe.transpose(psum[:, 0:82], rows[:], core.ident[0:82, 0:82]).then_inc(rowsT, 1)

            def mod_chunks(c0, n):
                with pe.Fori(0, n // 2) as i:
                    for s in range(2):
                        pe.wait_ge(mw_in[s], i * 16 + (16 + 8 * c0))
                        pe.wait_ge(mod_free, i * 2 + (c0 + s + 1))
                        for b in range(2):
                            for k in range(KT):
                                last = pe.matmul(psum[:, 3072 + 512 * s + 2 * b:3072 + 512 * s + 2 * b + 2],
                                                 mw[s][:, k, b * P:(b + 1) * P], scond[:, k, :],
                                                 start=(k == 0), stop=(k == KT - 1))
                        last.then_inc(mw_used, 1)

            pe.wait_ge(cond_rdy, 2)
            mod_chunks(0, 8)
            pe.wait_ge(tab_in, 64)
            pe.wait_ge(fold_rdy, 1)
            pe.wait_ge(odd_rdy, 2)
            pe.wait_ge(mod_free, 2 + 8)
            for k in range(KT):
                b = 3 * (k % 2) * 512
                ch = slice(k * P, (k + 1) * P)
                if k >= 2:
                    pe.wait_ge(dft_free_a, k - 1)
                    pe.wait_ge(dft_free_v, k - 1)
                for t in range(4):
                    pe.matmul(psum[:, b:b + HL], ev[:, t, ch], cosL[:, t, :], start=(t == 0), stop=False)
                pe.matmul(psum[:, b:b + HL], b0[0:1, ch], altr[0:1, 0:HL], start=False, stop=True).then_inc(dft_mm, 1)
                pe.matmul(psum[:, b + 1024:b + 1024 + HC], ev[:, 4, ch], cosC, start=True, stop=False)
                pe.matmul(psum[:, b + 1024:b + 1024 + HC], b0[32:33, ch], altr[32:33, 0:HC],
                          start=False, stop=True)
                for t in range(4):
                    pe.matmul(psum[:, b + 512:b + 1024], xm[:, t, ch], sinL[:, t, :], start=(t == 0), stop=False,
                              skip_group_check=True)
                for t in range(4):
                    pe.matmul(psum[:, b + 512:b + 513], ev[:, t, ch], altc[:, 0:1], start=False, stop=False,
                              skip_group_check=True)
                pe.matmul(psum[:, b + 512:b + 513], b0[0:1, ch], altr[0:1, 0:1], start=False, stop=True,
                          skip_group_check=True)
                o = b + 1024 + HC
                pe.matmul(psum[:, o:o + HC], xm[:, 4, ch], sinC, start=True, stop=False, skip_group_check=True)
                pe.matmul(psum[:, o:o + 1], ev[:, 4, ch], altc[:, 1:2], start=False, stop=False, skip_group_check=True)
                pe.matmul(psum[:, o:o + 1], b0[32:33, ch], altr[32:33, 0:1], start=False, stop=True,
                          skip_group_check=True).then_inc(dft_mm, 1)
                for j, (t0, nt) in enumerate(((0, 4), (4, 4), (8, 2))):
                    g = 3 * k + j
                    bb = (6 + g % 2) * 512
                    if g >= 2:
                        pe.wait_ge(tr_free, g - 1)
                    for t in range(nt):
                        last = pe.transpose(psum[:, bb + t * P:bb + (t + 1) * P], xn[:, t0 + t, ch], core.ident[:])
                    last.then_inc(tr_mm, 1)
            pe.wait_ge(tr_free, 3 * KT)
            mod_chunks(8, 4)


def z_phase(core, io):
    nc, psum = core.nc, core.psum
    pqT = core.at("pqT", [P, KT, TOK], 0)
    pqTl = core.at("pqT_lo", [P, KT, TOK], 0, F32R)
    pqTh = core.at("pqT_hi", [P, KT, TOK], 80, F32R)
    n = [core.at("nT_hi", [P, KT, TOK], 120, F32R)[:], core.at("nT_lo", [P, KT, TOK], 40, F32R)[:]]
    stage = [core.at(f"fstage{s}", [P, KT, P], 160 + 4 * s) for s in range(2)]
    w = [[core.at(f"fw{q}{s}", [P, KT, P], 168 + 8 * s + 4 * j, F32R) for j, q in enumerate("hl")] for s in range(2)]
    zs = [core.at(f"zsf{s}", [P, TOK], 184 + 5 * s) for s in range(2)]
    mz = [core.at(f"mz{s}", [P, KT, P], 194 + 4 * s) for s in range(2)]
    mod_v = io["mod_w"][1].rearrange("(k p) (n c) -> n p k c", p=P, c=P)
    w_z = io["fn_w_in"][0][:, FW:2 * FW].rearrange("(k p) (n c) -> n p k c", p=P, c=P)
    z_v = core.zf_d.rearrange("(n p) t -> n p t", p=P)
    TILES = FW // P
    SET = [0, 1536]
    with ExitStack() as st:
        sem = sems(nc, st, core.early_sems)
        w_in, stored = [sem("wz_in0"), sem("wz_in1")], [sem("zf_stored0"), sem("zf_stored1")]
        mz_in, mz_mm, mz_rdy, coef = [sem("mz_in0"), sem("mz_in1")], sem("mz_mm"), sem("mz_rdy"), sem("coef1")
        w_hi, w_rdy, z_mm, zs_rdy, pq_hi = sem("wz_hi"), sem("wz_rdy"), sem("z_mm"), sem("zs_rdy"), sem("pqT_hi_rdy")
        block = st.enter_context(nc.Block())

        @block.sync
        def _(sp):
            for s in range(2):
                sp.dma_start(stage[s][:], w_z[s]).then_inc(w_in[s], 16)
                sp.sem_inc(stored[s], 16)
            for s in range(2):
                sp.dma_start(mz[s][:], mod_v[s]).then_inc(mz_in[s], 16)
            with sp.Fori(0, TILES // 2 - 1) as i:
                for s in range(2):
                    sp.wait_ge(w_rdy, i * 2 + (s + 1))
                    sp.dma_start(stage[s][:], w_z[i * 2 + (s + 2)]).then_inc(w_in[s], 16)
                    sp.wait_ge(zs_rdy, i * 2 + (s + 3))
                    sp.dma_start(z_v[i * 2 + s], zs[s][:]).then_inc(stored[s], 16)
                    sp.wait_ge(mz_mm, i * 2 + (s + 1))
                    sp.dma_start(mz[s][:], mod_v[i * 2 + (s + 2)]).then_inc(mz_in[s], 16)
            for s in range(2):
                sp.wait_ge(zs_rdy, TILES + s + 1)
                sp.dma_start(z_v[TILES - 2 + s], zs[s][:]).then_inc(stored[s], 16)
            for s in range(2):
                sp.wait_ge(stored[s], 16 * (TILES // 2 + 1))

        @block.tensor
        def _(pe):
            with pe.Fori(0, TILES // 2) as i:
                for s in range(2):
                    pe.wait_ge(w_rdy, i * 2 + (s + 1))
                    pe.wait_ge(zs_rdy, i * 2 + (s + 1))
                    for lo, c in ((0, 512), (512, 512), (1024, 256)):
                        for k in range(KT):
                            last = product3(pe, psum[:, SET[s] + lo:SET[s] + lo + c], [q[:, k, :] for q in w[s]],
                                            [q[:, k, lo:lo + c] for q in n], k == 0, k == KT - 1)
                    last.then_inc(z_mm, 1)
                    pe.wait_ge(mz_in[s], i * 16 + 16)
                    pe.wait_ge(mz_rdy, i * 2 + (s + 1))
                    for k in range(KT):
                        last = pe.matmul(psum[:, 3072 + 512 * s:3072 + 512 * s + 2], mz[s][:, k, :], core.scond[:, k, :],
                                         start=(k == 0), stop=(k == KT - 1))
                    last.then_inc(mz_mm, 1)

        @block.scalar
        def _(act):
            act.sem_inc(zs_rdy, 2)
            with act.Fori(0, TILES // 2) as i:
                for s in range(2):
                    act.wait_ge(z_mm, i * 2 + (s + 3))
                    act.wait_ge(stored[s], i * 16 + 16)
                    act.activation(zs[s][:], psum[:, SET[s]:SET[s] + TOK], ACT.Silu).then_inc(zs_rdy, 1)

        @block.gpsimd
        def _(pool):
            pool.sem_inc(z_mm, 2)
            with pool.Fori(0, TILES // 2) as i:
                for s in range(2):
                    pool.wait_ge(w_in[s], i * 16 + 16)
                    pool.wait_ge(z_mm, i * 2 + (s + 1))
                    pool.sem_inc(core.carried, 1)
                    split_parts(pool, w[s][0][:], w[s][1][:], stage[s][:], w_hi, i * 2 + (s + 1)).then_inc(w_rdy, 1)

        @block.vector
        def _(dve):
            dve.sem_inc(mz_rdy, 2)
            for k in range(KT):
                dve.tensor_copy(pqTh[:, k, :], pqT[:, k, :]).then_inc(pq_hi, 1)
                dve.wait_ge(pq_hi, k + 1)
                dve.tensor_tensor(pqTl[:, k, :], pqT[:, k, :], pqTh[:, k, :].bitcast(F32), ALU.subtract)
            with dve.Fori(0, TILES // 2) as i:
                for s in range(2):
                    n = i * 2 + s
                    dve.wait_ge(mz_mm, n + 1)
                    dve.tensor_tensor(core.modT[:, bass.ds(n + 24, 1), :],
                                      psum[:, 3072 + 512 * s:3072 + 512 * s + 2].rearrange("p (a b) -> p a b", a=1),
                                      core.cols[:, bass.ds(n + 24, 1)].unsqueeze(2).broadcast_to([P, 1, 2]),
                                      ALU.add).then_inc(mz_rdy, 1)
            dve.wait_ge(mz_rdy, TILES + 2)
            norm_coefs(core, dve, 1, 0).then_inc(coef, 1)
            dve.wait_ge(coef, 1)
            norm_coefs(core, dve, 1, 1)


def fourier_phase(core, io):
    nc, psum = core.nc, core.psum
    pqT = [core.at("pqT_hi", [P, KT, TOK], 80, F32R)[:], core.at("pqT_lo", [P, KT, TOK], 0, F32R)[:]]
    csw = [[core.at(f"csw{q}{s}", [P, 2, 2, FD], 40 + 8 * s + 4 * j, F32R) for j, q in enumerate("hl")] for s in range(2)]
    wg = [core.at(f"wg{s}", [P, 2, FD], 56 + 2 * s) for s in range(2)]
    chd = core.at("chd", [P, 2, 2, FD], 60)
    es = core.at("es", [P, 2, HL + HC], 64)
    zs = core.at("zs", [P, 2, TOK], 70)
    pq = [[core.at(f"pq{q}{s}", [P, 2, TOK], 120 + 20 * s + 10 * j, F32R) for j, q in enumerate("hl")] for s in range(2)]
    stage = [core.at(f"fstage{s}", [P, KT, P], 160 + 4 * s) for s in range(2)]
    w = [[core.at(f"fw{q}{s}", [P, KT, P], 168 + 8 * s + 4 * j, F32R) for j, q in enumerate("hl")] for s in range(2)]
    y = core.at("y", [P, 2, TOK], 184)
    f = core.at("f", [P, 2, TOK], 194)
    w_u = io["fn_w_in"][0][:, 0:FW].rearrange("(k p) (n c) -> n p k c", p=P, c=P)
    w_grp = io["fn_w_grp"][0].rearrange("g (k p) c -> g p k c", p=P)
    y_v = core.y_d.rearrange("(n p) t -> n p t", p=P)
    z_v = core.zf_d.rearrange("(n p) t -> n p t", p=P)
    PQ, EO, CW = 0, 1536, 3072
    LC = 1024 + 2 * HC
    with ExitStack() as st:
        sem = sems(nc, st, core.early_sems)
        chd_in = sem("chd_in")
        w_in, wg_in, zs_in, y_stored = ([sem(f"{n}{s}") for s in range(2)] for n in ("wu_in", "wg_in", "zs_in", "y_stored"))
        w_hi, w_rdy = sem("wu_hi"), sem("wu_rdy")
        cw_mm, pq_mm, eo_mm = sem("cw_mm"), sem("pq_mm"), sem("eo_mm")
        cw_hi, cw_rdy, pq_hi, pq_rdy = sem("cw_hi"), sem("cw_rdy"), sem("pq_hi"), sem("pq_rdy")
        es_rdy, f_rdy, y_rdy = sem("es_rdy"), sem("f_rdy"), sem("y_rdy")
        block = st.enter_context(nc.Block())

        def groups(body):
            def run(eng):
                body(0, 0, 0)
                with eng.Fori(0, FG // 2 - 1) as i:
                    body(i * 2 + 1, 1, i)
                    body(i * 2 + 2, 0, i + 1)
                body(FG - 1, 1, FG // 2 - 1)
            return run

        first = lambda g: isinstance(g, int) and g == 0
        last_group = lambda g: isinstance(g, int) and g == FG - 1

        @block.sync
        def _(sp):
            sp.dma_start(chd[:], io["ch_dft"]).then_inc(chd_in, 16)
            for m in range(2):
                sp.dma_start(wg[m][:], w_grp[m]).then_inc(wg_in[m], 16)
                sp.dma_start(stage[m][:], w_u[m]).then_inc(w_in[m], 16)
                sp.dma_start(zs[:, m, :], z_v[m]).then_inc(zs_in[m], 16)
                sp.sem_inc(y_stored[m], 16)

            def finished(g, m, more):
                sp.wait_ge(y_rdy, g * 2 + (m + 3))
                sp.dma_start(y_v[g * 2 + m], y[:, m, :]).then_inc(y_stored[m], 16)
                if more:
                    sp.dma_start(zs[:, m, :], z_v[g * 2 + (m + 2)]).then_inc(zs_in[m], 16)

            def body(g, s, gi):
                for m in range(2):
                    if not last_group(g):
                        sp.wait_ge(w_rdy, g * 2 + (m + 1))
                        sp.dma_start(stage[m][:], w_u[g * 2 + (m + 2)]).then_inc(w_in[m], 16)
                    if not first(g):
                        finished(g - 1, m, True)

            def wg_next(g, s):
                sp.wait_ge(cw_mm, g + 1)
                sp.dma_start(wg[s][:], w_grp[g + 2]).then_inc(wg_in[s], 16)

            body(0, 0, 0)
            with sp.Fori(0, FG // 2 - 1) as i:
                wg_next(i * 2, 0)
                body(i * 2 + 1, 1, i)
                wg_next(i * 2 + 1, 1)
                body(i * 2 + 2, 0, i + 1)
            body(FG - 1, 1, FG // 2 - 1)
            for m in range(2):
                finished(FG - 1, m, False)
            for m in range(2):
                sp.wait_ge(y_stored[m], 16 * (FG + 1))

        @block.tensor
        def _(pe):
            def group_weights(g, s, gi):
                pe.wait_ge(wg_in[s], gi * 16 + 16)
                pe.wait_ge(cw_rdy, g + 1)
                for t in range(2):
                    for ct in range(2):
                        for k in range(2):
                            last = pe.matmul(psum[:, CW + 512 * t + FD * ct:CW + 512 * t + FD * ct + FD],
                                             chd[:, t, k, ct * P:(ct + 1) * P], wg[s][:, k, :],
                                             start=(k == 0), stop=(k == 1))
                last.then_inc(cw_mm, 1)

            def p_q(g, m):
                pe.wait_ge(w_rdy, g * 2 + (m + 1))
                pe.wait_ge(pq_rdy, g * 2 + (m + 1))
                for lo, n in ((0, 512), (512, 512), (1024, 256)):
                    for k in range(KT):
                        last = product3(pe, psum[:, PQ + lo:PQ + lo + n], [q[:, k, :] for q in w[m]],
                                        [q[:, k, lo:lo + n] for q in pqT], k == 0, k == KT - 1)
                last.then_inc(pq_mm, 1)

            def e_o(g, s, m):
                if m == 0:
                    pe.wait_ge(cw_rdy, g + 2)
                    pe.wait_ge(pq_rdy, g * 2 + 3)
                pe.wait_ge(f_rdy, g * 2 + (m + 1))
                for t, off, lo, n in ((0, 0, 0, HL), (1, 512, HL, HL), (0, 1024, LAT, HC), (1, 1024 + HC, LAT + HC, HC),
                                      (0, LC, HL, 2), (0, LC + 2, LAT + HC, 2)):
                    for k in range(2):
                        last = product3(pe, psum[:, EO + off:EO + off + n], [q[:, t, k, m * P:(m + 1) * P] for q in csw[s]],
                                        [q[:, k, lo:lo + n] for q in pq[s]], k == 0, k == 1)
                last.then_inc(eo_mm, 1)

            def body(g, s, gi):
                group_weights(g, s, gi)
                for m in range(2):
                    p_q(g, m)
                    if not first(g):
                        e_o(g - 1, 1 - s, m)

            pe.wait_ge(chd_in, 16)
            groups(body)(pe)
            for m in range(2):
                e_o(FG - 1, 1, m)

        @block.scalar
        def _(act):
            act.sem_inc(cw_rdy, 1)
            act.sem_inc(pq_rdy, 1)

            def e_o(g, m):
                act.wait_ge(eo_mm, g * 2 + (m + 1))
                act.wait_ge(y_rdy, g * 2 + (m + 1))
                act.activation(es[:, m, 0:HL], psum[:, EO:EO + HL], ACT.Copy)
                act.activation(es[:, m, HL:HL + HC], psum[:, EO + 1024:EO + 1024 + HC], ACT.Copy)
                act.activation(f[:, m, 0:LAT + 1:LAT], psum[:, EO:EO + 1025:1024], ACT.Copy)
                act.activation(f[:, m, HL:LAT + HC + 1:HL + HC], psum[:, EO + LC:EO + LC + 3:2], ACT.Copy).then_inc(es_rdy, 1)

            def body(g, s, gi):
                act.wait_ge(cw_mm, g + 1)
                act.activation(csw[s][0][:].rearrange("p a b c -> p (a b c)"), psum[:, CW:CW + 1024], ACT.Copy).then_inc(cw_hi, 1)
                for m in range(2):
                    act.wait_ge(pq_mm, g * 2 + (m + 3))
                    act.activation(pq[s][0][:, m, :], psum[:, PQ:PQ + TOK], ACT.Copy).then_inc(pq_hi, 1)
                    if not first(g):
                        e_o(g - 1, m)

            groups(body)(act)
            for m in range(2):
                e_o(FG - 1, m)

        @block.vector
        def _(dve):
            dve.sem_inc(f_rdy, 1)
            dve.sem_inc(y_rdy, 2)

            def low_part(x, parts):
                return dve.tensor_tensor(parts[1], x, parts[0].bitcast(F32), ALU.subtract)

            def out(g, m):
                dve.wait_ge(es_rdy, g * 2 + (m + 1))
                for o, lo, L in ((512, 0, LAT), (1024 + HC, HL, CTX)):
                    t0, h = (0 if L == LAT else LAT), L // 2
                    for op, dst in ((ALU.subtract, f[:, m, t0 + 1:t0 + h]), (ALU.add, f[:, m, t0 + L - 1:t0 + h:-1])):
                        last = dve.tensor_tensor(dst, es[:, m, lo + 1:lo + h], psum[:, EO + o + 1:EO + o + h], op)
                last.then_inc(f_rdy, 1)
                dve.wait_ge(f_rdy, g * 2 + (m + 2))
                dve.wait_ge(zs_in[m], g * 16 + 16)
                dve.wait_ge(y_stored[m], g * 16 + 16)
                dve.tensor_tensor(y[:, m, :], f[:, m, :], zs[:, m, :], ALU.mult).then_inc(y_rdy, 1)

            def body(g, s, gi):
                dve.wait_ge(cw_hi, g + 1)
                low_part(psum[:, CW:CW + 1024], [q[:].rearrange("p a b c -> p (a b c)") for q in csw[s]]).then_inc(cw_rdy, 1)
                for m in range(2):
                    dve.wait_ge(pq_hi, g * 2 + (m + 1))
                    low_part(psum[:, PQ:PQ + TOK], [q[:, m, :] for q in pq[s]]).then_inc(pq_rdy, 1)
                    if not first(g):
                        out(g - 1, m)

            groups(body)(dve)
            for m in range(2):
                out(FG - 1, m)

        @block.gpsimd
        def _(pool):
            pool.sem_inc(pq_mm, 2)
            with pool.Fori(0, FG) as g:
                for m in range(2):
                    pool.wait_ge(w_in[m], g * 16 + 16)
                    pool.wait_ge(pq_mm, g * 2 + (m + 1))
                    pool.sem_inc(core.carried, 1)
                    split_parts(pool, w[m][0][:], w[m][1][:], stage[m][:], w_hi, g * 2 + (m + 1)).then_inc(w_rdy, 1)


def output_phase(core, io, layer):
    nc, psum, ident = core.nc, core.psum, core.ident
    last_layer = layer == 1
    name = lambda n: f"{n}_o{layer}"
    if not last_layer:
        n1 = [core.at(f"n1{q}", [P, KT, TOK], 40 * j, F32R) for j, q in enumerate("hl")]
    if last_layer:
        wo, y2 = core.at("wo_last", [P, 16, D], 128), core.at("y2", [P, 16, LAT], 64)
        fg = core.at("fg", [P, D], 24)
    else:
        wo = core.at("wo", [P, 16, D], 80)
        yb = [core.at(f"yb{s}", [P, 16, P], 144 + 8 * s) for s in range(2)]
        nf = [core.at(f"nf{s}", [P, KT, P], 193 + 4 * s) for s in range(2)]
    kb = 0 if last_layer else 160
    h = [core.at(name(f"h{s}"), [P, D], kb + 4 * s) for s in range(2)]
    gx = [core.at(name(f"gx{s}"), [P, D], kb + 8 + 4 * s) for s in range(2)]
    gate = core.at(name("gate"), [P, 2, D], kb + 16)
    junk = core.at(name("junk"), [P, D], kb + 28)
    st_ = core.at(name("st"), [P, 2, 4], kb + 32)
    y_v = core.y_d.rearrange("(c p) (n t) -> n p c t", p=P, t=P)
    h_v = (core.h_d if last_layer else io["x"][0]).rearrange("(n p) d -> n p d", p=P)
    c_v = io["ctx"][0].rearrange("(n p) d -> n p d", p=P)
    dst_v = (io["out"][0] if last_layer else core.h_d).rearrange("(n p) d -> n p d", p=P)
    w_v = io["fn_w_out"][0].rearrange("(c p) d -> p c d", p=P)
    tiles = NL if last_layer else NT
    conds = 1 if last_layer else 2
    with ExitStack() as st:
        sem = sems(nc, st)
        if not last_layer:
            wo_in = [sem(f"wo_in{q}") for q in range(4)]
        y_in, h_in, stored = ([sem(f"{n}{s}") for s in range(2)] for n in ("y_in", "h_in", "h_stored"))
        fg_in, g_mm, gate_rdy = sem("fg_in"), sem("g_mm"), sem("gate_rdy")
        o_mm, gx_rdy, h_rdy, ss_rdy, var_rdy = sem("o_mm"), sem("gx_rdy"), sem("h_rdy"), sem("ss_rdy"), sem("var_rdy")
        std_rdy, rstd_rdy, n_rdy = sem("std_rdy"), sem("rstd_rdy"), sem("n_rdy")
        if not last_layer:
            t_mm, t_free, hi_rdy, n1_rdy = sem("t_mm"), sem("t_free"), sem("n1_hi_rdy"), sem("n1_rdy")
        block = st.enter_context(nc.Block())

        def tiles_loop(eng, body):
            with eng.Fori(0, NL // 2) as i:
                for s in range(2):
                    body(i * 2 + s, s, i, 0)
            for n in range(NL, tiles):
                body(n, n % 2, n // 2, 1)

        @block.sync
        def _(sp):
            def load(n, s, ctx_tile):
                if not last_layer:
                    sp.dma_start(yb[s][:], y_v[n]).then_inc(y_in[s], 16)
                sp.dma_start(h[s][:], c_v[n - NL] if ctx_tile else h_v[n]).then_inc(h_in[s], 16)

            load(0, 0, 0)
            if not last_layer:
                for q in range(4):
                    rows, half = slice(8 * (q % 2), 8 * (q % 2) + 8), slice(512 * (q // 2), 512 * (q // 2) + 512)
                    sp.dma_start(wo[:, rows, half], w_v[:, rows, half]).then_inc(wo_in[q], 16)
            load(1, 1, 0)
            if last_layer:
                sp.dma_start(fg[:], io["final_g"].rearrange("(a n) -> a n", a=1).broadcast_to([P, D])).then_inc(fg_in, 16)

            def turn(n, s, i, store_it, load_ctx):
                if store_it:
                    sp.wait_ge(n_rdy if last_layer else h_rdy, n + 1)
                    sp.dma_start(dst_v[n], h[s][:]).then_inc(stored[s], 16)
                if load_ctx is not None:
                    sp.wait_ge(o_mm, n + 1)
                    sp.wait_ge(n_rdy, n + 1)
                    if store_it:
                        sp.wait_ge(stored[s], i * 16 + 16)
                    load(n + 2, s, load_ctx)

            with sp.Fori(0, NL // 2 - 1) as i:
                for s in range(2):
                    turn(i * 2 + s, s, i, True, 0)
            for n in range(NL - 2, NL):
                turn(n, n % 2, n // 2, True, 1 if tiles > NL else None)
            for s in range(2):
                sp.wait_ge(stored[s], 16 * NL // 2)

        @block.tensor
        def _(pe):
            for c in range(conds):
                for k in range(KT):
                    col = core.modT[:, 24 * layer + 16 + k, c:c + 1].broadcast_to([P, P])
                    last = pe.matmul(psum[:, 1024 * c + k * P:1024 * c + (k + 1) * P], col, ident[:], start=True, stop=True)
            last.then_inc(g_mm, 1)
            pe.wait_ge(gate_rdy, 1)

            def norm_transposes(n, s):
                pe.wait_ge(n_rdy, n + 1)
                pe.wait_ge(t_free, n + 1)
                b = 2048 + 1024 * s
                for k in range(KT):
                    last = pe.transpose(psum[:, b + k * P:b + (k + 1) * P], gx[s][:, k * P:(k + 1) * P], ident[:])
                last.then_inc(t_mm, 1)

            def product(n, s, y_tile, wo_arrives=False):
                pe.wait_ge(gx_rdy, n + 1)
                for half in range(2):
                    o = 1024 * s + 512 * half
                    for k in range(16):
                        if wo_arrives and k % 8 == 0:
                            pe.wait_ge(wo_in[2 * half + k // 8], 16)
                        last = pe.matmul(psum[:, o:o + 512], y_tile(k), wo[:, k, 512 * half:512 * half + 512],
                                         start=(k == 0), stop=(k == 15))
                last.then_inc(o_mm, 1)

            if last_layer:
                for n in range(NL):
                    product(n, n % 2, lambda k: y2[:, k, n * P:(n + 1) * P])
            else:
                pe.wait_ge(y_in[0], 16)
                product(0, 0, lambda k: yb[0][:, k, :], True)
                with pe.Fori(0, NL // 2) as i:
                    for s in range(2):
                        n = i * 2 + s
                        pe.wait_ge(y_in[1 - s], i * 16 + (16 + 16 * s))
                        product(n + 1, 1 - s, lambda k: yb[1 - s][:, k, :])
                        norm_transposes(n, s)
                pe.wait_ge(y_in[1], (NL // 2 + 1) * 16)
                product(NL + 1, 1, lambda k: yb[1][:, k, :])
                norm_transposes(NL, 0)
                norm_transposes(NL + 1, 1)

        @block.vector
        def _(dve):
            dve.sem_inc(gx_rdy, 2)
            dve.wait_ge(g_mm, 1)
            dve.tensor_copy(gate[:, 0:conds, :].rearrange("p c d -> p (c d)"), psum[:, 0:1024 * conds]).then_inc(gate_rdy, 1)
            dve.wait_ge(gate_rdy, 1)
            if last_layer:
                dve.wait_ge(fg_in, 16)

            def body(n, s, i, c):
                dve.wait_ge(o_mm, n + 1)
                if not last_layer:
                    dve.wait_ge(t_free, n + 1)
                dve.tensor_tensor(gx[s][:], psum[:, 1024 * s:1024 * s + 1024], gate[:, c, :], ALU.mult).then_inc(gx_rdy, 1)
                dve.wait_ge(gx_rdy, n + 3)
                dve.wait_ge(h_in[s], i * 16 + 16)
                dve.tensor_tensor(h[s][:], h[s][:], gx[s][:], ALU.add).then_inc(h_rdy, 1)
                dve.wait_ge(ss_rdy, n + 1)
                dve.tensor_scalar(st_[:, s, 1:2], st_[:, s, 0:1], 1.0 / D, EPS, ALU.mult, ALU.add).then_inc(var_rdy, 1)
                dve.wait_ge(std_rdy, n + 1)
                dve.reciprocal(st_[:, s, 3:4], st_[:, s, 2:3]).then_inc(rstd_rdy, 1)
                dve.wait_ge(rstd_rdy, n + 1)
                if last_layer:
                    dve.scalar_tensor_tensor(h[s][:], h[s][:], st_[:, s, 3:4], fg[:], ALU.mult, ALU.mult).then_inc(n_rdy, 1)
                else:
                    dve.tensor_scalar(gx[s][:], h[s][:], st_[:, s, 3:4], None, ALU.mult).then_inc(n_rdy, 1)

            tiles_loop(dve, body)

        @block.scalar
        def _(act):
            if not last_layer:
                act.sem_inc(t_free, 2)

            def stats(n, s, i, c):
                act.wait_ge(h_rdy, n + 1)
                act.activation(junk[:], h[s][:], ACT.Square, accum_out=st_[:, s, 0:1]).then_inc(ss_rdy, 1)
                act.wait_ge(var_rdy, n + 1)
                act.activation(st_[:, s, 2:3], st_[:, s, 1:2], ACT.Sqrt).then_inc(std_rdy, 1)

            def to_n1T(n, s, i, c):
                act.wait_ge(t_mm, n + 1)
                act.wait_ge(n1_rdy, n + 1)
                b = 2048 + 1024 * s
                for k in range(KT):
                    last = act.activation(nf[s][:, k, :], psum[:, b + k * P:b + (k + 1) * P], ACT.Identity,
                                          scale=core.acoef[:, 1, k, c:c + 1], bias=core.modT[:, 24 + k, c:c + 1])
                last.then_inc(t_free, 1)

            def body(n, s, i, c):
                stats(n, s, i, c)
                if not last_layer:
                    to_n1T(n, s, i, c)

            tiles_loop(act, body)

        @block.gpsimd
        def _(pool):
            def body(n, s, i, c):
                pool.wait_ge(t_free, n + 3)
                pool.sem_inc(core.carried, 1)
                hi, lo = (q[:, :, bass.ts(n, P)] for q in n1)
                pool.tensor_copy(hi, nf[s][:]).then_inc(hi_rdy, 1)
                pool.wait_ge(hi_rdy, n + 1)
                pool.tensor_tensor(lo, nf[s][:], hi.bitcast(F32), ALU.subtract).then_inc(n1_rdy, 1)

            if not last_layer:
                pool.sem_inc(n1_rdy, 2)
                tiles_loop(pool, body)


def project_phase(core, io):
    nc, psum, ident = core.nc, core.psum, core.ident
    n1 = [core.at(f"n1{q}", [P, KT, TOK], 40 * j, F32R) for j, q in enumerate("hl")]
    stage = [core.at(f"wstage{s}", [P, KT, P], 80 + 4 * s) for s in range(2)]
    w = [[core.at(f"w{q}{s}", [P, KT, P], 88 + 8 * s + 4 * j, F32R) for j, q in enumerate("hl")] for s in range(2)]
    PADR, PADC = GR + 2, GW + 2
    NPAD = PADR * PADC + CTX + 2
    pad = [core.at(f"pad{s}", [P, NPAD], 104 + 6 * s) for s in range(2)]
    acc = [core.at(f"acc{s}", [P, TOK], 116 + 5 * s) for s in range(2)]
    sil = [core.at(f"sil{s}", [P, TOK], 126 + 5 * s) for s in range(2)]
    qt = core.at("qt", [P, NL, P], 136)
    kt = core.at("kt", [P, NT, P], 140)
    vt = [core.at(f"vt{s}", [P, NT, P], 145 + 5 * s) for s in range(2)]
    qT = core.at("qT", [P, LAT], 155)
    kT = core.at("kT", [P, TOK], 159)
    zs = [core.at(f"zs_d{s}", [P, LAT], 164 + 4 * s) for s in range(2)]
    sq = core.at("sq", [P, NT, P], 172)
    ssq = core.at("ssq", [P, 2, 3, 16], 177)
    crow = core.at("crow", [9, 4096], 178)
    cw = core.at("cw", [P, 32, 9], 194)
    cwh = core.at("cwh", [P, 4, 9], 195.25)
    ab = core.at("ab", [P, 2, 16], 195.5)
    gw = [core.at(f"gw{s}", [P, NT, 16], 196 + 0.75 * s) for s in range(4)]
    wab = core.at("wab", [P, KT, 32], 199)
    wabs = [core.at(f"wab{q}", [P, KT, 32], 200 + j, F32R) for j, q in enumerate("hl")]
    abT = core.at("abT", [32, TOK], 172)
    wi = io["dn_w_in"][0].rearrange("(k p) c -> p k c", p=P)
    QO, KO, VO, ZO, AO = 0, D, 2 * D, 2 * D + FW, 2 * D + 2 * FW
    k_v = core.k_d.rearrange("(n p) (h c) -> h p n c", p=P, c=P)
    v_v = core.v_d.rearrange("(n p) (h c) -> h p n c", p=P, c=P)
    z_v = core.z_d.rearrange("(n p) t -> n p t", p=P)
    SET = [0, 1536]
    FULL, LATO = ((0, 512), (512, 512), (1024, 256)), ((0, 512), (512, 512))
    with ExitStack() as st:
        sem = sems(nc, st)
        misc_in = sem("misc_in")
        w_in = [sem("w_in0"), sem("w_in1")]
        w_hi, w_rdy = sem("w_hi"), sem("w_rdy")
        abT_mm, abT_rdy, wab_hi = sem("abT_mm"), sem("abT_rdy"), sem("wab_hi")
        ab_mm, tap_mm, tap_rdy = sem("ab_mm"), sem("tap_mm"), sem("tap_rdy")
        gch, gact = sem("decay_vec"), sem("decay_act")
        mm = sem("proj_mm")
        evac = sem("proj_evac")
        conv = sem("conv_done")
        silu = sem("silu_done")
        tmm, tfree = sem("t_mm"), sem("t_free_d")
        sq_rdy, red, var, std, nrm = sem("sq_rdy"), sem("red"), sem("var"), sem("std"), sem("nrm")
        taps, taps_used = sem("taps"), sem("taps_used")
        vec = sem("conv_chain")
        out_s = {n: sem(f"{n}_stored") for n in ("qT", "k", "kT", "v0", "v1", "z0", "z1")}
        block = st.enter_context(nc.Block())
        T = {"q": 0, "k": 2, "qT": 5, "v0": 7, "kT": 10, "v1": 13}
        NB = 16

        @block.sync
        def _(sp):
            sp.dma_start(wab[:], wi[:, :, AO:AO + 32]).then_inc(misc_in, 16)
            sp.dma_start(ab[:, 0, :], io["dn_dt_bias"].rearrange("a b c -> a (b c)").broadcast_to([P, 16])).then_inc(misc_in, 16)
            sp.dma_start(ab[:, 1, :], io["dn_a_log"].rearrange("a b c -> a (b c)").broadcast_to([P, 16])).then_inc(misc_in, 16)
            sp.dma_start(crow[:], io["dn_conv"][0].rearrange("a b c -> (a b) c")).then_inc(misc_in, 16)
            cols_of = lambda o, n: wi[:, :, o:o + n * P].rearrange("p k (t c) -> t p k c", c=P)
            tiles = ((cols_of(QO, H), 1, 0), (cols_of(KO, H), 1, 0), (cols_of(VO, 2 * H), 2, 0), (cols_of(VO, 2 * H), 2, 1),
                     (cols_of(ZO, 2 * H), 2, 0), (cols_of(ZO, 2 * H), 2, 1))

            def load(j, hh, wait):
                if wait is not None:
                    sp.wait_ge(w_rdy, wait)
                src, stride, off = tiles[j]
                sp.dma_start(stage[j % 2][:], src[hh * stride + off]).then_inc(w_in[j % 2], 16)

            load(0, 0, None)
            load(1, 0, None)
            for n in out_s:
                sp.sem_inc(out_s[n], 16)

            def turn(hh, more):
                nxt = lambda j: load(j, hh + 1, hh * 6 + (j + 5)) if more else None
                load(2, hh, hh * 6 + 1)
                load(3, hh, hh * 6 + 2)
                load(4, hh, hh * 6 + 3)
                sp.wait_ge(tfree, hh * NB + (2 + T["qT"] + 2))
                sp.dma_start(core.qT_d[hh], qT[:]).then_inc(out_s["qT"], 16)
                load(5, hh, hh * 6 + 4)
                nxt(0)
                sp.wait_ge(nrm, hh * 2 + 2)
                sp.sem_inc(core.carried, 1)
                sp.wait_ge(tfree, hh * NB + (2 + T["v0"] + 3))
                sp.dma_start(k_v[hh], kt[:]).then_inc(out_s["k"], 16)
                sp.dma_start(v_v[hh * 2], vt[0][:]).then_inc(out_s["v0"], 16)
                sp.wait_ge(tfree, hh * NB + (2 + T["kT"] + 3))
                sp.dma_start(core.kT_d[hh], kT[:]).then_inc(out_s["kT"], 16)
                nxt(1)
                sp.wait_ge(evac, hh * 6 + 7)
                sp.dma_start(z_v[hh * 2], zs[0][:]).then_inc(out_s["z0"], 16)
                sp.wait_ge(tfree, hh * NB + (2 + T["v1"] + 3))
                sp.sem_inc(core.carried, 1)
                sp.dma_start(v_v[hh * 2 + 1], vt[1][:]).then_inc(out_s["v1"], 16)
                sp.wait_ge(evac, hh * 6 + 8)
                sp.dma_start(z_v[hh * 2 + 1], zs[1][:]).then_inc(out_s["z1"], 16)

            with sp.Fori(0, H - 1) as hh:
                turn(hh, True)
            turn(H - 1, False)
            for n in out_s:
                sp.wait_ge(out_s[n], 16 * (H + 1))

        @block.tensor
        def _(pe):
            pe.wait_ge(misc_in, 64)
            pe.wait_ge(wab_hi, 2)
            for lo, n in FULL:
                for k in range(KT):
                    last = product3(pe, psum[0:32, lo:lo + n], [q[:, k, :] for q in wabs], [q[:, k, lo:lo + n] for q in n1],
                                    k == 0, k == KT - 1)
            last.then_inc(abT_mm, 1)
            pe.wait_ge(abT_rdy, 1)
            for n in range(NT):
                last = pe.transpose(psum[:, n * 32:(n + 1) * 32], abT[:, n * P:(n + 1) * P], ident[0:32, 0:32])
            last.then_inc(ab_mm, 1)
            for t in range(32):
                last = pe.transpose(psum[:, 3072 + 9 * t:3072 + 9 * t + 9], crow[:, t * P:(t + 1) * P], ident[0:9, 0:9])
            last.then_inc(tap_mm, 1)
            pe.wait_ge(gch, 2)
            pe.wait_ge(tap_rdy, 1)

            with pe.Fori(0, H) as hh:
                def product(j, groups):
                    pe.wait_ge(w_rdy, hh * 6 + (j + 1))
                    pe.wait_ge(evac, hh * 6 + (j + 1))
                    for lo, n in groups:
                        for k in range(KT):
                            last = product3(pe, psum[:, SET[j % 2] + lo:SET[j % 2] + lo + n],
                                            [q[:, k, :] for q in w[j % 2]], [q[:, k, lo:lo + n] for q in n1],
                                            k == 0, k == KT - 1)
                    last.then_inc(mm, 1)

                def transposes(what, src, tiles):
                    for j, t0 in enumerate(range(0, tiles, 4)):
                        b = T[what] + j
                        pe.wait_ge(tfree, hh * NB + (b + 1))
                        for t in range(t0, min(t0 + 4, tiles)):
                            o = 3072 + 512 * (b % 2) + (t - t0) * P
                            last = pe.transpose(psum[:, o:o + P], src(t), ident[:])
                        last.then_inc(tmm, 1)

                chan = lambda s: (lambda t: sil[s][:, t * P:(t + 1) * P])
                product(0, LATO)
                product(1, FULL)
                pe.wait_ge(silu, hh * 4 + 1)
                transposes("q", chan(0), NL)
                product(2, FULL)
                pe.wait_ge(silu, hh * 4 + 2)
                transposes("k", chan(1), NT)
                pe.wait_ge(nrm, hh * 2 + 1)
                transposes("qT", lambda t: qt[:, t, :], NL)
                product(3, FULL)
                pe.wait_ge(silu, hh * 4 + 3)
                transposes("v0", chan(0), NT)
                pe.wait_ge(nrm, hh * 2 + 2)
                transposes("kT", lambda t: kt[:, t, :], NT)
                product(4, LATO)
                pe.wait_ge(silu, hh * 4 + 4)
                transposes("v1", chan(1), NT)
                product(5, LATO)

        def inner(s):
            g = pad[s][:, 0:PADR * PADC].rearrange("p (r c) -> p r c", c=PADC)
            return g, pad[s][:, PADR * PADC:NPAD]

        @block.scalar
        def _(act):
            act.sem_inc(evac, 2)
            act.sem_inc(tfree, 2)
            act.wait_ge(tap_mm, 1)
            act.activation(cw[:].rearrange("p t n -> p (t n)"), psum[:, 3072:3072 + 288], ACT.Copy).then_inc(tap_rdy, 1)
            act.wait_ge(gch, 8)
            act.activation(gw[1][:], gw[1][:], ACT.Exp, scale=-1.0).then_inc(gact, 1)
            act.activation(gw[3][:], gw[3][:], ACT.Exp, scale=-1.0).then_inc(gact, 1)
            act.activation(gw[2][:], gw[2][:], ACT.Exp).then_inc(gact, 1)
            act.activation(ab[:, 1, :], ab[:, 1, :], ACT.Exp).then_inc(gact, 1)
            act.wait_ge(gch, 10)
            act.activation(gw[1][:], gw[1][:], ACT.Ln).then_inc(gact, 1)
            act.wait_ge(vec, 1)

            with act.Fori(0, H) as hh:
                def to_pad(j):
                    act.wait_ge(mm, hh * 6 + (j + 3))
                    s, b = j % 2, SET[j % 2]
                    g, c = inner(s)
                    last = act.activation(g[:, 1:GR + 1, 1:GW + 1], psum[:, b:b + LAT].rearrange("p (r c) -> p r c", c=GW), ACT.Copy)
                    if j:
                        last = act.activation(c[:, 1:CTX + 1], psum[:, b + LAT:b + TOK], ACT.Copy)
                    last.then_inc(evac, 1)

                def do_silu(j):
                    act.wait_ge(conv, hh * 4 + (j + 1))
                    n = TOK if j else LAT
                    act.activation(sil[j % 2][:, 0:n], acc[j % 2][:, 0:n], ACT.Silu).then_inc(silu, 1)

                def tokens(what, dst, tiles, squares):
                    for j, t0 in enumerate(range(0, tiles, 4)):
                        b, n = T[what] + j, min(4, tiles - t0)
                        src = psum[:, 3072 + 512 * (b % 2):3072 + 512 * (b % 2) + n * P].rearrange("p (t c) -> p t c", c=P)
                        act.wait_ge(tmm, hh * NB + (b + 1))
                        if squares:
                            act.activation(sq[:, t0:t0 + n, :], src, ACT.Square).then_inc(sq_rdy, 1)
                        act.activation(dst[:, t0:t0 + n, :], src, ACT.Copy).then_inc(tfree, 1)

                def std_of(j):
                    act.wait_ge(var, hh * 2 + (j + 1))
                    act.activation(ssq[:, j, 1, 0:NT], ssq[:, j, 0, 0:NT], ACT.Sqrt).then_inc(std, 1)

                act.wait_ge(taps_used, hh + 1)
                for j, lo in ((0, hh), (1, hh + 8), (2, hh * 2 + 16), (3, hh * 2 + 17)):
                    last = act.activation(cwh[:, j, :], cw[:, bass.ds(lo, 1), :].rearrange("p a n -> p (a n)"), ACT.Copy)
                last.then_inc(taps, 1)
                cm = lambda t: t[:].rearrange("p (t c) -> p t c", c=P)
                to_pad(0)
                do_silu(0)
                to_pad(1)
                tokens("q", qt, NL, True)
                do_silu(1)
                std_of(0)
                to_pad(2)
                act.wait_ge(out_s["k"], hh * 16 + 16)
                tokens("k", kt, NT, True)
                act.wait_ge(out_s["qT"], hh * 16 + 16)
                tokens("qT", cm(qT), NL, False)
                do_silu(2)
                std_of(1)
                to_pad(3)
                act.wait_ge(out_s["v0"], hh * 16 + 16)
                tokens("v0", vt[0], NT, False)
                act.wait_ge(out_s["kT"], hh * 16 + 16)
                tokens("kT", cm(kT), NT, False)
                do_silu(3)
                for m in range(2):
                    act.wait_ge(mm, hh * 6 + (7 + m))
                    act.wait_ge(out_s[f"z{m}"], hh * 16 + 16)
                    act.activation(zs[m][:], psum[:, SET[m]:SET[m] + LAT], ACT.Silu).then_inc(evac, 1)
                    if m == 0:
                        act.wait_ge(out_s["v1"], hh * 16 + 16)
                        tokens("v1", vt[1], NT, False)

        @block.gpsimd
        def _(pool):
            for old in core.early_sems:
                pool.sem_clear(old)
            pool.wait_ge(misc_in, 64)
            split_parts(pool, wabs[0][:], wabs[1][:], wab[:], wab_hi, 1).then_inc(wab_hi, 1)
            pool.sem_inc(mm, 2)
            with pool.Fori(0, H) as hh:
                for j in range(6):
                    pool.wait_ge(w_in[j % 2], hh * 48 + (16 * (j // 2) + 16))
                    pool.wait_ge(mm, hh * 6 + (j + 1))
                    pool.sem_inc(core.carried, 1)
                    split_parts(pool, w[j % 2][0][:], w[j % 2][1][:], stage[j % 2][:], w_hi,
                                hh * 6 + (j + 1)).then_inc(w_rdy, 1)

        @block.vector
        def _(dve):
            dve.sem_inc(taps_used, 1)
            dve.memset(pad[0][:], 0.0)
            dve.memset(pad[1][:], 0.0).then_inc(vec, 1)
            dve.memset(ssq[:], 1.0).then_inc(vec, 1)
            dve.wait_ge(abT_mm, 1)
            dve.tensor_copy(abT[:], psum[0:32, 0:TOK]).then_inc(abT_rdy, 1)
            dve.wait_ge(ab_mm, 1)
            ga = psum[:, 0:320].rearrange("p (n c) -> p n c", c=32)
            dt = ab[:, 0, :].unsqueeze(1).broadcast_to([P, NT, 16])
            n = [0]

            def link(ins):
                n[0] += 1
                ins.then_inc(gch, 1)
                dve.wait_ge(gch, n[0])

            link(dve.tensor_copy(gw[3][:], ga[:, :, 16:32]))
            link(dve.tensor_tensor(gw[0][:], ga[:, :, 0:16], dt, ALU.add))
            link(dve.tensor_scalar(gw[1][:], gw[0][:], -1.0, None, ALU.mult))
            link(dve.tensor_tensor(gw[1][:], gw[1][:], gw[0][:], ALU.max))
            link(dve.tensor_scalar(gw[0][:], gw[0][:], 0.0, None, ALU.max))
            link(dve.tensor_scalar(gw[2][:], gw[3][:], -1.0, None, ALU.mult))
            link(dve.tensor_tensor(gw[3][:], gw[3][:], gw[2][:], ALU.max))
            link(dve.tensor_scalar(gw[2][:], gw[2][:], 0.0, -1.0, ALU.max, ALU.mult))
            dve.wait_ge(gact, 4)
            link(dve.tensor_scalar(gw[3][:], gw[3][:], 1.0, None, ALU.add))
            link(dve.tensor_scalar(gw[1][:], gw[1][:], 1.0, None, ALU.add))
            link(dve.reciprocal(gw[3][:], gw[3][:]))
            link(dve.tensor_tensor(core.beta[:], gw[2][:], gw[3][:], ALU.mult))
            link(dve.tensor_scalar(core.nbeta[:], core.beta[:], -1.0, None, ALU.mult))
            dve.wait_ge(gact, 5)
            link(dve.tensor_tensor(gw[0][:], gw[0][:], gw[1][:], ALU.add))
            link(dve.scalar_tensor_tensor(core.gtok[:], gw[0][:], -1.0,
                                          ab[:, 1, :].unsqueeze(1).broadcast_to([P, NT, 16]), ALU.mult, ALU.mult))

            with dve.Fori(0, H) as hh:
                NV = 8 + 3 * 10
                at = [0]

                def chain(ins):
                    at[0] += 1
                    ins.then_inc(vec, 1)
                    dve.wait_ge(vec, hh * NV + (2 + at[0]))

                def convolve(j):
                    s = j % 2
                    dve.wait_ge(evac, hh * 6 + (j + 3))
                    g, c = inner(s)
                    a = acc[s][:, 0:LAT].rearrange("p (r c) -> p r c", c=GW)
                    ac = acc[s][:, LAT:TOK]
                    tap = lambda t: cwh[:, j, t:t + 1]
                    if j:
                        dve.tensor_scalar(ac, c[:, 0:CTX], tap(3), None, ALU.mult)
                    chain(dve.tensor_scalar(a, g[:, 0:GR, 0:GW], tap(0), None, ALU.mult))
                    for t in range(1, 9):
                        last = dve.scalar_tensor_tensor(a, g[:, t // 3:t // 3 + GR, t % 3:t % 3 + GW], tap(t), a, ALU.mult, ALU.add)
                        if t < 8:
                            chain(last)
                        if j and t in (4, 5):
                            last = dve.scalar_tensor_tensor(ac, c[:, t - 3:t - 3 + CTX], tap(t), ac, ALU.mult, ALU.add)
                            chain(last)
                    return last

                def norm(j, x, tiles, scale):
                    nb = (tiles + 3) // 4
                    dve.wait_ge(sq_rdy, hh * 5 + (2 if j == 0 else 5))
                    dve.reduce_sum(ssq[:, j, 2, 0:tiles], sq[:, 0:tiles, :], AXX).then_inc(red, 1)
                    dve.wait_ge(red, hh * 4 + (2 * j + 1))
                    dve.tensor_scalar(ssq[:, j, 0, 0:tiles], ssq[:, j, 2, 0:tiles], EPS, 1.0 / scale ** 2, ALU.add, ALU.mult).then_inc(var, 1)
                    dve.wait_ge(std, hh * 2 + (j + 1))
                    dve.reciprocal(ssq[:, j, 2, 0:tiles], ssq[:, j, 1, 0:tiles]).then_inc(red, 1)
                    dve.wait_ge(red, hh * 4 + (2 * j + 2))
                    dve.wait_ge(tfree, hh * NB + (2 + T["qk"[j]] + nb))
                    dve.tensor_tensor(x[:], x[:], ssq[:, j, 2, 0:tiles].unsqueeze(2).broadcast_to([P, tiles, P]),
                                      ALU.mult).then_inc(nrm, 1)

                dve.wait_ge(taps, hh + 1)
                convolve(0).then_inc(conv, 1)
                convolve(1).then_inc(conv, 1)
                norm(0, qt, NL, DK ** -0.5)
                convolve(2).then_inc(conv, 1)
                norm(1, kt, NT, 1.0)
                convolve(3).then_inc(conv, 1)
                dve.wait_ge(conv, hh * 4 + 4)
                dve.sem_inc(taps_used, 1)
                assert at[0] == NV


class Steps:

    def __init__(self, names):
        self.names = names.split()
        self.n = len(self.names)

    def done(self, step, name):
        return step * self.n + (self.names.index(name) + 1)


LAG = 1
NB = 32
TOP = (5, 6)
SUBST = " ".join(f"m{k} a{k}" for k in range(NB - 1))
PE_EV = Steps("gb gp kk0 kk1 kk2 kk3 " + " ".join(f"rp{r}" for r in range(NB // 2)) + " x5 d5 t5 x6 t6 "
              + " ".join(f"{w}{p}" for w in ("ks", "vn", "o", "su") for p in range(4)))
ACT_EV = Steps("eg el tl dt hi tt x5 x6 vn0 vn1 vn2 vn3")
DVE_EV = Steps("gps td gm gms db na0 na1 na2 na3 pt lo " + SUBST + " tr tu5 tt5 tt6 "
               + " ".join(f"{w}{p}" for w in ("r", "oa", "su") for p in range(4)))
POOL_EV = Steps("gc bc z qg kg kta")


def delta_phase(core, io):
    nc, psum = core.nc, core.psum
    o = core.at("o", [P, NL, FW], 0)
    per = lambda n, shape, kb, dt=F32: [core.at(f"{n}_{d}", shape, 64 + 60 * d + kb, dt) for d in range(2)]
    S = per("S", [P, H, DV], 0)
    kq = per("kq", [P, H, 2, P], 8)
    kk = per("kk", [P, H, P], 16)
    v = per("v", [P, H, DV], 20)
    T = per("T", [P, H, P], 28)
    TT = per("TT", [P, H, P], 32)
    X = per("X", [P, H, P], 36)
    nA = per("nA", [P, H, P], 40)
    DT = per("DT", [P, H, P], 44)
    EG = per("EG", [P, H, P], 48)
    QG = per("QG", [P, H, P], 52)
    R = per("R", [P, H, NB], 56)
    tmp = per("tmp", [P, H, NB], 57)
    ahi = per("ahi", [P, H, NB], 58, F32R)
    alo = per("alo", [P, H, NB], 59, F32R)
    U = core.at("U", [P, 2, P], 184)
    NM = core.at("NM", [P, 2, P], 185)
    lm = core.at("lm", [P, 2, 2, 64], 186, I32)
    sel = core.at("sel", [P, NB, P], 187, F32R)
    selst = core.at("selst", [P, NB, P], 0)
    eye = core.at("eye", [P, NB], 203)
    small = lambda n, k: [core.at(f"{n}_{d}", [P, H], 203.125 + (2 * k + d) / 32) for d in range(2)]
    gc, bc, nb, gps, td, tl, el = (small(n, k) for k, n in enumerate(("gc", "bc", "nb", "gps", "td", "tl", "el")))
    kT_v = core.kT_d.rearrange("h p (n t) -> n p h t", t=P)
    qT_v = core.qT_d.rearrange("h p (n t) -> n p h t", t=P)
    k_v = core.k_d.rearrange("(n p) (h c) -> n p h c", p=P, h=H)
    v_v = core.v_d.rearrange("(n p) (h c) -> n p h c", p=P, h=H)
    LAST = (P - 1, 0)
    b3 = lambda a: a[:].unsqueeze(2).broadcast_to([P, H, P])
    quad = [slice(NB * q, NB * (q + 1)) for q in range(4)]

    def half(t, l, which):
        return t[:].rearrange("p h (n two s) -> p h n two s", two=2, s=1 << l)[:, :, :, which, :]

    def packed(bank, l):
        return bank.rearrange("p (h n s) -> p h n s", h=H, s=1 << l)

    def mask(l, which):
        m = lm[:, l - TOP[0], which, :].rearrange("p (n s) -> p n s", s=1 << l)
        return m.unsqueeze(1).broadcast_to([P, H, 64 >> l, 1 << l])

    with ExitStack() as st:
        sem = sems(nc, st)
        tab_in, nm_rdy, init_rdy, sel_rdy = sem("tab_in5"), sem("nm_rdy"), sem("init_rdy"), sem("sel_rdy")
        kT_in, qT_in, k_in, v_in = ([sem(f"{n}{d}") for d in (0, 1)] for n in ("kT_in", "qT_in", "k_in", "v_in"))
        pe_done = [sem("pe_fwd"), sem("pe_bwd")]
        act_done = [sem("act_fwd"), sem("act_bwd")]
        dve_done = [sem("dve_fwd"), sem("dve_bwd")]
        pool_done = [sem("pool_fwd"), sem("pool_bwd")]
        block = st.enter_context(nc.Block())

        def bank(d, b):
            return psum[:, (4 * d + b) * 512:(4 * d + b + 1) * 512]

        def head2(d, p):
            return bank(d, p).rearrange("p (a c) -> p a c", a=2)

        class At:

            def __init__(self, d, step, chunk, lat):
                self.d, self.step, self.chunk, self.lat = d, step, chunk, lat
                self.first = isinstance(step, int) and step == 0

        def ctx_at(d, step):
            return At(d, step, NL + step if d == 0 else NL + 1 - step, False)

        def all_halves(eng, half_step, start, end):
            c = ctx_at
            lat = lambda d, n: At(d, n + 2, n if d == 0 else NL - 1 - n, True)
            start(c(0, 0))
            half_step(c(0, 0), None, c(1, 0))
            half_step(c(1, 0), c(0, 0), c(0, 1))
            half_step(c(0, 1), c(1, 0), c(1, 1))
            half_step(c(1, 1), c(0, 1), lat(0, 0))
            half_step(lat(0, 0), c(1, 1), lat(1, 0))
            regs = [eng.alloc_register(n) for n in ("up", "up1", "down", "down1")]
            for r, n in zip(regs, (0, 1, NL - 1, NL - 2)):
                eng.reg_mov(r, n)
            with eng.Fori(0, NL - 1) as i:
                up, up1, down, down1 = (eng.snap(r, min_val=0, max_val=NL - 1) for r in regs)
                half_step(At(1, i + 2, down, True), At(0, i + 2, up, True), At(0, i + 3, up1, True))
                half_step(At(0, i + 3, up1, True), At(1, i + 2, down, True), At(1, i + 3, down1, True))
                for r in regs[:2]:
                    eng.reg_add(r, r, 1)
                for r in regs[2:]:
                    eng.reg_sub(r, r, 1)
            half_step(lat(1, NL - 1), lat(0, NL - 1), None)
            end(lat(1, NL - 1))

        @block.sync
        def _(sp):
            sp.dma_start(U[:], io["tri"]).then_inc(tab_in, 16)
            sp.dma_start(lm[:], io["level_mask"]).then_inc(tab_in, 16)
            sp.dma_start(eye[:], io["block_eye"]).then_inc(tab_in, 16)
            sp.dma_start(selst[:], io["block_sel"]).then_inc(tab_in, 16)

            def load_kq(a):
                if not a.first:
                    sp.wait_ge(pe_done[a.d], PE_EV.done(a.step - 1, "kk3"))
                    sp.wait_ge(pool_done[a.d], POOL_EV.done(a.step - 1, "kg"))
                sp.dma_start(kq[a.d][:, :, 0, :], kT_v[a.chunk]).then_inc(kT_in[a.d], 16)
                if a.lat:
                    sp.dma_start(kq[a.d][:, :, 1, :], qT_v[a.chunk]).then_inc(qT_in[a.d], 16)

            def load_kv(a):
                if not a.first:
                    sp.wait_ge(pe_done[a.d], PE_EV.done(a.step - 1, "su3"))
                sp.dma_start(kk[a.d][:], k_v[a.chunk]).then_inc(k_in[a.d], 16)
                sp.dma_start(v[a.d][:], v_v[a.chunk]).then_inc(v_in[a.d], 16)

            def start(a):
                load_kq(a)
                load_kv(a)

            def half_step(a, other, nxt):
                if nxt is not None:
                    load_kq(nxt)
                    load_kv(nxt)

            all_halves(sp, half_step, start, lambda a: None)

        @block.tensor
        def _(pe):
            def decays(a):
                d = a.d
                pe.wait_ge(pool_done[d], POOL_EV.done(a.step, "gc"))
                if not a.first:
                    pe.wait_ge(dve_done[d], DVE_EV.done(a.step - 1, "su3"))
                for h in range(H):
                    last = pe.matmul(bank(d, h // 4)[:, (h % 4) * P:(h % 4 + 1) * P],
                                     gc[d][:, h:h + 1].broadcast_to([P, P]), U[:, d, :], start=True, stop=True)
                last.then_inc(pe_done[d], 1)
                pe.matmul(bank(d, 2)[:, 0:H], U[:, d, :], gc[d][:], start=True, stop=True).then_inc(pe_done[d], 1)

            def products(a):
                d = a.d
                pe.wait_ge(kT_in[d], a.step * 16 + 16)
                if a.lat:
                    pe.wait_ge(qT_in[d], a.step * 16 - 16)
                pe.wait_ge(act_done[d], ACT_EV.done(a.step, "el"))
                for p in range(4):
                    for h in (2 * p, 2 * p + 1):
                        out = head2(d, p)[:, h % 2, :]
                        if a.lat:
                            last = pe.matmul(out, kq[d][:, h, 0, :], kq[d][:, h, :, :].rearrange("p a c -> p (a c)"),
                                             start=True, stop=True)
                        else:
                            last = pe.matmul(out[:, 0:P], kq[d][:, h, 0, :], kq[d][:, h, 0, :], start=True, stop=True)
                    last.then_inc(pe_done[d], 1)

            def replicate(a, r):
                d = a.d
                if r == 0:
                    pe.wait_ge(dve_done[d], DVE_EV.done(a.step, "lo"))
                if r >= 4:
                    pe.wait_ge(dve_done[d], DVE_EV.done(a.step, f"a{2 * (r - 4) + 1}"))
                for k in (2 * r, 2 * r + 1):
                    if k == NB - 1:
                        continue
                    j = k if d == 0 else NB - 1 - k
                    out = head2(d, r % 4)[:, k % 2, :]
                    pe.matmul(out, sel[:, j, :], ahi[d][:].rearrange("p h i -> p (h i)"), start=True, stop=False)
                    last = pe.matmul(out, sel[:, j, :], alo[d][:].rearrange("p h i -> p (h i)"), start=False, stop=True)
                last.then_inc(pe_done[d], 1)

            def double(a, l):
                d, xc = a.d, a.d
                if l == 5:
                    pe.wait_ge(dve_done[d], DVE_EV.done(a.step, "tr"))
                    pe.wait_ge(act_done[d], ACT_EV.done(a.step, "tt"))
                else:
                    pe.wait_ge(dve_done[d], DVE_EV.done(a.step, "tt5"))
                for h in range(H):
                    last = pe.matmul(packed(bank(d, 0), l)[:, h], nA[d][:, h, :], half(T[d], l, xc)[:, h], start=True, stop=True)
                last.then_inc(pe_done[d], 1)
                pe.wait_ge(act_done[d], ACT_EV.done(a.step, f"x{l}"))
                if l == 5:
                    for h in range(H):
                        last = pe.matmul(packed(bank(d, 1), l)[:, h], TT[d][:, h, :], half(X[d], l, xc)[:, h], start=True, stop=True)
                    last.then_inc(pe_done[d], 1)
                for h in range(H):
                    last = pe.matmul(packed(bank(d, 2), l)[:, h], X[d][:, h, :], half(TT[d], l, 1 - xc)[:, h], start=True, stop=True)
                last.then_inc(pe_done[d], 1)

            def scan(a, n):
                d, p = a.d, n % 4
                heads = (2 * p, 2 * p + 1)
                out = lambda h: head2(d, p)[:, h % 2, :]
                if n < 4:
                    if n == 0:
                        pe.wait_ge(pool_done[d], POOL_EV.done(a.step, "kg"))
                        pe.wait_ge(dve_done[d], DVE_EV.done(a.step, "tt6"))
                        if a.first:
                            pe.wait_ge(init_rdy, 1)
                    for h in heads:
                        last = pe.matmul(out(h), EG[d][:, h, :], S[d][:, h, :], start=True, stop=True)
                elif n < 8:
                    pe.wait_ge(dve_done[d], DVE_EV.done(a.step, f"r{p}"))
                    for h in heads:
                        last = pe.matmul(out(h), TT[d][:, h, :], v[d][:, h, :], start=True, stop=True)
                elif n < 12:
                    if not a.lat:
                        if p == 3:
                            pe.wait_ge(pe_done[d], PE_EV.done(a.step, "vn3"))
                            pe.sem_inc(pe_done[d], 4)
                        return
                    pe.wait_ge(pool_done[d], POOL_EV.done(a.step, "qg"))
                    pe.wait_ge(act_done[d], ACT_EV.done(a.step, f"vn{p}"))
                    for h in heads:
                        pe.matmul(out(h), QG[d][:, h, :], S[d][:, h, :], start=True, stop=False)
                        last = pe.matmul(out(h), DT[d][:, h, :], v[d][:, h, :], start=False, stop=True)
                else:
                    pe.wait_ge(pool_done[d], POOL_EV.done(a.step, "kta"))
                    if a.lat:
                        pe.wait_ge(dve_done[d], DVE_EV.done(a.step, f"oa{p}"))
                    else:
                        pe.wait_ge(act_done[d], ACT_EV.done(a.step, f"vn{p}"))
                    for h in heads:
                        last = pe.matmul(out(h), kk[d][:, h, :], v[d][:, h, :], start=True, stop=True)
                last.then_inc(pe_done[d], 1)

            def start(a):
                pe.wait_ge(tab_in, 64)
                pe.wait_ge(sel_rdy, 1)
                decays(a)
                products(a)

            def half_step(a, other, nxt):
                for t in range(16 + LAG):
                    if t < 16 and other is not None:
                        scan(other, t)
                    if t >= LAG:
                        replicate(a, t - LAG)
                if nxt is not None:
                    decays(nxt)
                double(a, 5)
                if nxt is not None:
                    products(nxt)
                double(a, 6)

            def end(a):
                for t in range(16):
                    scan(a, t)

            all_halves(pe, half_step, start, end)

        @block.scalar
        def _(act):
            def decays(a):
                d = a.d
                gb = psum[:, 2048 * d:2048 * d + 1024].rearrange("p (h c) -> p h c", h=H)
                act.wait_ge(dve_done[d], DVE_EV.done(a.step, "gm"))
                act.activation(EG[d][:], gb, ACT.Exp).then_inc(act_done[d], 1)
                act.activation(el[d][:].unsqueeze(2), gb[:, :, LAST[d]:LAST[d] + 1], ACT.Exp).then_inc(act_done[d], 1)
                act.activation(tl[d][:], td[d][:], ACT.Exp).then_inc(act_done[d], 1)
                act.wait_ge(dve_done[d], DVE_EV.done(a.step, "gms"))
                act.activation(DT[d][:], nA[d][:], ACT.Exp).then_inc(act_done[d], 1)

            def high_parts(a):
                d = a.d
                act.wait_ge(dve_done[d], DVE_EV.done(a.step, "na3"))
                for q in quad:
                    last = act.activation(ahi[d][q], nA[d][q, :, q], ACT.Copy)
                last.then_inc(act_done[d], 1)

            def to_TT(a):
                d = a.d
                act.wait_ge(dve_done[d], DVE_EV.done(a.step, f"a{NB - 2}"))
                act.wait_ge(pool_done[d], POOL_EV.done(a.step, "z"))
                for q in quad:
                    last = act.activation(TT[d][q, :, q], R[d][q], ACT.Copy)
                last.then_inc(act_done[d], 1)

            def x_out(a, l):
                d = a.d
                act.wait_ge(pe_done[d], PE_EV.done(a.step, f"x{l}"))
                act.activation(half(X[d], l, d), packed(bank(d, 0), l), ACT.Copy).then_inc(act_done[d], 1)

            def v_new(a, p):
                d = a.d
                act.wait_ge(pe_done[d], PE_EV.done(a.step, f"vn{p}"))
                for h in (2 * p, 2 * p + 1):
                    last = act.activation(v[d][:, h, :], head2(d, p)[:, h % 2, :], ACT.Copy, scale=bc[d][:, h:h + 1])
                last.then_inc(act_done[d], 1)

            def half_step(a, other, nxt):
                high_parts(a)
                if other is not None:
                    for p in range(4):
                        v_new(other, p)
                to_TT(a)
                if nxt is not None:
                    decays(nxt)
                x_out(a, 5)
                x_out(a, 6)

            def end(a):
                for p in range(4):
                    v_new(a, p)

            act.wait_ge(tab_in, 64)
            act.activation(sel[:], selst[:], ACT.Copy).then_inc(sel_rdy, 1)
            act.wait_ge(init_rdy, 1)
            all_halves(act, half_step, decays, end)

        @block.vector
        def _(dve):
            for d in (0, 1):
                dve.memset(X[d][:], 0.0)
                dve.memset(S[d][:], 0.0)
            dve.wait_ge(sel_rdy, 1)
            dve.memset(o[:], 0.0).then_inc(init_rdy, 1)
            dve.wait_ge(init_rdy, 1)
            dve.wait_ge(nm_rdy, 1)

            def decays(a):
                d, sig = a.d, dve_done[a.d]
                gb = psum[:, 2048 * d:2048 * d + 1024].rearrange("p (h c) -> p h c", h=H)
                dve.wait_ge(pe_done[d], PE_EV.done(a.step, "gp"))
                dve.tensor_copy(gps[d][:], bank(d, 2)[:, 0:H]).then_inc(sig, 1)
                dve.wait_ge(sig, DVE_EV.done(a.step, "gps"))
                dve.tensor_tensor(td[d][:], gb[:, :, LAST[d]], gps[d][:], ALU.subtract).then_inc(sig, 1)
                dve.tensor_tensor(nA[d][:], gb, NM[:, d, :].unsqueeze(1).broadcast_to([P, H, P]), ALU.add).then_inc(sig, 1)
                dve.wait_ge(sig, DVE_EV.done(a.step, "gm"))
                dve.tensor_tensor(nA[d][:], nA[d][:], b3(gps[d]), ALU.subtract).then_inc(sig, 1)
                dve.wait_ge(pool_done[d], POOL_EV.done(a.step, "gc"))
                dve.wait_ge(act_done[d], ACT_EV.done(a.step, "dt"))
                dve.tensor_tensor(nA[d][:], DT[d][:], b3(nb[d]), ALU.mult).then_inc(sig, 1)

            def products(a):
                d, sig = a.d, dve_done[a.d]
                dve.wait_ge(sig, DVE_EV.done(a.step, "db"))
                for p in range(4):
                    dve.wait_ge(pe_done[d], PE_EV.done(a.step, f"kk{p}"))
                    hs = slice(2 * p, 2 * p + 2)
                    dve.tensor_tensor(nA[d][:, hs, :], head2(d, p)[:, :, 0:P], nA[d][:, hs, :], ALU.mult).then_inc(sig, 1)
                    if a.lat:
                        last = dve.tensor_tensor(DT[d][:, hs, :], head2(d, p)[:, :, P:2 * P], DT[d][:, hs, :], ALU.mult)
                if a.lat:
                    last.then_inc(sig, 1)
                else:
                    dve.wait_ge(sig, DVE_EV.done(a.step, "na3"))
                    dve.sem_inc(sig, 1)

            def low_parts(a):
                d = a.d
                dve.wait_ge(act_done[d], ACT_EV.done(a.step, "hi"))
                for q in quad:
                    last = dve.tensor_tensor(alo[d][q], nA[d][q, :, q], ahi[d][q].bitcast(F32), ALU.subtract)
                last.then_inc(dve_done[d], 1)

            def substitute(a, r):
                d, sig = a.d, dve_done[a.d]
                dve.wait_ge(pe_done[d], PE_EV.done(a.step, f"rp{r}"))
                for k in (2 * r, 2 * r + 1):
                    if k == NB - 1:
                        continue
                    if k:
                        dve.wait_ge(sig, DVE_EV.done(a.step, f"a{k - 1}"))
                    else:
                        dve.wait_ge(pool_done[d], POOL_EV.done(a.step, "z"))
                    j = k if d == 0 else NB - 1 - k
                    i = slice(j + 1, NB) if d == 0 else slice(0, j)
                    n = NB - 1 - k
                    row = head2(d, r % 4)[:, k % 2, :].rearrange("p (h i) -> p h i", h=H)[:, :, i]
                    dve.tensor_tensor(tmp[d][:, :, 0:n], row, R[d][:, :, j:j + 1].broadcast_to([P, H, n]), ALU.mult).then_inc(sig, 1)
                    dve.wait_ge(sig, DVE_EV.done(a.step, f"m{k}"))
                    dve.tensor_tensor(R[d][:, :, i], R[d][:, :, i], tmp[d][:, :, 0:n], ALU.add).then_inc(sig, 1)

            def to_T(a):
                d, sig = a.d, dve_done[a.d]
                dve.wait_ge(sig, DVE_EV.done(a.step, f"a{NB - 2}"))
                for q in quad:
                    last = dve.transpose(T[d][q, :, q], R[d][q])
                last.then_inc(sig, 1)

            def merge(a, l):
                d, sig = a.d, dve_done[a.d]
                xc, tc = d, 1 - d
                if l == 5:
                    dve.wait_ge(pe_done[d], PE_EV.done(a.step, "d5"))
                    dve.sem_inc(core.carried, 1)
                    dve.copy_predicated(half(T[d], l, xc), mask(l, 1 - d), packed(bank(d, 1), l)).then_inc(sig, 1)
                dve.wait_ge(pe_done[d], PE_EV.done(a.step, f"t{l}"))
                dve.sem_inc(core.carried, 1)
                dve.copy_predicated(half(TT[d], l, tc), mask(l, d), packed(bank(d, 2), l)).then_inc(sig, 1)

            def scan(a, n):
                d, p, sig = a.d, n % 4, dve_done[a.d]
                hs = slice(2 * p, 2 * p + 2)
                if n < 4:
                    if n == 0:
                        dve.wait_ge(v_in[d], a.step * 16 + 16)
                    dve.wait_ge(pe_done[d], PE_EV.done(a.step, f"ks{p}"))
                    dve.tensor_tensor(v[d][:, hs, :], v[d][:, hs, :], head2(d, p), ALU.subtract).then_inc(sig, 1)
                elif 8 <= n < 12:
                    if a.lat:
                        dve.wait_ge(pe_done[d], PE_EV.done(a.step, f"o{p}"))
                        oc = o[:, bass.ds(a.chunk, 1), 512 * p:512 * p + 512].rearrange("p a c -> p (a c)")
                        dve.tensor_tensor(oc, oc, bank(d, p), ALU.add).then_inc(sig, 1)
                    elif p == 3:
                        dve.wait_ge(sig, DVE_EV.done(a.step, "r3"))
                        dve.sem_inc(sig, 4)
                elif n >= 12:
                    dve.wait_ge(pe_done[d], PE_EV.done(a.step, f"su{p}"))
                    if n == 12:
                        dve.wait_ge(act_done[d], ACT_EV.done(a.step, "el"))
                    for h in (2 * p, 2 * p + 1):
                        last = dve.scalar_tensor_tensor(S[d][:, h, :], S[d][:, h, :], el[d][:, h:h + 1],
                                                        head2(d, p)[:, h % 2, :], ALU.mult, ALU.add)
                    last.then_inc(sig, 1)

            def start(a):
                decays(a)
                products(a)

            def half_step(a, other, nxt):
                for t in range(16 + LAG):
                    if t < 16 and other is not None:
                        scan(other, t)
                    if t == LAG - 1:
                        low_parts(a)
                    if t >= LAG:
                        substitute(a, t - LAG)
                to_T(a)
                if nxt is not None:
                    decays(nxt)
                merge(a, 5)
                if nxt is not None:
                    products(nxt)
                merge(a, 6)

            def end(a):
                for t in range(16):
                    scan(a, t)

            all_halves(dve, half_step, start, end)

        @block.gpsimd
        def _(pool):
            pool.wait_ge(tab_in, 64)
            pool.tensor_scalar(NM[:], U[:], -1.0, -BIG, ALU.add, ALU.mult).then_inc(nm_rdy, 1)

            def chunk_cols(a, dst, src):
                return pool.tensor_copy(dst[a.d][:], src[:, bass.ds(a.chunk, 1), 8 * a.d:8 * a.d + 8].rearrange("p a h -> p (a h)"))

            def decays(a):
                d, sig = a.d, pool_done[a.d]
                if not a.first:
                    pool.wait_ge(pe_done[d], PE_EV.done(a.step - 1, "gp"))
                chunk_cols(a, gc, core.gtok)
                chunk_cols(a, nb, core.nbeta).then_inc(sig, 1)

            def half_step(a, other, nxt):
                d, sig = a.d, pool_done[a.d]
                if not a.first:
                    pool.wait_ge(pe_done[d], PE_EV.done(a.step - 1, "su3"))
                chunk_cols(a, bc, core.beta).then_inc(sig, 1)
                pool.memset(T[d][:], 0.0)
                pool.memset(TT[d][:], 0.0)
                pool.tensor_copy(R[d][:], eye[:].unsqueeze(1).broadcast_to([P, H, NB])).then_inc(sig, 1)
                pool.wait_ge(act_done[d], ACT_EV.done(a.step, "dt"))
                pool.wait_ge(kT_in[d], a.step * 16 + 16)
                if a.lat:
                    pool.wait_ge(qT_in[d], a.step * 16 - 16)
                    pool.tensor_tensor(QG[d][:], kq[d][:, :, 1, :], EG[d][:], ALU.mult).then_inc(sig, 1)
                    pool.wait_ge(sig, POOL_EV.done(a.step, "qg"))
                else:
                    pool.wait_ge(sig, POOL_EV.done(a.step, "z"))
                    pool.sem_inc(sig, 1)
                pool.tensor_tensor(EG[d][:], kq[d][:, :, 0, :], EG[d][:], ALU.mult).then_inc(sig, 1)
                pool.wait_ge(k_in[d], a.step * 16 + 16)
                pool.tensor_tensor(kk[d][:], kk[d][:], b3(tl[d]), ALU.mult).then_inc(sig, 1)
                if nxt is not None:
                    decays(nxt)

            all_halves(pool, half_step, decays, lambda a: None)


def gate_phase(core, io):
    nc, psum, ident = core.nc, core.psum, core.ident
    o = core.at("o", [P, NL, FW], 0)
    zt = [core.at(f"zt{s}", [P, LAT], 192 + 4 * s) for s in range(2)]
    sq = [core.at(f"sq_g{s}", [P, FW], 64 + 8 * s) for s in range(2)]
    mg = [core.at(f"mg{q}", [P, KT, 256], 80 + 8 * q) for q in range(4)]
    y = core.at("y2", [P, 16, LAT], 64)
    wo = core.at("wo_last", [P, 16, D], 128)
    st_ = core.at("st_g", [P, 3, NL * H], 200)
    cols = core.cols
    z_v = core.z_d.rearrange("(n p) t -> n p t", p=P)
    mod_v = io["mod_w"][1].rearrange("(k p) (n c) -> n p k c", p=P, c=256)
    w_v = io["dn_w_out"][0].rearrange("(c p) d -> p c d", p=P)
    with ExitStack() as st:
        sem = sems(nc, st)
        z_in = [sem("zt_in0"), sem("zt_in1")]
        mg_in, mg_mm, wo_in = [sem(f"mg_in{q}") for q in range(4)], sem("mg_mm"), sem("wo_last_in")
        sq_rdy, red, std, rstd, on = sem("sqg_rdy"), sem("red_g"), sem("std_g"), sem("rstd_g"), sem("on_rdy")
        t_mm, y_rdy = sem("tg_mm"), sem("yg_rdy")
        block = st.enter_context(nc.Block())
        NCT = 16

        @block.sync
        def _(sp):
            for s in range(2):
                sp.dma_start(zt[s][:], z_v[s]).then_inc(z_in[s], 16)
            for q in range(4):
                sp.dma_start(mg[q][:], mod_v[8 + q]).then_inc(mg_in[q], 16)
            for q in range(4):
                sp.dma_start(wo[:, 4 * q:4 * q + 4, :], w_v[:, 4 * q:4 * q + 4, :]).then_inc(wo_in, 16)
            with sp.Fori(0, NCT // 2 - 1) as i:
                for s in range(2):
                    sp.wait_ge(y_rdy, i * 2 + (s + 3))
                    sp.dma_start(zt[s][:], z_v[i * 2 + (s + 2)]).then_inc(z_in[s], 16)
            sp.wait_ge(wo_in, 64)

        @block.scalar
        def _(act):
            for n in range(NL):
                if n >= 2:
                    act.wait_ge(red, n - 1)
                act.activation(sq[n % 2][:], o[:, n, :], ACT.Square).then_inc(sq_rdy, 1)
            act.wait_ge(red, NL + 1)
            act.activation(st_[:, 1, :], st_[:, 0, :], ACT.Sqrt).then_inc(std, 1)

        @block.vector
        def _(dve):
            dve.sem_inc(y_rdy, 2)
            for n in range(NL):
                dve.wait_ge(sq_rdy, n + 1)
                dve.reduce_sum(st_[:, 2, n * H:(n + 1) * H], sq[n % 2][:].rearrange("p (h c) -> p h c", h=H), AXX).then_inc(red, 1)
            dve.wait_ge(red, NL)
            dve.tensor_scalar(st_[:, 0, :], st_[:, 2, :], 1.0 / DV, EPS, ALU.mult, ALU.add).then_inc(red, 1)
            dve.wait_ge(std, 1)
            dve.reciprocal(st_[:, 2, :], st_[:, 1, :]).then_inc(rstd, 1)
            dve.wait_ge(rstd, 1)
            for n in range(NL):
                on_ = o[:, n, :].rearrange("p (h c) -> p h c", h=H)
                r = st_[:, 2, n * H:(n + 1) * H].unsqueeze(2).broadcast_to([P, H, DV])
                dve.tensor_tensor(on_, on_, r, ALU.mult).then_inc(on, 1)
            dve.wait_ge(mg_mm, 1)
            dve.tensor_tensor(core.modT[:, 40:48, :], psum[:, 2048:2064].rearrange("p (a b) -> p a b", b=2),
                              cols[:, 40:48].unsqueeze(2).broadcast_to([P, 8, 2]), ALU.add)
            with dve.Fori(0, NCT // 2) as i:
                for s in range(2):
                    n = i * 2 + s
                    dve.wait_ge(t_mm, n + 1)
                    dve.wait_ge(z_in[s], i * 16 + 16)
                    yn = y[:, bass.ds(n, 1), :].rearrange("p a t -> p (a t)")
                    dve.scalar_tensor_tensor(yn, psum[:, 1024 * s:1024 * s + 1024], cols[:, COL_DN + s:COL_DN + s + 1],
                                             zt[s][:], ALU.mult, ALU.mult).then_inc(y_rdy, 1)

        @block.tensor
        def _(pe):
            for q in range(4):
                pe.wait_ge(mg_in[q], 16)
                for b in range(2):
                    col = 2048 + 2 * (2 * q + b)
                    for k in range(KT):
                        last = pe.matmul(psum[:, col:col + 2], mg[q][:, k, b * P:(b + 1) * P], core.scond[:, k, :],
                                         start=(k == 0), stop=(k == KT - 1))
            last.then_inc(mg_mm, 1)
            pe.wait_ge(on, NL)
            for n in range(NCT):
                pe.wait_ge(y_rdy, n + 1)
                for t in range(NL):
                    o_ = 1024 * (n % 2) + t * P
                    last = pe.transpose(psum[:, o_:o_ + P], o[:, t, n * P:(n + 1) * P], ident[:])
                last.then_inc(t_mm, 1)


def tables():
    t = {}
    f = lambda L: 2 * np.pi / L * np.outer(np.arange(L // 2), np.arange(L // 2))
    lat = [m.reshape(4, P, HL).transpose(1, 0, 2).reshape(P, -1) for m in (np.cos(f(LAT)), np.sin(f(LAT)))]
    t["dft_tab"] = np.concatenate([m / LAT ** 0.5 for m in lat] + [np.cos(f(CTX)) / CTX ** 0.5, np.sin(f(CTX)) / CTX ** 0.5], 1)
    alt = 1.0 - 2.0 * (np.arange(P) % 2)
    t["alt_col"] = np.stack([alt / LAT ** 0.5, alt / CTX ** 0.5], 1)
    t["alt_row"] = np.concatenate([np.tile(alt, 4) / LAT ** 0.5, alt / CTX ** 0.5])[None]
    a = 2 * np.pi / FD * np.outer(np.arange(FD), np.arange(FD))
    t["ch_dft"] = np.stack([m.reshape(2, P, FD).transpose(1, 0, 2) for m in (np.cos(a) / FD ** 0.5, np.sin(a) / FD ** 0.5)], 1)
    t["ident"] = np.eye(P)
    i = np.arange(P)
    t["tri"] = np.stack([i[:, None] <= i[None], i[:, None] >= i[None]], 1)
    t = {n: np.ascontiguousarray(v, np.float32) for n, v in t.items()}
    t["block_eye"] = np.ascontiguousarray(np.eye(NB, dtype=np.float32)[i % NB])
    j = np.arange(NB)
    t["block_sel"] = np.ascontiguousarray((i[:, None, None] == (i[None, None] // NB * NB + j[None, :, None])), np.float32)
    lm = np.zeros((P, 2, 2, 64), np.int32)
    for n, l in enumerate(TOP):
        s = 1 << l
        c = np.arange(64)
        for half in range(2):
            lm[:, n, half] = (i[:, None] // (2 * s) == c[None] // s) & ((i[:, None] % (2 * s)) // s == half)
    t["level_mask"] = lm
    return t


def program(nc, io):
    with ExitStack() as st:
        core = Core(nc)
        core.carried = st.enter_context(nc.semaphore("carried"))
        input_phase(core, io)
        z_phase(core, io)
        fourier_phase(core, io)
        output_phase(core, io, 0)
        project_phase(core, io)
        delta_phase(core, io)
        gate_phase(core, io)
        output_phase(core, io, 1)


INPUTS = ("x", "c", "ctx", "c_ctx", "mod_w", "mod_b", "norm_g", "final_g", "fn_w_in", "fn_w_grp", "fn_w_out",
          "dn_w_in", "dn_conv", "dn_a_log", "dn_dt_bias", "dn_norm_g", "dn_w_out")


def kernel(**inputs):
    import concourse.bacc as _bacc
    from concourse.bass_utils import run_bass_kernel_spmd as _run

    nc = _bacc.Bacc("TRN2", target_bir_lowering=False, num_devices=1)
    arrays = {n: np.ascontiguousarray(inputs[n]) for n in INPUTS}
    x, ctx = arrays["x"][0], arrays["ctx"][0]
    arrays["x_mirror"] = np.ascontiguousarray(np.concatenate([x[HL:HL + 1], x[:HL:-1]]))
    arrays["ctx_mirror"] = np.ascontiguousarray(np.concatenate([ctx[HC:HC + 1], ctx[:HC:-1]]))
    arrays.update(tables())
    io = {n: nc.dram_tensor(f"in_{n}", a.shape, mybir.dt.from_np(a.dtype), kind="ExternalInput").ap() for n, a in arrays.items()}
    io["out"] = nc.dram_tensor("out", (1, LAT, D), F32, kind="ExternalOutput").ap()
    program(nc, io)
    r = _run(nc, [{f"in_{n}": a for n, a in arrays.items()}], core_ids=[0])
    return r.results[0]["out"]
```
